# Optimizing a Trainium2 kernel written in Bass

```python
import jax, jax.numpy as jnp
from jax import lax
import numpy as np

D_MODEL = 1024
BATCH = 1
SEQ = 256
DEPTH = 1

MEM_LEN = 256
HEAD_DIM = 64
Q_BLOCK = 128
EPS = 1e-6
SB_HEADS = 8
SB_WIDTH = SB_HEADS * HEAD_DIM
DIL_CONFIG = ((128, 1), (512, 4), (2048, 16))
N_DIL_GROUPS = 3
DIL_HEADS_PER_GROUP = 4
DIL_HEADS = N_DIL_GROUPS * DIL_HEADS_PER_GROUP
DIL_WIDTH = DIL_HEADS * HEAD_DIM
DIL_OUT_WIDTH = DIL_HEADS_PER_GROUP * HEAD_DIM
DIL_STREAM_KEYS = 128
ALIBI_MAX_BIAS = 8.0
MEM_HEADS = 4
MEM_HEAD_DIM = 128
MEM_WIDTH = MEM_HEADS * MEM_HEAD_DIM
N_BRANCHES = 3
IN_WIDTH = 3 * SB_WIDTH + 3 * DIL_WIDTH + MEM_WIDTH
IN_SPLITS = (SB_WIDTH, 2 * SB_WIDTH, 3 * SB_WIDTH,
             3 * SB_WIDTH + DIL_WIDTH, 3 * SB_WIDTH + 2 * DIL_WIDTH, 3 * SB_WIDTH + 3 * DIL_WIDTH)
PEER_HEADS = 8
PEER_KEYS = 128
PEER_EXPERTS = PEER_KEYS * PEER_KEYS
PEER_TOPK = 16
PEER_QDIM = 256
PEER_HALF = PEER_QDIM // 2
PEER_CHUNK = 128


def rms_norm(x, g):
    xf = x.astype(jnp.float32)
    y = xf * lax.rsqrt(jnp.mean(xf * xf, axis=-1, keepdims=True) + EPS)
    return (y * g.astype(jnp.float32)).astype(x.dtype)

def alibi_slopes(n):
    return jnp.exp2(-ALIBI_MAX_BIAS * jnp.arange(1, n + 1, dtype=jnp.float32) / n)

def stick_breaking_attention(q, k, v):
    B, H, S, dh = q.shape
    nb = S // Q_BLOCK
    q_blocks = q.reshape(B, H, nb, Q_BLOCK, dh).transpose(2, 0, 1, 3, 4)
    kpos = jnp.arange(S)
    scale = dh ** -0.5

    def block(args):
        q_blk, n = args
        z = jnp.einsum('bhqd,bhkd->bhqk', q_blk, k).astype(jnp.float32) * scale
        qpos = n * Q_BLOCK + jnp.arange(Q_BLOCK)
        past = kpos[None, :] < qpos[:, None]
        log_keep = jnp.where(past, jax.nn.log_sigmoid(-z), 0.0)
        between = lax.cumsum(log_keep, axis=3, reverse=True) - log_keep
        a = jnp.where(past, jnp.exp(jax.nn.log_sigmoid(z) + between), 0.0)
        return jnp.einsum('bhqk,bhkd->bhqd', a.astype(v.dtype), v)

    o = lax.map(block, (q_blocks, jnp.arange(nb)))
    return o.transpose(1, 2, 0, 3, 4).reshape(B, H, S, dh)

def dilated_group_attention(q, k, v, dilation, slopes):
    B, S, H, dh = q.shape
    L = S // dilation
    nb = -(-L // Q_BLOCK)
    Lp = nb * Q_BLOCK

    def to_streams(t):
        t = t.reshape(B, L, dilation, H, dh).transpose(0, 2, 3, 1, 4)
        t = jnp.pad(t, ((0, 0), (0, 0), (0, 0), (0, Lp - L), (0, 0)))
        return t.reshape(B, dilation, H, nb, Q_BLOCK, dh)

    qs, ks, vs = to_streams(q), to_streams(k), to_streams(v)

    def with_prev(t):
        prev = jnp.pad(t, ((0, 0), (0, 0), (0, 0), (1, 0), (0, 0), (0, 0)))[:, :, :, :nb]
        return jnp.concatenate([prev, t], axis=4)

    kc, vc = with_prev(ks), with_prev(vs)
    qi = jnp.arange(Q_BLOCK)
    kj = jnp.arange(2 * Q_BLOCK) - Q_BLOCK
    gap = qi[:, None] - kj[None, :]
    blk = jnp.arange(nb)
    valid = ((gap >= 0) & (gap <= DIL_STREAM_KEYS))[None] & \
            ((blk[:, None, None] * Q_BLOCK + kj[None, None, :]) >= 0)
    s = jnp.einsum('brhnqd,brhnkd->brhnqk', qs, kc).astype(jnp.float32) * dh ** -0.5
    s = s - slopes[:, None, None, None] * (gap * dilation).astype(jnp.float32)
    s = jnp.where(valid, s, -1e30)
    lse = jax.nn.logsumexp(s, axis=-1)
    p = jnp.exp(s - lse[..., None])
    o = jnp.einsum('brhnqk,brhnkd->brhnqd', p.astype(v.dtype), vc)
    o = o.reshape(B, dilation, H, Lp, dh)[:, :, :, :L].transpose(0, 3, 1, 2, 4).reshape(B, S, H, dh)
    lse = lse.reshape(B, dilation, H, Lp)[..., :L].transpose(0, 3, 1, 2).reshape(B, S, H)
    return o, lse

def dilated_mixture(q, k, v, g_q, g_k):
    q = rms_norm(q, g_q)
    k = rms_norm(k, g_k)
    slopes = alibi_slopes(DIL_HEADS)
    outs, lses = [], []
    for g, (window, dilation) in enumerate(DIL_CONFIG):
        hs = slice(g * DIL_HEADS_PER_GROUP, (g + 1) * DIL_HEADS_PER_GROUP)
        o, lse = dilated_group_attention(q[:, :, hs], k[:, :, hs], v[:, :, hs], dilation, slopes[hs])
        outs.append(o)
        lses.append(lse)
    w = jax.nn.softmax(jnp.stack(lses, axis=2), axis=2)
    o = jnp.stack(outs, axis=2)
    return jnp.sum(w[..., None].astype(o.dtype) * o, axis=2)

def memory_attention(q, mem_h, w_kv, g_q, g_k):
    B, M, _ = mem_h.shape
    kv = (mem_h @ w_kv).reshape(B, M, 2, MEM_HEADS, MEM_HEAD_DIM)
    k = rms_norm(kv[:, :, 0], g_k)
    v = kv[:, :, 1]
    q = rms_norm(q, g_q)
    s = jnp.einsum('bshd,bmhd->bhsm', q, k).astype(jnp.float32) * MEM_HEAD_DIM ** -0.5
    p = jax.nn.softmax(s, axis=-1)
    return jnp.einsum('bhsm,bmhd->bshd', p.astype(v.dtype), v)

def peer_ffn(h, w_q, subkeys, u, v):
    B, S, D = h.shape
    T = B * S
    hf = h.reshape(T, D)
    q = (hf @ w_q).reshape(T, PEER_HEADS, 2, PEER_HALF)
    sc = jnp.einsum('thpd,hpkd->thpk', q, subkeys).astype(jnp.float32)
    s1, i1 = lax.top_k(sc[:, :, 0], PEER_TOPK)
    s2, i2 = lax.top_k(sc[:, :, 1], PEER_TOPK)
    cand = (s1[..., :, None] + s2[..., None, :]).reshape(T, PEER_HEADS, PEER_TOPK * PEER_TOPK)
    cand_idx = (i1[..., :, None] * PEER_KEYS + i2[..., None, :]).reshape(T, PEER_HEADS, PEER_TOPK * PEER_TOPK)
    top_s, pos = lax.top_k(cand, PEER_TOPK)
    idx = jnp.take_along_axis(cand_idx, pos, axis=-1)
    gate = jax.nn.softmax(top_s, axis=-1)
    nc = T // PEER_CHUNK

    def chunk(args):
        hc, ic, gc = args
        act = jax.nn.gelu(jnp.einsum('chkd,cd->chk', u[ic], hc).astype(jnp.float32), approximate=False)
        w = (gc * act).astype(h.dtype)
        return jnp.einsum('chk,chkd->cd', w, v[ic])

    out = lax.map(chunk, (hf.reshape(nc, PEER_CHUNK, D),
                          idx.reshape(nc, PEER_CHUNK, PEER_HEADS, PEER_TOPK),
                          gate.reshape(nc, PEER_CHUNK, PEER_HEADS, PEER_TOPK)))
    return out.reshape(B, S, D)

def first_inputs(seed: int = 0) -> dict:
    key = jax.random.key(seed)
    ks = jax.random.split(key, 24)
    D = D_MODEL

    def nrm(k, shape, scale):
        return jax.random.normal(k, shape, jnp.float32) * scale

    def gain(k, n):
        return 1.0 + 0.02 * jax.random.normal(k, (DEPTH, n), jnp.float32)

    return {
        'x': nrm(ks[0], (BATCH, SEQ, D), 1.0),
        'mem': nrm(ks[1], (BATCH, MEM_LEN, D), 1.0),
        'g_mix': gain(ks[2], D),
        'g_mem': gain(ks[3], D),
        'w_in': nrm(ks[4], (DEPTH, D, IN_WIDTH), D ** -0.5),
        'w_mem_kv': nrm(ks[5], (DEPTH, D, 2 * MEM_WIDTH), D ** -0.5),
        'g_q_dil': gain(ks[6], HEAD_DIM),
        'g_k_dil': gain(ks[7], HEAD_DIM),
        'g_q_mem': gain(ks[8], MEM_HEAD_DIM),
        'g_k_mem': gain(ks[9], MEM_HEAD_DIM),
        'w_o_sb': nrm(ks[10], (DEPTH, SB_WIDTH, D), SB_WIDTH ** -0.5),
        'w_o_dil': nrm(ks[11], (DEPTH, DIL_OUT_WIDTH, D), DIL_OUT_WIDTH ** -0.5),
        'w_o_mem': nrm(ks[12], (DEPTH, MEM_WIDTH, D), MEM_WIDTH ** -0.5),
        'w_gate': nrm(ks[13], (DEPTH, D, N_BRANCHES * D), D ** -0.5),
        'b_gate': nrm(ks[14], (DEPTH, N_BRANCHES * D), 0.02),
        'w_out': nrm(ks[15], (DEPTH, D, D), D ** -0.5),
        'g_ffn': gain(ks[16], D),
        'w_peer_q': nrm(ks[17], (DEPTH, D, PEER_HEADS * PEER_QDIM), D ** -0.5),
        'peer_subkeys': nrm(ks[18], (DEPTH, PEER_HEADS, 2, PEER_KEYS, PEER_HALF), PEER_HALF ** -0.5),
        'peer_u': nrm(ks[19], (DEPTH, PEER_EXPERTS, D), D ** -0.5),
        'peer_v': nrm(ks[20], (DEPTH, PEER_EXPERTS, D), (PEER_HEADS * PEER_TOPK) ** -0.5),
    }

def first_block(x, mem, g_mix, g_mem, w_in, w_mem_kv, g_q_dil, g_k_dil, g_q_mem, g_k_mem,
              w_o_sb, w_o_dil, w_o_mem, w_gate, b_gate, w_out, g_ffn, w_peer_q,
              peer_subkeys, peer_u, peer_v):
    B, S, D = x.shape
    for l in range(DEPTH):
        h = rms_norm(x, g_mix[l])
        proj = h @ w_in[l]
        sb_q, sb_k, sb_v, d_q, d_k, d_v, m_q = jnp.split(proj, IN_SPLITS, axis=-1)

        def sb_heads(t):
            return t.reshape(B, S, SB_HEADS, HEAD_DIM).transpose(0, 2, 1, 3)

        y_sb = stick_breaking_attention(sb_heads(sb_q), sb_heads(sb_k), sb_heads(sb_v))
        y_sb = y_sb.transpose(0, 2, 1, 3).reshape(B, S, SB_WIDTH) @ w_o_sb[l]

        def dil_heads(t):
            return t.reshape(B, S, DIL_HEADS, HEAD_DIM)

        y_dil = dilated_mixture(dil_heads(d_q), dil_heads(d_k), dil_heads(d_v), g_q_dil[l], g_k_dil[l])
        y_dil = y_dil.reshape(B, S, DIL_OUT_WIDTH) @ w_o_dil[l]

        mem_h = rms_norm(mem, g_mem[l])
        y_mem = memory_attention(m_q.reshape(B, S, MEM_HEADS, MEM_HEAD_DIM), mem_h, w_mem_kv[l],
                                 g_q_mem[l], g_k_mem[l])
        y_mem = y_mem.reshape(B, S, MEM_WIDTH) @ w_o_mem[l]

        gates = jax.nn.sigmoid(h @ w_gate[l] + b_gate[l]).reshape(B, S, N_BRANCHES, D)
        merged = gates[:, :, 0] * y_sb + gates[:, :, 1] * y_dil + gates[:, :, 2] * y_mem
        x = x + merged @ w_out[l]

        h2 = rms_norm(x, g_ffn[l])
        x = x + peer_ffn(h2, w_peer_q[l], peer_subkeys[l], peer_u[l], peer_v[l])
    return x


DEPTH_2 = 2

GRID_W = 64
CTX_LEN = 256
N_MIXERS = 2
N_A_LAYERS = (DEPTH_2 + 1) // 2
N_B_LAYERS = DEPTH_2 // 2
CHUNK = 64
N_MOD = 6
A_HEADS = 8
A_DK = D_MODEL // 16
A_DV = D_MODEL // 8
A_PROJ = 2 * A_HEADS * A_DK + 2 * A_HEADS * A_DV + 4 * A_HEADS
CONV_W = 5
B_HEADS = 8
B_DK = D_MODEL // B_HEADS
B_DV = D_MODEL // B_HEADS
B_PROJ = 2 * B_HEADS * B_DK + 2 * B_HEADS * B_DV
ROPE_BASE = 10000.0
N_EXPERTS = 16
EXPERT_FF = D_MODEL
CAPACITY_FACTOR = 2


def rmsnorm(x, g):
    xf = x.astype(jnp.float32)
    y = xf * lax.rsqrt(jnp.mean(xf * xf, axis=-1, keepdims=True) + EPS)
    return (y * g.astype(jnp.float32)).astype(x.dtype)

def modulate(h, shift, scale):
    return h * (1 + scale) + shift

def heads(a, n_heads):
    b, t, _ = a.shape
    return a.reshape(b, t, n_heads, -1).transpose(0, 2, 1, 3)

def dwconv_centred(x, w, b):
    pad = CONV_W // 2
    y = lax.conv_general_dilated(x, w[:, None, :].astype(x.dtype), window_strides=(1,),
                                 padding=[(pad, pad)], dimension_numbers=('NWC', 'WIO', 'NWC'),
                                 feature_group_count=x.shape[-1])
    return y + b.astype(x.dtype)

def to_chunks(a):
    b, h, t = a.shape[:3]
    return jnp.moveaxis(a.reshape(b, h, t // CHUNK, CHUNK, *a.shape[3:]), 2, 0)

def from_chunks(a):
    nc, b, h, l = a.shape[:4]
    return jnp.moveaxis(a, 0, 2).reshape(b, h, nc * l, *a.shape[4:])

def mlstm_scan(q, k, v, ig, lf, state):
    tril = jnp.tril(jnp.ones((CHUNK, CHUNK), bool))

    def step(carry, inp):
        C, n, m = carry
        qc, kc, vc, ic, fc = inp
        b = jnp.cumsum(fc, axis=-1)
        dmat = jnp.where(tril, b[..., :, None] - b[..., None, :] + ic[..., None, :], -jnp.inf)
        inter = b + m[..., None]
        m_row = jnp.maximum(inter, dmat.max(-1))
        s = jnp.einsum('bhid,bhjd->bhij', qc, kc) * jnp.exp(dmat - m_row[..., None])
        w_inter = jnp.exp(inter - m_row)
        num = jnp.einsum('bhij,bhjv->bhiv', s, vc) + w_inter[..., None] * jnp.einsum('bhid,bhdv->bhiv', qc, C)
        den = s.sum(-1) + w_inter * jnp.einsum('bhid,bhd->bhi', qc, n)
        h = num / jnp.maximum(jnp.abs(den), jnp.exp(-m_row))[..., None]
        b_last = b[..., -1]
        gk = b_last[..., None] - b + ic
        m_new = jnp.maximum(b_last + m, gk.max(-1))
        wk = jnp.exp(gk - m_new[..., None])
        wc = jnp.exp(b_last + m - m_new)
        C_new = wc[..., None, None] * C + jnp.einsum('bhj,bhjd,bhjv->bhdv', wk, kc, vc)
        n_new = wc[..., None] * n + jnp.einsum('bhj,bhjd->bhd', wk, kc)
        return (C_new, n_new, m_new), h

    xs = tuple(to_chunks(a) for a in (q, k, v, ig, lf))
    state, h = lax.scan(step, state, xs)
    return from_chunks(h), state

def retention_scan(q, k, v, logg, S):
    idx = jnp.arange(CHUNK, dtype=jnp.float32)
    tril = jnp.tril(jnp.ones((CHUNK, CHUNK), bool))
    diff = jnp.where(tril, idx[:, None] - idx[None, :], 0.0)
    dmat = jnp.where(tril, jnp.exp(diff * logg[:, None, None]), 0.0)
    inter = jnp.exp((idx + 1.0) * logg[:, None])
    kdec = jnp.exp((CHUNK - 1.0 - idx) * logg[:, None])
    sdec = jnp.exp(CHUNK * logg)

    def step(S, inp):
        qc, kc, vc = inp
        o = jnp.einsum('bhij,bhjv->bhiv', jnp.einsum('bhid,bhjd->bhij', qc, kc) * dmat, vc) \
            + inter[..., None] * jnp.einsum('bhid,bhdv->bhiv', qc, S)
        S_new = sdec[:, None, None] * S + jnp.einsum('hj,bhjd,bhjv->bhdv', kdec, kc, vc)
        return S_new, o

    xs = tuple(to_chunks(a) for a in (q, k, v))
    S, o = lax.scan(step, S, xs)
    return from_chunks(o), S

def run_bidirectional(scan_f, scan_b, ctx_f, lat_f, ctx_b, lat_b, state0):
    flip = lambda t: tuple(jnp.flip(a, 2) for a in t)
    oc_f, s = scan_f(ctx_f, state0)
    ol_f, _ = scan_f(lat_f, s)
    oc_b, s = scan_b(flip(ctx_b), state0)
    ol_b, _ = scan_b(flip(lat_b), s)
    return oc_f + jnp.flip(oc_b, 2), ol_f + jnp.flip(ol_b, 2)

def mlstm_mixer(h_ctx, h_lat, w_in, conv_w, conv_b, ig_b, fg_b, norm_g, w_out, need_ctx_out):
    nq = A_HEADS * A_DK
    nv = A_HEADS * A_DV
    f32 = jnp.float32

    def project(h):
        bn, t, _ = h.shape
        p = h @ w_in
        qk = jax.nn.silu(dwconv_centred(p[..., :2 * nq], conv_w, conv_b)).astype(f32)
        q = heads(qk[..., :nq], A_HEADS) * (A_DK ** -0.5)
        k = heads(qk[..., nq:], A_HEADS)
        v = heads(p[..., 2 * nq:2 * nq + nv].astype(f32), A_HEADS)
        o = p[..., 2 * nq + nv:2 * nq + 2 * nv]
        g = p[..., 2 * nq + 2 * nv:].astype(f32)
        ig = g[..., :2 * A_HEADS].reshape(bn, t, 2, A_HEADS) + ig_b.astype(f32)
        lf = jax.nn.log_sigmoid(g[..., 2 * A_HEADS:].reshape(bn, t, 2, A_HEADS) + fg_b.astype(f32))
        ig = jnp.transpose(ig, (0, 2, 3, 1))
        lf = jnp.transpose(lf, (0, 2, 3, 1))
        fwd = (q, k, v, ig[:, 0], lf[:, 0])
        bwd = (q, k, v, ig[:, 1], lf[:, 1])
        return fwd, bwd, o

    cf, cb, o_ctx = project(h_ctx)
    lf_, lb, o_lat = project(h_lat)
    bn = h_lat.shape[0]
    state0 = (jnp.zeros((bn, A_HEADS, A_DK, A_DV), f32), jnp.zeros((bn, A_HEADS, A_DK), f32),
              jnp.zeros((bn, A_HEADS), f32))
    scan = lambda args, s: mlstm_scan(*args, s)
    y_ctx, y_lat = run_bidirectional(scan, scan, cf, lf_, cb, lb, state0)

    def finish(y, o):
        b_, h_, t_, d_ = y.shape
        y = jnp.transpose(y, (0, 2, 1, 3))
        y = y * lax.rsqrt(jnp.mean(y * y, axis=-1, keepdims=True) + EPS)
        y = y.reshape(b_, t_, h_ * d_) * norm_g.astype(f32) * jax.nn.sigmoid(o.astype(f32))
        return y.astype(o.dtype) @ w_out

    out_ctx = finish(y_ctx, o_ctx) if need_ctx_out else None
    return out_ctx, finish(y_lat, o_lat)

def rope_angles(t):
    rows = t // GRID_W
    r = jnp.broadcast_to(jnp.arange(rows, dtype=jnp.float32)[:, None], (rows, GRID_W)).reshape(-1)
    col = jnp.broadcast_to(jnp.arange(GRID_W, dtype=jnp.float32)[None, :], (rows, GRID_W)).reshape(-1)
    nf = B_DK // 4
    inv = ROPE_BASE ** (-jnp.arange(nf, dtype=jnp.float32) / nf)
    return r[:, None] * inv, col[:, None] * inv

def rope(x, ang):
    x1, x2 = jnp.split(x, 2, axis=-1)
    cos, sin = jnp.cos(ang), jnp.sin(ang)
    return jnp.concatenate([x1 * cos - x2 * sin, x1 * sin + x2 * cos], axis=-1)

def rope2d(x, ang_r, ang_c):
    half = B_DK // 2
    return jnp.concatenate([rope(x[..., :half], ang_r), rope(x[..., half:], ang_c)], axis=-1)

def retention_mixer(h_ctx, h_lat, w_in, decay_logit, gn_g, w_out, need_ctx_out):
    n = B_HEADS * B_DK
    f32 = jnp.float32

    def project(h, angles):
        p = h @ w_in
        q = heads(p[..., :n].astype(f32), B_HEADS)
        k = heads(p[..., n:2 * n].astype(f32), B_HEADS) * (B_DK ** -0.5)
        v = heads(p[..., 2 * n:3 * n].astype(f32), B_HEADS)
        g = p[..., 3 * n:]
        if angles is not None:
            q = rope2d(q, *angles)
            k = rope2d(k, *angles)
        return (q, k, v), g

    c_args, g_ctx = project(h_ctx, None)
    l_args, g_lat = project(h_lat, rope_angles(h_lat.shape[1]))
    logg = jax.nn.log_sigmoid(decay_logit.astype(f32))
    bn = h_lat.shape[0]
    state0 = jnp.zeros((bn, B_HEADS, B_DK, B_DV), f32)
    scan_f = lambda args, s: retention_scan(*args, logg[0], s)
    scan_b = lambda args, s: retention_scan(*args, logg[1], s)
    y_ctx, y_lat = run_bidirectional(scan_f, scan_b, c_args, l_args, c_args, l_args, state0)

    def finish(y, g):
        b_, h_, t_, d_ = y.shape
        y = jnp.transpose(y, (0, 2, 1, 3))
        mu = jnp.mean(y, axis=-1, keepdims=True)
        var = jnp.mean(jnp.square(y - mu), axis=-1, keepdims=True)
        y = ((y - mu) * lax.rsqrt(var + EPS)).reshape(b_, t_, h_ * d_) * gn_g.astype(f32)
        y = y * jax.nn.silu(g.astype(f32))
        return y.astype(g.dtype) @ w_out

    out_ctx = finish(y_ctx, g_ctx) if need_ctx_out else None
    return out_ctx, finish(y_lat, g_lat)

def expert_choice_ffn(h, router, w_gate, w_up, w_down):
    bn, t, _ = h.shape
    cap = CAPACITY_FACTOR * t // N_EXPERTS
    aff = jax.nn.softmax(h.astype(jnp.float32) @ router.astype(jnp.float32), axis=-1)
    gate, idx = lax.top_k(jnp.swapaxes(aff, 1, 2), cap)
    bidx = jnp.arange(bn)[:, None, None]
    xs = h[bidx, idx]
    hid = jax.nn.silu(jnp.einsum('becd,edf->becf', xs, w_gate)) * jnp.einsum('becd,edf->becf', xs, w_up)
    y = jnp.einsum('becf,efd->becd', hid, w_down) * gate[..., None].astype(h.dtype)
    return jnp.zeros_like(h).at[bidx, idx].add(y)

def second_inputs(seed: int = 0) -> dict:
    key = jax.random.key(seed)
    ks = jax.random.split(key, 24)
    f32 = jnp.float32
    D = D_MODEL
    nqk = 2 * A_HEADS * A_DK
    nrm = lambda k, shape, s: jax.random.normal(k, shape, f32) * s
    fbase = jnp.linspace(3.0, 6.0, A_HEADS, dtype=f32)
    dbase = jnp.log(2.0 ** (5.0 + jnp.arange(B_HEADS, dtype=f32)) - 1.0)
    return {
        "x": nrm(ks[0], (BATCH, SEQ, D), 1.0),
        "c": nrm(ks[1], (BATCH, D), 1.0),
        "ctx": nrm(ks[2], (BATCH, CTX_LEN, D), 1.0),
        "c_ctx": nrm(ks[3], (D,), 1.0),
        "ada_w": nrm(ks[4], (DEPTH_2, D, N_MOD * D), 0.5 * D ** -0.5),
        "ada_b": nrm(ks[5], (DEPTH_2, N_MOD * D), 0.02),
        "norm_mix_g": 1.0 + nrm(ks[6], (DEPTH_2, D), 0.02),
        "norm_ffn_g": 1.0 + nrm(ks[7], (DEPTH_2, D), 0.02),
        "final_norm_g": 1.0 + nrm(ks[8], (D,), 0.02),
        "mlstm_w_in": nrm(ks[9], (N_A_LAYERS, D, A_PROJ), D ** -0.5),
        "mlstm_conv_w": nrm(ks[10], (N_A_LAYERS, CONV_W, nqk), CONV_W ** -0.5),
        "mlstm_conv_b": nrm(ks[11], (N_A_LAYERS, nqk), 0.02),
        "mlstm_igate_b": nrm(ks[12], (N_A_LAYERS, 2, A_HEADS), 0.1),
        "mlstm_fgate_b": fbase + nrm(ks[13], (N_A_LAYERS, 2, A_HEADS), 0.1),
        "mlstm_head_norm_g": 1.0 + nrm(ks[14], (N_A_LAYERS, A_HEADS * A_DV), 0.02),
        "mlstm_w_out": nrm(ks[15], (N_A_LAYERS, A_HEADS * A_DV, D), (A_HEADS * A_DV) ** -0.5),
        "ret_w_in": nrm(ks[16], (N_B_LAYERS, D, B_PROJ), D ** -0.5),
        "ret_decay_logit": dbase + nrm(ks[17], (N_B_LAYERS, 2, B_HEADS), 0.1),
        "ret_group_norm_g": 1.0 + nrm(ks[18], (N_B_LAYERS, B_HEADS * B_DV), 0.02),
        "ret_w_out": nrm(ks[19], (N_B_LAYERS, B_HEADS * B_DV, D), (B_HEADS * B_DV) ** -0.5),
        "moe_router": nrm(ks[20], (DEPTH_2, D, N_EXPERTS), D ** -0.5),
        "moe_w_gate": nrm(ks[21], (DEPTH_2, N_EXPERTS, D, EXPERT_FF), D ** -0.5),
        "moe_w_up": nrm(ks[22], (DEPTH_2, N_EXPERTS, D, EXPERT_FF), D ** -0.5),
        "moe_w_down": nrm(ks[23], (DEPTH_2, N_EXPERTS, EXPERT_FF, D), EXPERT_FF ** -0.5),
    }

def second_block(x, c, ctx, c_ctx, ada_w, ada_b, norm_mix_g, norm_ffn_g, final_norm_g,
              mlstm_w_in, mlstm_conv_w, mlstm_conv_b, mlstm_igate_b, mlstm_fgate_b,
              mlstm_head_norm_g, mlstm_w_out, ret_w_in, ret_decay_logit, ret_group_norm_g,
              ret_w_out, moe_router, moe_w_gate, moe_w_up, moe_w_down):
    c_lat = jax.nn.silu(c)[:, None, :]
    c_con = jax.nn.silu(c_ctx)[None, None, :]
    for i in range(DEPTH_2):
        last = i == DEPTH_2 - 1
        mod_l = jnp.split(c_lat @ ada_w[i] + ada_b[i], N_MOD, axis=-1)
        mod_c = jnp.split(c_con @ ada_w[i] + ada_b[i], N_MOD, axis=-1)
        h_lat = modulate(rmsnorm(x, norm_mix_g[i]), mod_l[0], mod_l[1])
        h_ctx = modulate(rmsnorm(ctx, norm_mix_g[i]), mod_c[0], mod_c[1])
        j = i // N_MIXERS
        if i % N_MIXERS == 0:
            o_ctx, o_lat = mlstm_mixer(h_ctx, h_lat, mlstm_w_in[j], mlstm_conv_w[j], mlstm_conv_b[j],
                                       mlstm_igate_b[j], mlstm_fgate_b[j], mlstm_head_norm_g[j],
                                       mlstm_w_out[j], not last)
        else:
            o_ctx, o_lat = retention_mixer(h_ctx, h_lat, ret_w_in[j], ret_decay_logit[j],
                                           ret_group_norm_g[j], ret_w_out[j], not last)
        x = x + mod_l[2] * o_lat
        h_lat = modulate(rmsnorm(x, norm_ffn_g[i]), mod_l[3], mod_l[4])
        x = x + mod_l[5] * expert_choice_ffn(h_lat, moe_router[i], moe_w_gate[i], moe_w_up[i], moe_w_down[i])
        if not last:
            ctx = ctx + mod_c[2] * o_ctx
            h_ctx = modulate(rmsnorm(ctx, norm_ffn_g[i]), mod_c[3], mod_c[4])
            ctx = ctx + mod_c[5] * expert_choice_ffn(h_ctx, moe_router[i], moe_w_gate[i], moe_w_up[i], moe_w_down[i])
    return rmsnorm(x, final_norm_g)


def setup_inputs(seed=0):
    out = dict(first_inputs(seed))
    for name, value in second_inputs(seed + 1).items():
        if name != "x":
            out[name + "_2"] = value
    return out


def reference(
    x, mem, g_mix, g_mem, w_in, w_mem_kv, g_q_dil, g_k_dil, g_q_mem, g_k_mem, w_o_sb, w_o_dil,
    w_o_mem, w_gate, b_gate, w_out, g_ffn, w_peer_q, peer_subkeys, peer_u, peer_v, c_2, ctx_2,
    c_ctx_2, ada_w_2, ada_b_2, norm_mix_g_2, norm_ffn_g_2, final_norm_g_2, mlstm_w_in_2,
    mlstm_conv_w_2, mlstm_conv_b_2, mlstm_igate_b_2, mlstm_fgate_b_2, mlstm_head_norm_g_2,
    mlstm_w_out_2, ret_w_in_2, ret_decay_logit_2, ret_group_norm_g_2, ret_w_out_2, moe_router_2,
    moe_w_gate_2, moe_w_up_2, moe_w_down_2,
):
    x = first_block(
        x, mem, g_mix, g_mem, w_in, w_mem_kv, g_q_dil, g_k_dil, g_q_mem, g_k_mem, w_o_sb,
        w_o_dil, w_o_mem, w_gate, b_gate, w_out, g_ffn, w_peer_q, peer_subkeys, peer_u, peer_v,
    )
    return second_block(
        x, c_2, ctx_2, c_ctx_2, ada_w_2, ada_b_2, norm_mix_g_2, norm_ffn_g_2, final_norm_g_2,
        mlstm_w_in_2, mlstm_conv_w_2, mlstm_conv_b_2, mlstm_igate_b_2, mlstm_fgate_b_2,
        mlstm_head_norm_g_2, mlstm_w_out_2, ret_w_in_2, ret_decay_logit_2, ret_group_norm_g_2,
        ret_w_out_2, moe_router_2, moe_w_gate_2, moe_w_up_2, moe_w_down_2,
    )


_drawn_inputs = setup_inputs


def setup_inputs(seed=0):
    import zlib

    import numpy as np

    out = dict(_drawn_inputs(seed))
    spreads = {}
    factors = {'g_mix': 4.783,
     'g_mem': 8.0,
     'g_q_dil': 8.0,
     'g_k_dil': 8.0,
     'g_q_mem': 8.0,
     'g_k_mem': 8.0,
     'b_gate': 8.0,
     'g_ffn': 7.588,
     'norm_mix_g_2': 6.476,
     'norm_ffn_g_2': 8.0,
     'final_norm_g_2': 19.918,
     'mlstm_conv_b_2': 24.742,
     'mlstm_igate_b_2': 8.0,
     'mlstm_head_norm_g_2': 8.0,
     'ret_group_norm_g_2': 21.617}
    for name, (base, spread) in spreads.items():
        noise = np.random.default_rng([zlib.crc32(name.encode()), seed]).standard_normal(out[name].shape)
        drawn = base * np.exp(spread * noise) if base else spread * noise
        out[name] = __import__('jax').numpy.asarray(drawn.astype(out[name].dtype))
    for name, factor in factors.items():
        out[name] = (out[name] * factor).astype(out[name].dtype)
    return out
```

```python
from contextlib import ExitStack

import numpy as np

import concourse.bass as bass
from concourse import mybir

F32 = mybir.dt.float32
I32 = mybir.dt.int32
U32 = mybir.dt.uint32
ALU = mybir.AluOpType
ACT = mybir.ActivationFunctionType
AX = mybir.AxisListType

P = 128
D = 1024
C = D // P
T = 256
TT = T // P
EPS = 1e-6
SLOTS = 6
SLOT = 4096
BANKS = 8
NEG = -1e30

SB_HEADS, SB_DIM = 8, 64
DIL_GROUPS, DIL_SLOTS, DIL_DIM = 3, 4, 64
DILATIONS = (1, 4, 16)
DIL_HEADS = DIL_GROUPS * DIL_SLOTS
DIL_REACH = 128
MEM_HEADS, MEM_DIM = 4, 128
PEER_HEADS, PEER_KEYS, PEER_TOPK = 8, 128, 16
EXPERTS = 16
CAPACITY = 2 * T // EXPERTS
A_HEADS, A_DK, A_DV = 8, 64, 128
CONV_W = 5
B_HEADS, B_DIM = 8, 128

R_X, R_CTX, R_RING = 0, 2048, 4096
R_WORK = R_RING + SLOTS * SLOT
BIG = R_WORK + 20992


def column_plan():
    widths = dict(g_mix=C, g_mem=C, g_ffn=C, norm_mix=2 * C, norm_ffn=2 * C, ada_b=2 * 48, cvec=2 * C,
                  gq_dil=1, gk_dil=1, gq_mem=1, gk_mem=1, conv_w=C * CONV_W, conv_b=C, ig_b=1, fg_b=1,
                  a_norm=C, b_norm=C, decay=16)
    plan, at = {}, 0
    for name, width in widths.items():
        plan[name] = (at, at + width)
        at += width
    return plan, at


COLUMNS, N_COLUMNS = column_plan()


class Steps:

    def __init__(self, sem):
        self.sem, self.n = sem, 0

    def after(self, eng, ins):
        ins.then_inc(self.sem, 1)
        self.n += 1
        eng.wait_ge(self.sem, self.n)


class Kernel:

    def __init__(self, nc, ctx, dram):
        self.nc, self.ctx, self.dram = nc, ctx, dram
        self.release = {}
        self.used = set()
        self.loads, self.issued, self.stage, self.peer_done = [], 0, {}, False

    def sem(self, name):
        return self.ctx.enter_context(self.nc.semaphore(name))

    def col(self, name):
        return self.cols[:, COLUMNS[name][0]:COLUMNS[name][1]]


class Tile:

    def __init__(self, pairs, n, load, m, row, dst, gate, bias, s, c):
        self.pairs, self.n, self.load, self.m, self.row = pairs, n, load, m, row
        self.dst, self.gate, self.bias, self.s, self.c = dst, gate, bias, s, c


class Shared:

    def __init__(self, sem):
        self.sem, self.base = sem, 0

    def at(self, n):
        return self.sem, self.base + n


def setup(nc, ctx, dram):
    k = Kernel(nc, ctx, dram)

    def sb(name, shape, dt=F32):
        return ctx.enter_context(nc.sbuf_tensor(name, shape, dt))

    k.big = sb("big", [P, BIG])
    k.ps = ctx.enter_context(nc.psum_tensor("ps", [P, BANKS, 512], F32))
    k.ident = sb("ident", [P, P])
    k.ones = sb("ones", [P, P])
    k.key_before = sb("key_before", [P, P])
    k.key_upto = sb("key_upto", [P, P])
    k.key_after = sb("key_after", [P, P])
    k.key_from = sb("key_from", [P, P])
    k.iota = sb("iota", [P, P])
    k.cols = sb("cols", [P, N_COLUMNS])
    k.mod = sb("mod", [P, 2, 48, 2])
    k.small = sb("small", [P, 512])
    k.step_v = Steps(k.sem("vector_steps"))
    k.step_a = Steps(k.sem("scalar_steps"))
    k.step_p = Steps(k.sem("pool_steps"))
    k.slot_loaded = [k.sem(f"slot{s}_loaded") for s in range(SLOTS)]
    k.x = k.big[:, R_X:R_X + 2048].rearrange("p (a d) -> p a d", a=TT)
    k.cx = k.big[:, R_CTX:R_CTX + 2048].rearrange("p (a d) -> p a d", a=TT)

    k.shared = {n: Shared(k.sem(n)) for n in ("tile_full", "tile_free", "rows_normed", "chunk_turned", "chunk_stored",
                                             "diag_made", "row_full", "row_kept")}
    return k


def work(k, at, n):
    assert at + n <= BIG - R_WORK, (at, n)
    return k.big[:, R_WORK + at:R_WORK + at + n]


def slot(k, n):
    s = R_RING + (n % SLOTS) * SLOT
    return k.big[:, s:s + SLOT]


def plan_loads(k):
    d = k.dram

    def add(name, width, view):
        k.stage.setdefault(name, len(k.loads))
        k.loads.append((width, view))

    def tiles(name, w, n0, n1, step=512):
        v = w.rearrange("(c p) n -> p c n", p=P)
        for a in range(n0, n1, step):
            b = min(a + step, n1)
            add(name, v.shape[1] * (b - a), v[:, :, a:b])

    def experts(name, layer):
        k.stage.setdefault(name, len(k.loads))
        for s in range(6):
            w = d[("moe_w_gate_2", "moe_w_up_2", "moe_w_down_2")[s // 2]][layer]
            k.loads.append((SLOT, w[0].rearrange("(c p) n -> p c n", p=P)[:, 4 * (s % 2):4 * (s % 2) + 4, :]))
        for s in range(6 * (EXPERTS - 1)):
            k.loads.append(None)

    tiles("proj", d["w_in"][0], 0, 4352)
    tiles("mem_kv", d["w_mem_kv"][0], 0, D)
    tiles("o_sb", d["w_o_sb"][0], 0, D, D)
    tiles("o_dil", d["w_o_dil"][0], 0, D, D)
    tiles("o_mem", d["w_o_mem"][0], 0, D, D)
    for half in range(2):
        for br in range(3):
            tiles("gate", d["w_gate"][0], br * D + half * 512, br * D + half * 512 + 512)
    tiles("mix_out", d["w_out"][0], 0, D)
    tiles("peer_q", d["w_peer_q"][0], 0, 2048)
    add("subkeys", 2048, d["subkeys_t"])
    for layer in range(2):
        tiles("ada", d["ada_w_2"][layer], 0, 6 * D)
    tiles("a_in", d["mlstm_w_in_2"][0], 0, 3072)
    tiles("a_gates", d["mlstm_w_in_2"][0], 3072, 3104)
    tiles("a_out", d["mlstm_w_out_2"][0], 0, D)
    experts("moe0", 0)
    tiles("b_in", d["ret_w_in_2"][0], 0, 4096)
    tiles("b_out", d["ret_w_out_2"][0], 0, D)
    experts("moe1", 1)


def issue(k, eng, upto):
    upto = min(upto, len(k.loads) if k.peer_done else k.stage["a_in"])
    for n in range(k.issued, upto):
        width, src = k.loads[n]
        m = n - SLOTS
        if m in k.release:
            eng.wait_ge(*k.release[m])
        else:
            assert m < 0 or m in k.used, (n, m)
        dst = slot(k, n)[:, 0:width]
        if len(src.shape) == 3:
            dst = dst.rearrange("p (c n) -> p c n", c=src.shape[1])
        eng.dma_start(dst, src).then_inc(k.slot_loaded[n % SLOTS], 16)
    k.issued = max(k.issued, upto)


def retire(k):
    k.used |= set(k.release)
    k.release.clear()


def arrived(k, eng, n):
    eng.wait_ge(k.slot_loaded[n % SLOTS], 16 * (n // SLOTS + 1))


def rsqrt(k, eng, v, r, tmp):
    st = k.step_v.after
    st(eng, eng.tensor_scalar(tmp.bitcast(I32), v.bitcast(I32), 1, None, ALU.arith_shift_right))
    st(eng, eng.tensor_scalar(r.bitcast(I32), tmp.bitcast(I32), -1.0, 1597463007.0, ALU.mult, ALU.add))
    for _ in range(4):
        st(eng, eng.tensor_tensor(tmp, r, r, ALU.mult))
        st(eng, eng.tensor_tensor(tmp, tmp, v, ALU.mult))
        st(eng, eng.tensor_scalar(tmp, tmp, -0.5, 1.5, ALU.mult, ALU.add))
        st(eng, eng.tensor_tensor(r, r, tmp, ALU.mult))


def constants(k):
    nc, d = k.nc, k.dram
    loaded = k.sem("inputs_loaded")
    made = k.sem("constants_made")
    mem = work(k, 0, 2048).rearrange("p (a d) -> p a d", a=TT)
    idx = work(k, 2048, P).bitcast(I32)
    with nc.Block(no_gpsimd_drain=True) as block:
        @block.sync
        def _(sp):
            for dst, name in ((k.x, "x"), (mem, "mem"), (k.cx, "ctx_2")):
                sp.dma_start(dst, d[name][0].rearrange("(a p) d -> p a d", p=P)).then_inc(loaded, 16)
            sp.dma_start(k.cols[:], d["columns"]).then_inc(loaded, 16)
            issue(k, sp, SLOTS)
            sp.wait_ge(loaded, 64)

        @block.gpsimd
        def _(pool):
            st = k.step_p.after
            st(pool, pool.memset(k.ones[:], 1.0))
            st(pool, pool.memset(k.ident[:], 0.0))
            pool.affine_select(out=k.ident[:], in_=k.ident[:], compare_op=ALU.not_equal, fill=1.0, base=0,
                               pattern=[[-1, P]], channel_multiplier=1).then_inc(made, 1)
            for dst, base, sign in ((k.key_before, -1, 1), (k.key_upto, 0, 1),
                                    (k.key_after, -1, -1), (k.key_from, 0, -1)):
                pool.affine_select(out=dst[:], in_=k.ones[:], compare_op=ALU.is_ge, fill=0.0, base=base,
                                   pattern=[[sign, P]], channel_multiplier=-sign).then_inc(made, 1)
            st(pool, pool.iota(idx, pattern=[[1, P]], base=0, channel_multiplier=0))
            pool.tensor_copy(k.iota[:], idx).then_inc(made, 1)
            pool.wait_ge(made, 6)


def norm_transpose(k, name, tiles, xn, ht, affine, upto=0):
    nc = k.nc
    n = len(tiles)
    normed, full, free = (k.shared[s] for s in ("rows_normed", "chunk_turned", "chunk_stored"))
    ss, v, r, tmp = (k.small[:, 4 * j:4 * j + n] for j in range(4))
    with nc.Block(no_gpsimd_drain=True) as block:
        @block.vector
        def _(dve):
            st = k.step_v.after
            for t in range(n):
                st(dve, dve.scalar_tensor_tensor(out=xn[:, t, :], in0=tiles[t], scalar=1.0, in1=tiles[t],
                                                 op0=ALU.mult, op1=ALU.mult, accum_out=ss[:, t:t + 1]))
            st(dve, dve.tensor_scalar(v, ss, 1.0 / D, EPS, ALU.mult, ALU.add))
            rsqrt(k, dve, v, r, tmp)
            for t in range(n):
                dve.tensor_scalar(xn[:, t, :], tiles[t], r[:, t:t + 1], None, ALU.mult).then_inc(normed.sem, 1)

        @block.tensor
        def _(pe):
            pe.wait_ge(*normed.at(n))
            for c in range(C):
                if c >= 4:
                    pe.wait_ge(*free.at(c - 3))
                for t in range(n):
                    last = pe.transpose(k.ps[:, c % 4, t * P:(t + 1) * P], xn[:, t, c * P:(c + 1) * P], k.ident[:])
                last.then_inc(full.sem, 1)

        @block.scalar
        def _(act):
            for c in range(C):
                act.wait_ge(*full.at(c + 1))
                for s, (scale, shift) in enumerate(affine):
                    a, b = s * T, s * T + T
                    last = act.activation(ht[:, c, a:b], k.ps[:, c % 4, a:b], ACT.Identity,
                                          scale=scale[:, c:c + 1], bias=0.0 if shift is None else shift[:, c:c + 1])
                last.then_inc(free.sem, 1)

        @block.sync
        def _(sp):
            issue(k, sp, upto)
    normed.base, full.base, free.base = normed.base + n, full.base + C, free.base + C


def gemm(k, name, tiles, evac, upto, engine="act", banks=4):
    nc = k.nc
    full, free = k.shared["tile_full"], k.shared["tile_free"]

    def bank(i):
        t = tiles[i]
        return k.ps[t.row:t.row + t.m, i % banks, 0:t.n]

    def empty(eng):
        for i, t in enumerate(tiles):
            eng.wait_ge(*full.at(i + 1))
            if i and engine == "dve":
                eng.wait_ge(*free.at(i))
            evac(eng, t, bank(i)).then_inc(free.sem, 1)

    with nc.Block(no_gpsimd_drain=True) as block:
        @block.tensor
        def _(pe):
            seen = None
            for i, t in enumerate(tiles):
                if t.load is not None and t.load != seen:
                    arrived(k, pe, t.load)
                    seen = t.load
                if i >= banks:
                    pe.wait_ge(*free.at(i - banks + 1))
                for j, (lhsT, rhs) in enumerate(t.pairs):
                    last = pe.matmul(bank(i), lhsT, rhs, start=(j == 0), stop=(j == len(t.pairs) - 1))
                last.then_inc(full.sem, 1)
                if t.load is not None:
                    k.release[t.load] = full.at(i + 1)

        if engine == "act":
            block.scalar(empty)
        else:
            block.vector(empty)

        @block.sync
        def _(sp):
            issue(k, sp, upto)
    retire(k)
    full.base, free.base = full.base + len(tiles), free.base + len(tiles)


def tile(pairs, n, load=None, m=P, row=0, dst=None, gate=None, bias=None, s=None, c=None):
    return Tile(pairs, n, load, m, row, dst, gate, bias, s, c)


def weights(k, n, step):
    w = slot(k, n)
    return w[:, 0:(k.loads[n][0])].rearrange("p (c n) -> p c n", n=step)


class Modulations:

    TILES = 24

    def __init__(self, k, at):
        self.k, self.first = k, k.stage["ada"]
        self.sc, self.pick = work(k, at, 16), work(k, at + 16, 2)
        self.res = [work(k, at + 18 + 512 * j, 512) for j in range(2)]
        self.ready, self.full, self.done, self.kept, self.turned = (
            k.sem(f"mod_{s}") for s in ("sigmoid", "full", "silu", "kept", "turned"))

    def scalar(self, act):
        k = self.k
        act.activation(self.sc, k.col("cvec"), ACT.Sigmoid).then_inc(self.ready, 1)
        for a in range(self.TILES):
            act.wait_ge(self.full, a + 1)
            if a >= 2:
                act.wait_ge(self.turned, a - 1)
            act.activation(self.res[a % 2], k.ps[:, 4 + a % 2, :], ACT.Copy).then_inc(self.kept, 1)

    def vector_start(self, dve):
        k, pick = self.k, self.pick
        st = k.step_v.after
        dve.memset(k.ps[:, 4:6, :], 0.0).then_inc(self.done, 1)
        st(dve, dve.tensor_tensor(pick, k.ident[:, 0:2], k.ident[:, 32:34], ALU.add))
        st(dve, dve.tensor_tensor(pick, pick, k.ident[:, 64:66], ALU.add))
        dve.tensor_tensor(pick, pick, k.ident[:, 96:98], ALU.add).then_inc(self.done, 1)
        dve.wait_ge(self.ready, 1)
        dve.tensor_tensor(self.sc, self.sc, k.col("cvec"), ALU.mult).then_inc(self.done, 1)

    def vector_end(self, dve):
        k = self.k
        for layer in range(2):
            dve.wait_ge(self.turned, 12 * (layer + 1))
            bias = k.col("ada_b")[:, 48 * layer:48 * layer + 48]
            k.step_v.after(dve, dve.tensor_tensor(k.mod[:, layer, :, :],
                                                  k.ps[:, 6 + layer, 0:96].rearrange("p (n s) -> p n s", s=2),
                                                  bias.unsqueeze(2).to_broadcast([P, 48, 2]), ALU.add))

    def tensor(self, pe):
        k = self.k

        def turn_rows(a):
            pe.wait_ge(self.kept, a + 1)
            for b in range(4):
                at = 2 * (4 * (a % 12) + b)
                last = pe.matmul(k.ps[:, 6 + a // 12, at:at + 2], self.res[a % 2][:, b * P:(b + 1) * P], self.pick,
                                 start=True, stop=True)
            last.then_inc(self.turned, 1)

        pe.wait_ge(self.done, 3)
        for a in range(self.TILES):
            n = self.first + a
            arrived(k, pe, n)
            if a >= 2:
                pe.wait_ge(self.kept, a - 1)
            w = weights(k, n, 512)
            for c in range(C):
                q = 32 * (c % 4)
                last = pe.matmul(k.ps[q:q + 2, 4 + a % 2, :], self.sc[:, 2 * c:2 * c + 2], w[:, c, :], start=(c < 4),
                                 stop=(c >= 4), skip_group_check=True)
            last.then_inc(self.full, 1)
            k.release[n] = (self.full, a + 1)
            if a:
                turn_rows(a - 1)
        turn_rows(self.TILES - 1)


def first_projections(k):
    xn = work(k, 0, 2048).rearrange("p (a d) -> p a d", a=TT)
    mem = work(k, 0, 2048).rearrange("p (a d) -> p a d", a=TT)
    k.ht = work(k, 2048, 2048).rearrange("p (c t) -> p c t", c=C)
    mht = work(k, 4096, 2048).rearrange("p (c t) -> p c t", c=C)
    k.tok = work(k, 6144, 6656).rearrange("p (a n) -> p a n", a=TT)
    k.kv = work(k, 12800, 2048).rearrange("p (a n) -> p a n", a=TT)
    k.qkt = work(k, 14848, 2048).rearrange("p (c t) -> p c t", c=C)
    mn = work(k, 16896, 2048).rearrange("p (a d) -> p a d", a=TT)
    norm_transpose(k, "mem", [mem[:, t, :] for t in range(TT)], mn, mht, [(k.col("g_mem"), None)])
    norm_transpose(k, "x1", [k.x[:, t, :] for t in range(TT)], xn, k.ht, [(k.col("g_mix"), None)])
    tiles = []
    p0, m0 = k.stage["proj"], k.stage["mem_kv"]
    for a in range(2):
        w = weights(k, p0 + a, 512)
        for b in range(4):
            tiles.append(tile([(w[:, c, b * P:(b + 1) * P], k.ht[:, c, :]) for c in range(C)], T, p0 + a,
                              dst=k.qkt[:, 4 * a + b, :]))
    for a in range(2, 9):
        n = min(512, 4352 - 512 * a)
        w = weights(k, p0 + a, n)
        for t in range(TT):
            at = 512 * (a - 2)
            tiles.append(tile([(k.ht[:, c, t * P:(t + 1) * P], w[:, c, :]) for c in range(C)], n, p0 + a,
                              dst=k.tok[:, t, at:at + n]))
    for a in range(2):
        w = weights(k, m0 + a, 512)
        for t in range(TT):
            tiles.append(tile([(mht[:, c, t * P:(t + 1) * P], w[:, c, :]) for c in range(C)], 512, m0 + a,
                              dst=k.kv[:, t, 512 * a:512 * a + 512]))
    gemm(k, "proj", tiles, lambda eng, t, ps: eng.activation(t.dst, ps, ACT.Copy), m0 + 2 + SLOTS)


def stick_breaking(k):
    nc = k.nc
    z_full, sp_ready, bet_full, a_ready, o_full, o_done = (
        k.sem(f"sb_{s}") for s in ("scores", "softplus", "between", "weights", "out", "stored"))
    act_in, act_out = k.sem("sb_abs"), k.sem("sb_logs")
    zb_ready, ex_done = k.sem("sb_exponent"), k.sem("sb_exp")
    W, HB = 384, 4
    A = work(k, 0, HB * W).rearrange("p (h w) -> p h w", h=HB)
    B = work(k, 4096, HB * W).rearrange("p (h w) -> p h w", h=HB)
    M = work(k, 16896, HB * W).rearrange("p (h w) -> p h w", h=HB)
    mask = work(k, 18432, W)
    k.o_sb = work(k, 18944, 1024).rearrange("p (c t) -> p c t", c=4)
    scale = SB_DIM ** -0.5

    def head(h):
        return h // 2, SB_DIM * (h % 2)

    with nc.Block(no_gpsimd_drain=True) as block:
        @block.tensor
        def _(pe):
            for g in range(SB_HEADS // HB):
                if g:
                    pe.wait_ge(o_done, g)
                for j in range(HB):
                    c, off = head(g * HB + j)
                    q, key = k.qkt[off:off + SB_DIM, c, :], k.qkt[off:off + SB_DIM, 4 + c, :]
                    pe.matmul(k.ps[:, j, 0:T], key[:, 0:P], q, start=True, stop=True)
                    last = pe.matmul(k.ps[:, j, T:W], key[:, P:T], q[:, P:T], start=True, stop=True)
                last.then_inc(z_full, 1)
                pe.wait_ge(sp_ready, g + 1)
                for j in range(HB):
                    out = k.ps[:, 4 + j, :]
                    pe.matmul(out[:, 0:P], k.key_after[:], M[:, j, 0:P], start=True, stop=True)
                    pe.matmul(out[:, P:T], k.key_after[:], M[:, j, P:T], start=True, stop=False)
                    pe.matmul(out[:, P:T], k.ones[:], M[:, j, T:W], start=False, stop=True)
                    last = pe.matmul(out[:, T:W], k.key_after[:], M[:, j, T:W], start=True, stop=True)
                last.then_inc(bet_full, 1)
                pe.wait_ge(a_ready, g + 1)
                for j in range(HB):
                    h = g * HB + j
                    c, off = head(h)
                    v = k.tok[:, :, h * SB_DIM:(h + 1) * SB_DIM]
                    out = k.ps[off:off + SB_DIM, c % 2, :]
                    pe.matmul(out[:, 0:P], v[:, 0, :], A[:, j, 0:P], start=True, stop=True)
                    pe.matmul(out[:, P:T], v[:, 0, :], A[:, j, P:T], start=True, stop=False)
                    last = pe.matmul(out[:, P:T], v[:, 1, :], A[:, j, T:W], start=False, stop=True)
                last.then_inc(o_full, 1)

        @block.scalar
        def _(act):
            st = k.step_a.after
            for g in range(SB_HEADS // HB):
                z = k.ps[:, 0:HB, 0:W]
                act.wait_ge(z_full, g + 1)
                st(act, act.activation(B, z, ACT.Copy, scale=scale))
                st(act, act.activation(A, B, ACT.Abs))
                st(act, act.activation(A, A, ACT.Exp, scale=-1.0))
                act.activation(A, A, ACT.Ln, bias=1.0).then_inc(act_out, 1)
                act.wait_ge(zb_ready, g + 1)
                act.activation(A, B, ACT.Exp).then_inc(ex_done, 1)
                act.wait_ge(o_full, g + 1)
                act.activation(k.o_sb[:, 2 * g:2 * g + 2, :], k.ps[:, 0:2, 0:T], ACT.Copy).then_inc(o_done, 1)

        @block.vector
        def _(dve):
            st = k.step_v.after
            st(dve, dve.tensor_copy(mask[:, 0:P], k.key_before[:]))
            st(dve, dve.tensor_copy(mask[:, P:T], k.ones[:]))
            st(dve, dve.tensor_copy(mask[:, T:W], k.key_before[:]))
            mb = mask.unsqueeze(1).to_broadcast([P, HB, W])
            for g in range(SB_HEADS // HB):
                dve.wait_ge(act_out, g + 1)
                A2, B2, M2 = (v.rearrange("p h w -> p (h w)") for v in (A, B, M))
                st(dve, dve.scalar_tensor_tensor(out=M2, in0=B2, scalar=0.0, in1=A2, op0=ALU.max, op1=ALU.add))
                st(dve, dve.tensor_tensor(B, B, M, ALU.subtract))
                dve.tensor_tensor(M, M, mb, ALU.mult).then_inc(sp_ready, 1)
                dve.wait_ge(bet_full, g + 1)
                dve.tensor_tensor(B, B, k.ps[:, 4:4 + HB, 0:W], ALU.subtract).then_inc(zb_ready, 1)
                dve.wait_ge(ex_done, g + 1)
                dve.tensor_tensor(A, A, mb, ALU.mult).then_inc(a_ready, 1)


def head_norms(k):
    nc = k.nc
    normed, full, free = k.sem("heads_normed"), k.sem("heads_turned"), k.sem("heads_stored")
    sq = work(k, 4096, 2048)
    nd, nm = 2 * DIL_HEADS, MEM_HEADS
    dq = k.tok[:, :, 512:512 + nd * DIL_DIM]
    mq = k.tok[:, :, 2816:3328]
    mk = k.kv[:, :, 0:512]
    groups = [(dq[:, t, :], nd, DIL_DIM) for t in range(TT)] + [(mq[:, t, :], nm, MEM_DIM) for t in range(TT)] \
        + [(mk[:, t, :], nm, MEM_DIM) for t in range(TT)]
    total = sum(g[1] for g in groups)
    ss, v, r, tmp = (k.small[:, 64 + 64 * j:64 + 64 * j + total] for j in range(4))
    k.dqt = work(k, 0, 1536).rearrange("p (c t) -> p c t", c=6)
    k.dkt = work(k, 4096 + 0, 1536).rearrange("p (c t) -> p c t", c=6)
    k.mqt = work(k, 14848, 1024).rearrange("p (c t) -> p c t", c=4)
    k.mkt = work(k, 15872, 1024).rearrange("p (c t) -> p c t", c=4)
    turns = [(dq[:, :, c * P:(c + 1) * P], k.dqt[:, c, :], "gq_dil") for c in range(6)] \
        + [(dq[:, :, 768 + c * P:768 + (c + 1) * P], k.dkt[:, c, :], "gk_dil") for c in range(6)] \
        + [(mq[:, :, c * P:(c + 1) * P], k.mqt[:, c, :], "gq_mem") for c in range(4)] \
        + [(mk[:, :, c * P:(c + 1) * P], k.mkt[:, c, :], "gk_mem") for c in range(4)]
    with nc.Block(no_gpsimd_drain=True) as block:
        @block.vector
        def _(dve):
            st = k.step_v.after
            at = 0
            for src, n, width in groups:
                s = sq[:, 0:n * width]
                st(dve, dve.tensor_tensor(s, src, src, ALU.mult))
                st(dve, dve.tensor_reduce(ss[:, at:at + n], s.rearrange("p (n w) -> p n w", n=n), AX.X, ALU.add))
                st(dve, dve.tensor_scalar(v[:, at:at + n], ss[:, at:at + n], 1.0 / width, EPS, ALU.mult, ALU.add))
                at += n
            rsqrt(k, dve, v, r, tmp)
            at = 0
            for src, n, width in groups:
                s = src.rearrange("p (n w) -> p n w", n=n)
                dve.tensor_tensor(s, s, r[:, at:at + n].unsqueeze(2).to_broadcast([P, n, width]), ALU.mult)\
                   .then_inc(normed, 1)
                at += n

        @block.tensor
        def _(pe):
            pe.wait_ge(normed, len(groups))
            for i, (src, _, _) in enumerate(turns):
                if i >= 4:
                    pe.wait_ge(free, i - 3)
                for t in range(TT):
                    last = pe.transpose(k.ps[:, i % 4, t * P:(t + 1) * P], src[:, t, :], k.ident[:])
                last.then_inc(full, 1)

        @block.scalar
        def _(act):
            for i, (_, dst, g) in enumerate(turns):
                act.wait_ge(full, i + 1)
                act.activation(dst, k.ps[:, i % 4, 0:T], ACT.Identity, scale=k.col(g), bias=0.0).then_inc(free, 1)


def softmax_attentions(k):
    nc = k.nc
    scores, soft, turned, copied, out_full, out_done, exped, maxed, idx_made = (
        k.sem(f"sm_{s}") for s in ("scores", "normed", "turned", "copied", "out", "stored", "exp", "max", "index"))
    S = [work(k, 6144 + 768 * b, 768) for b in range(2)]
    PT = [work(k, 9472 + 768 * b, 768) for b in range(2)]
    idx = work(k, 7680, 512).bitcast(I32)
    low = work(k, 6144, 512).bitcast(I32)
    far = work(k, 6656, 512)
    dist = work(k, 11008, 512)
    bar = work(k, 16896, 1536)
    k.o_dil = work(k, 18432, 512).rearrange("p (c t) -> p c t", c=2)
    k.o_mem = work(k, 19968, 1024).rearrange("p (c t) -> p c t", c=4)
    neg, tot, inv = (k.small[:, 320 + 2 * j:322 + 2 * j] for j in range(3))
    units = [("dil", h, t) for t in range(TT) for h in range(DIL_SLOTS)] + \
            [("mem", h, t) for t in range(TT) for h in range(MEM_HEADS)]
    dv = k.tok[:, :, 2048:2816]
    mv = k.kv[:, :, 512:1024]
    flat = k.ps[:].rearrange("p b n -> p (b n)")

    def width(u):
        return P * (u[2] + 1) if u[0] == "dil" else T

    def groups(u):
        return DIL_GROUPS if u[0] == "dil" else 1

    def block_of(u, buf):
        return buf[:, 0:groups(u) * T].rearrange("p (g j) -> p g j", j=T)[:, :, 0:width(u)]

    with nc.Block(no_gpsimd_drain=True) as block:
        @block.gpsimd
        def _(pool):
            pool.iota(idx, pattern=[[P, TT], [-1, T]], base=0, channel_multiplier=1).then_inc(idx_made, 1)

        @block.tensor
        def _(pe):
            def score(i):
                kind, h, t = u = units[i]
                if i >= 2:
                    pe.wait_ge(maxed, i - 1)
                base = 1024 * (i % 2)
                for g in range(groups(u)):
                    out = flat[:, base + T * g:base + T * g + width(u)]
                    if kind == "dil":
                        head = DIL_SLOTS * g + h
                        off, c = DIL_DIM * (head % 2), head // 2
                        last = pe.matmul(out, k.dqt[off:off + DIL_DIM, c, t * P:(t + 1) * P],
                                         k.dkt[off:off + DIL_DIM, c, 0:width(u)], start=True, stop=True)
                    else:
                        last = pe.matmul(out, k.mqt[:, h, t * P:(t + 1) * P], k.mkt[:, h, :], start=True, stop=True)
                last.then_inc(scores, 1)

            score(0)
            score(1)
            for i, u in enumerate(units):
                kind, h, t = u
                kts = width(u) // P
                pe.wait_ge(soft, i + 1)
                if i:
                    pe.wait_ge(copied, i)
                for g in range(groups(u)):
                    for j in range(kts):
                        at = 2048 + P * (g * kts + j)
                        last = pe.transpose(flat[:, at:at + P], S[i % 2][:, T * g + P * j:T * g + P * j + P], k.ident[:])
                last.then_inc(turned, 1)
                if i + 2 < len(units):
                    score(i + 2)
                pe.wait_ge(copied, i + 1)
                if i >= 2:
                    pe.wait_ge(out_done, i - 1)
                n = groups(u) * kts
                off = DIL_DIM * (h % 2)
                for j in range(n):
                    g, kt = j // kts, j % kts
                    if kind == "dil":
                        v = dv[:, kt, (DIL_SLOTS * g + h) * DIL_DIM:(DIL_SLOTS * g + h + 1) * DIL_DIM]
                        out = k.ps[off:off + DIL_DIM, 6 + i % 2, 0:P]
                    else:
                        v, out = mv[:, kt, h * P:(h + 1) * P], k.ps[:, 6 + i % 2, 0:P]
                    last = pe.matmul(out, v, PT[i % 2][:, j * P:(j + 1) * P], start=(j == 0), stop=(j == n - 1))
                last.then_inc(out_full, 1)

        @block.vector
        def _(dve):
            st = k.step_v.after
            dve.wait_ge(idx_made, 1)
            st(dve, dve.tensor_copy(dist, idx))
            st(dve, dve.tensor_scalar(far, dist, 0.0, NEG, ALU.is_lt, ALU.mult))
            for g, dil in enumerate(DILATIONS):
                b = bar[:, 512 * g:512 * g + 512]
                st(dve, dve.tensor_scalar(low, idx, dil - 1, None, ALU.bitwise_and))
                st(dve, dve.tensor_scalar(b, low, 0.0, NEG, ALU.not_equal, ALU.mult))
                st(dve, dve.tensor_tensor(b, b, far, ALU.min))
            for g, dil in enumerate(DILATIONS):
                if DIL_REACH * dil < T:
                    b = bar[:, 512 * g:512 * g + 512]
                    st(dve, dve.tensor_scalar(far, dist, float(DIL_REACH * dil), NEG, ALU.is_gt, ALU.mult))
                    st(dve, dve.tensor_tensor(b, b, far, ALU.min))

            def biased(i):
                kind, h, t = u = units[i]
                dve.wait_ge(scores, i + 1)
                if i >= 2:
                    dve.wait_ge(turned, i - 1)
                s = block_of(u, S[i % 2])
                ps = block_of(u, flat[:, 1024 * (i % 2):1024 * (i % 2) + 1024])
                if kind == "dil":
                    b = bar.rearrange("p (g t j) -> p g t j", g=DIL_GROUPS, t=TT)[:, :, t, 0:width(u)]
                    st(dve, dve.scalar_tensor_tensor(out=s, in0=ps, scalar=DIL_DIM ** -0.5, in1=b,
                                                     op0=ALU.mult, op1=ALU.add))
                    for g in range(DIL_GROUPS):
                        slope = 2.0 ** (-8.0 * (DIL_SLOTS * g + h + 1) / DIL_HEADS)
                        sg = S[i % 2][:, T * g:T * g + width(u)]
                        last = dve.scalar_tensor_tensor(out=sg, in0=dist[:, T * t:T * t + width(u)], scalar=-slope,
                                                        in1=sg, op0=ALU.mult, op1=ALU.add)
                        st(dve, last)
                else:
                    st(dve, dve.tensor_scalar(s, ps, MEM_DIM ** -0.5, None, ALU.mult))
                dve.tensor_reduce(neg[:, i % 2:i % 2 + 1], s, AX.XY, ALU.max, negate=True).then_inc(maxed, 1)

            biased(0)
            for i, u in enumerate(units):
                if i + 1 < len(units):
                    biased(i + 1)
                dve.wait_ge(exped, i + 1)
                b = slice(i % 2, i % 2 + 1)
                st(dve, dve.reciprocal(inv[:, b], tot[:, b]))
                s = block_of(u, S[i % 2])
                dve.tensor_scalar(s, s, inv[:, b], None, ALU.mult).then_inc(soft, 1)

        @block.scalar
        def _(act):
            def exp(i):
                act.wait_ge(maxed, i + 1)
                b = slice(i % 2, i % 2 + 1)
                if i >= 2:
                    act.wait_ge(soft, i - 1)
                s = block_of(units[i], S[i % 2])
                act.activation(s, s, ACT.Exp, bias=neg[:, b], accum_out=tot[:, b]).then_inc(exped, 1)

            exp(0)
            for i, u in enumerate(units):
                kind, h, t = u
                if i + 1 < len(units):
                    exp(i + 1)
                act.wait_ge(turned, i + 1)
                if i >= 2:
                    act.wait_ge(out_full, i - 1)
                n = P * groups(u) * (width(u) // P)
                act.activation(PT[i % 2][:, 0:n], flat[:, 2048:2048 + n], ACT.Copy).then_inc(copied, 1)
                act.wait_ge(out_full, i + 1)
                if kind == "dil":
                    off = DIL_DIM * (h % 2)
                    act.activation(k.o_dil[off:off + DIL_DIM, h // 2, t * P:(t + 1) * P],
                                   k.ps[off:off + DIL_DIM, 6 + i % 2, 0:P], ACT.Copy).then_inc(out_done, 1)
                else:
                    act.activation(k.o_mem[:, h, t * P:(t + 1) * P], k.ps[:, 6 + i % 2, 0:P], ACT.Copy)\
                       .then_inc(out_done, 1)


def gated_merge(k):
    nc = k.nc
    y = work(k, 4096, 6144).rearrange("p (b a d) -> p b a d", b=3, a=TT)
    merged = work(k, 10240, 2048).rearrange("p (a d) -> p a d", a=TT)
    gates = [work(k, 12288 + 512 * b, 512) for b in range(2)]
    b_gate = work(k, 13312, 3072)[0:1, :]
    mt = work(k, 16384, 2048).rearrange("p (c t) -> p c t", c=C)
    tiles = []
    for br, (name, o) in enumerate((("o_sb", k.o_sb), ("o_dil", k.o_dil), ("o_mem", k.o_mem))):
        n = k.stage[name]
        w = weights(k, n, D)
        for t in range(TT):
            for half in range(2):
                cs = slice(512 * half, 512 * half + 512)
                tiles.append(tile([(o[:, c, t * P:(t + 1) * P], w[:, c, cs]) for c in range(w.shape[1])], 512, n,
                                  dst=y[:, br, t, cs]))
    gemm(k, "branches", tiles, lambda eng, t, ps: eng.activation(t.dst, ps, ACT.Copy), k.stage["gate"] + SLOTS)

    loaded, full, opened, merged_n = (k.sem(f"gates_{s}") for s in ("bias", "full", "open", "merged"))
    g0 = k.stage["gate"]
    order = [(half, br, t) for half in range(2) for br in range(3) for t in range(TT)]
    with nc.Block(no_gpsimd_drain=True) as block:
        @block.tensor
        def _(pe):
            pe.wait_ge(loaded, 16)
            for i, (half, br, t) in enumerate(order):
                n = g0 + 3 * half + br
                arrived(k, pe, n)
                if i >= 4:
                    pe.wait_ge(opened, i - 3)
                w = weights(k, n, 512)
                for c in range(C):
                    pe.matmul(k.ps[:, i % 4, :], k.ht[:, c, t * P:(t + 1) * P], w[:, c, :], start=(c == 0), stop=False)
                at = D * br + 512 * half
                pe.matmul(k.ps[:, i % 4, :], k.ones[0:1, :], b_gate[:, at:at + 512], start=False, stop=True)\
                  .then_inc(full, 1)
                k.release[n] = (full, i + 1)

        @block.scalar
        def _(act):
            for i in range(len(order)):
                act.wait_ge(full, i + 1)
                if i >= 2:
                    act.wait_ge(merged_n, i - 1)
                act.activation(gates[i % 2], k.ps[:, i % 4, :], ACT.Sigmoid).then_inc(opened, 1)

        @block.vector
        def _(dve):
            for i, (half, br, t) in enumerate(order):
                dve.wait_ge(opened, i + 1)
                cs = slice(512 * half, 512 * half + 512)
                g, out = gates[i % 2], merged[:, t, cs]
                if br == 0:
                    dve.tensor_tensor(out, g, y[:, br, t, cs], ALU.mult).then_inc(merged_n, 1)
                else:
                    k.step_v.after(dve, dve.tensor_tensor(g, g, y[:, br, t, cs], ALU.mult))
                    dve.wait_ge(merged_n, i)
                    dve.tensor_tensor(out, out, g, ALU.add).then_inc(merged_n, 1)

        @block.sync
        def _(sp):
            sp.dma_start(b_gate, k.dram["b_gate"]).then_inc(loaded, 16)
            issue(k, sp, g0 + 6 + SLOTS)
            sp.wait_ge(loaded, 16)
    retire(k)
    turn(k, "merged", merged, mt, None)
    n0 = k.stage["mix_out"]
    tiles = []
    for a in range(2):
        w = weights(k, n0 + a, 512)
        for t in range(TT):
            tiles.append(tile([(mt[:, c, t * P:(t + 1) * P], w[:, c, :]) for c in range(C)], 512, n0 + a,
                              dst=k.x[:, t, 512 * a:512 * a + 512]))
    gemm(k, "mix_out", tiles, lambda eng, t, ps: eng.tensor_tensor(t.dst, t.dst, ps, ALU.add), n0 + 2 + SLOTS, "dve")


def turn(k, name, src, dst, scale):
    full, free = k.shared["chunk_turned"], k.shared["chunk_stored"]
    n, chunks = src.shape[1], src.shape[2] // P
    with k.nc.Block(no_gpsimd_drain=True) as block:
        @block.tensor
        def _(pe):
            for c in range(chunks):
                if c >= 4:
                    pe.wait_ge(*free.at(c - 3))
                for t in range(n):
                    last = pe.transpose(k.ps[:, c % 4, t * P:(t + 1) * P], src[:, t, c * P:(c + 1) * P], k.ident[:])
                last.then_inc(full.sem, 1)

        @block.scalar
        def _(act):
            for c in range(chunks):
                act.wait_ge(*full.at(c + 1))
                ps = k.ps[:, c % 4, 0:n * P]
                if scale is None:
                    act.activation(dst[:, c, :], ps, ACT.Copy).then_inc(free.sem, 1)
                else:
                    act.activation(dst[:, c, :], ps, ACT.Identity, scale=scale[:, c:c + 1], bias=0.0).then_inc(free.sem, 1)
    full.base, free.base = full.base + chunks, free.base + chunks


def peer_select(k):
    nc = k.nc
    xn = work(k, 4096, 2048).rearrange("p (a d) -> p a d", a=TT)
    k.h2t = work(k, 8192, 2048).rearrange("p (c t) -> p c t", c=C)
    qpt = work(k, 0, 4096).rearrange("p (h t) -> p h t", h=16)
    sc = work(k, 10240, 4096).rearrange("p (a h n) -> p a h n", a=TT, h=16)
    norm_transpose(k, "x2", [k.x[:, t, :] for t in range(TT)], xn, k.h2t, [(k.col("g_ffn"), None)])
    q0, s0 = k.stage["peer_q"], k.stage["subkeys"]
    tiles = []
    for a in range(4):
        w = weights(k, q0 + a, 512)
        for b in range(4):
            tiles.append(tile([(w[:, c, b * P:(b + 1) * P], k.h2t[:, c, :]) for c in range(C)], T, q0 + a,
                              dst=qpt[:, 4 * a + b, :]))
    gemm(k, "peer_q", tiles, lambda eng, t, ps: eng.activation(t.dst, ps, ACT.Copy), s0 + SLOTS)
    keys = slot(k, s0)[:, 0:2048].rearrange("p (h n) -> p h n", h=16)
    tiles = [tile([(qpt[:, h, t * P:(t + 1) * P], keys[:, h, :])], P, s0, dst=sc[:, t, h, :])
             for t in range(TT) for h in range(16)]
    gemm(k, "peer_scores", tiles, lambda eng, t, ps: eng.activation(t.dst, ps, ACT.Copy), s0 + 1 + SLOTS, banks=8)

    K, H = PEER_TOPK, PEER_HEADS
    NV = 2 * H * K
    vals = work(k, 0, 512).rearrange("p (a h n) -> p a h n", a=TT, h=16)
    inds = work(k, 512, 512).bitcast(U32).rearrange("p (a h n) -> p a h n", a=TT, h=16)
    indf = work(k, 1024, 512).rearrange("p (a h n) -> p a h n", a=TT, h=16)
    tops = work(k, 1536, 256).rearrange("p (a h n) -> p a h n", a=TT, h=H)
    pos = work(k, 1792, 256).bitcast(U32).rearrange("p (a h n) -> p a h n", a=TT, h=H)
    rest = work(k, 2048, P)
    cand = work(k, 2176, 256)
    rest2 = work(k, 2432, 256)
    half = work(k, 2688, 256).bitcast(U32)
    halff = work(k, 2944, 256).rearrange("p (a h n) -> p a h n", a=TT, h=H)
    pick = work(k, 3200, 512).rearrange("p (s a h n) -> p s a h n", s=2, a=TT, h=H)
    gate = work(k, 3712, 256).rearrange("p (a h n) -> p a h n", a=TT, h=H)
    one_hot = work(k, 4096, 2048).rearrange("p (h n m) -> p h n m", h=H, n=K)
    k.e_t = work(k, 18432, 768).rearrange("p (s t) -> p s t", s=3)
    sums, inv = k.small[:, 0:16], k.small[:, 16:32]
    mods = Modulations(k, 6144)
    shifted, exped, ready, full, stored = (k.sem(f"select_{s}") for s in ("shifted", "exp", "ready", "turned", "stored"))
    with nc.Block(no_gpsimd_drain=True) as block:
        @block.vector
        def _(dve):
            st = k.step_v.after
            low = -3.0e38
            mods.vector_start(dve)

            def best(v, i, src, scratch):
                st(dve, dve.max(v[:, 0:8], src))
                st(dve, dve.max_index(i[:, 0:8], v[:, 0:8], src))
                st(dve, dve.match_replace(scratch, v[:, 0:8], src, low))
                st(dve, dve.max(v[:, 8:16], scratch))
                st(dve, dve.max_index(i[:, 8:16], v[:, 8:16], scratch))

            for t in range(TT):
                for h in range(16):
                    best(vals[:, t, h, :], inds[:, t, h, :], sc[:, t, h, :], rest)
                for h in range(H):
                    st(dve, dve.tensor_tensor(cand.rearrange("p (a b) -> p a b", a=K),
                                              vals[:, t, 2 * h, :].unsqueeze(2).to_broadcast([P, K, K]),
                                              vals[:, t, 2 * h + 1, :].unsqueeze(1).to_broadcast([P, K, K]), ALU.add))
                    best(tops[:, t, h, :], pos[:, t, h, :], cand, rest2)
            st(dve, dve.tensor_copy(indf, inds))
            for s in range(2):
                h_ = half.rearrange("p (a h n) -> p a h n", a=TT, h=H)
                if s == 0:
                    st(dve, dve.tensor_scalar(h_, pos, 4, None, ALU.logical_shift_right))
                else:
                    st(dve, dve.tensor_scalar(h_, pos, 15, None, ALU.bitwise_and))
                st(dve, dve.tensor_copy(halff, h_))
                for t in range(TT):
                    st(dve, dve.tensor_tensor(one_hot.rearrange("p h n m -> p (h n) m"),
                                              halff[:, t, :, :].rearrange("p h n -> p (h n)").unsqueeze(2)
                                              .to_broadcast([P, H * K, K]),
                                              k.iota[:, 0:K].unsqueeze(1).to_broadcast([P, H * K, K]), ALU.is_equal))
                    src = indf[:, t, :, :].rearrange("p (h s) n -> p s h n", s=2)[:, s, :, :]
                    st(dve, dve.tensor_tensor(one_hot, one_hot, src.unsqueeze(2).to_broadcast([P, H, K, K]), ALU.mult))
                    st(dve, dve.tensor_reduce(pick[:, s, t, :, :].rearrange("p h n -> p (h n)"),
                                              one_hot.rearrange("p h n m -> p (h n) m"), AX.X, ALU.add))
            t3 = tops.rearrange("p a h n -> p (a h) n")
            g3 = gate.rearrange("p a h n -> p (a h) n")
            dve.tensor_tensor(g3, t3, t3[:, :, 0:1].to_broadcast([P, TT * H, K]), ALU.subtract).then_inc(shifted, 1)
            dve.wait_ge(exped, 1)
            st(dve, dve.tensor_reduce(sums, g3, AX.X, ALU.add))
            st(dve, dve.reciprocal(inv, sums))
            dve.tensor_tensor(g3, g3, inv.unsqueeze(2).to_broadcast([P, TT * H, K]), ALU.mult).then_inc(ready, 1)
            mods.vector_end(dve)

        @block.scalar
        def _(act):
            mods.scalar(act)
            act.wait_ge(shifted, 1)
            act.activation(gate, gate, ACT.Exp).then_inc(exped, 1)
            act.wait_ge(full, 1)
            act.activation(k.e_t, k.ps[:, 0:3, 0:T], ACT.Copy).then_inc(stored, 1)

        @block.tensor
        def _(pe):
            mods.tensor(pe)
            pe.wait_ge(ready, 1)
            for s in range(3):
                for t in range(TT):
                    src = (gate[:, t, :, :] if s == 2 else pick[:, s, t, :, :]).rearrange("p h n -> p (h n)")
                    last = pe.transpose(k.ps[:, s, t * P:(t + 1) * P], src, k.ident[:])
            last.then_inc(full, 1)

        @block.sync
        def _(sp):
            issue(k, sp, k.stage["a_in"])
    retire(k)


def peer_gates(k):
    nc = k.nc
    N, STEPS = 8, 2
    TURNS = T // (N * STEPS)
    k.gates = k.big[:, R_RING:R_RING + PEER_KEYS * T].rearrange("p (i t) -> p i t", i=PEER_KEYS)
    first = [work(k, 10240 + 1024 * b, 1024).rearrange("p (t i) -> p t i", t=N) for b in range(STEPS)]
    second = [work(k, 12288 + 1024 * b, 1024).rearrange("p (t i) -> p t i", t=N) for b in range(STEPS)]
    row = k.iota[:].unsqueeze(1).to_broadcast([P, N, P])
    hot, made, full, stored = (k.sem(f"gates_{s}") for s in ("hot", "weighted", "products", "spread"))
    e_t = k.e_t

    def columns(s, t):
        return e_t[:, s, bass.ds(t, N)].unsqueeze(2).to_broadcast([P, N, P])

    with nc.Block(no_gpsimd_drain=True) as block:
        def turns(eng, body):
            for b in range(STEPS):
                body(b, b, False)
            with eng.Fori(1, TURNS) as i:
                for b in range(STEPS):
                    body(i * STEPS + b, b, True)

        @block.vector
        def _(dve):
            def step(n, b, later):
                if later:
                    dve.wait_ge(full, n - 1)
                dve.tensor_tensor(first[b], row, columns(0, n * N), ALU.is_equal).then_inc(hot, 1)
                dve.tensor_tensor(second[b], row, columns(1, n * N), ALU.is_equal).then_inc(hot, 1)
            turns(dve, step)

        @block.gpsimd
        def _(pool):
            def step(n, b, later):
                pool.wait_ge(hot, n * 2 + 1)
                pool.tensor_tensor(first[b], first[b], columns(2, n * N), ALU.mult).then_inc(made, 1)
            turns(pool, step)

        @block.tensor
        def _(pe):
            def step(n, b, later):
                pe.wait_ge(made, n + 1)
                pe.wait_ge(hot, n * 2 + 2)
                if later:
                    pe.wait_ge(stored, n - 1)
                for t in range(N):
                    last = pe.matmul(k.ps[:, 2 * b + t // 4, (t % 4) * P:(t % 4 + 1) * P],
                                     first[b][:, t, :], second[b][:, t, :], start=True, stop=True)
                last.then_inc(full, 1)
            turns(pe, step)

        @block.scalar
        def _(act):
            def step(n, b, later):
                act.wait_ge(full, n + 1)
                src = k.ps[:, 2 * b:2 * b + 2, :].rearrange("p b (t i) -> p i (b t)", i=P)
                act.activation(k.gates[:, :, bass.ds(n * N, N)], src, ACT.Copy).then_inc(stored, 1)
            turns(act, step)


def peer_experts(k):
    nc = k.nc
    RING = 4
    u_slot = [work(k, 10240 + 1024 * b, 1024).rearrange("p (c i) -> p c i", c=C) for b in range(RING)]
    v_slot = [work(k, 14336 + 1024 * b, 1024) for b in range(RING)]
    act_buf = [work(k, 19200 + T * b, T) for b in range(2)]
    w_buf = [work(k, 19712 + T * b, T) for b in range(2)]
    u_loaded = [k.sem(f"u_loaded{b}") for b in range(RING)]
    v_loaded = [k.sem(f"v_loaded{b}") for b in range(RING)]
    act_full, gelu_done, w_ready, out_done, added = (
        k.sem(f"peer_{s}") for s in ("act_full", "gelu_done", "w_ready", "out_done", "added"))
    u = k.dram["peer_u_t"].rearrange("j p c i -> p j (c i)")
    v = k.dram["peer_v"][0].rearrange("(i j) d -> i j d", j=PEER_KEYS)
    TURNS = PEER_KEYS // RING

    def one(eng, n):
        return bass.ds(n, 1)

    with nc.Block(no_gpsimd_drain=True) as block:
        @block.sync
        def _(sp):
            def load(n, b, later, turn=0):
                if later:
                    sp.wait_ge(act_full, n - 3)
                sp.dma_start(u_slot[b].rearrange("p c i -> p (c i)").unsqueeze(1), u[:, one(sp, n), :])\
                  .then_inc(u_loaded[b], 16)
                if later:
                    sp.wait_ge(out_done, n - 3)
                sp.dma_start(v_slot[b].unsqueeze(1), v[:, one(sp, n), :]).then_inc(v_loaded[b], 16)
            for b in range(RING):
                load(b, b, False)
            with sp.Fori(1, TURNS) as i:
                for b in range(RING):
                    load(i * RING + b, b, True)

        @block.tensor
        def _(pe):
            def act_of(n, b, turn, first):
                pe.wait_ge(u_loaded[b], turn * 16 + 16)
                if not first:
                    pe.wait_ge(gelu_done, n - 1)
                for c in range(C):
                    last = pe.matmul(k.ps[:, 4 + b % 2, 0:T], u_slot[b][:, c, :], k.h2t[:, c, :],
                                     start=(c == 0), stop=(c == C - 1))
                last.then_inc(act_full, 1)

            def out_of(n, b, turn, first, final):
                pe.wait_ge(w_ready, n + 1)
                pe.wait_ge(v_loaded[b], turn * 16 + 16)
                for t in range(TT):
                    for half in range(2):
                        last = pe.matmul(k.ps[:, 2 * t + half, :], w_buf[b % 2][:, t * P:(t + 1) * P],
                                         v_slot[b][:, 512 * half:512 * half + 512], start=first, stop=final,
                                         skip_group_check=True)
                last.then_inc(out_done, 1)

            def tiles(turn, first, final):
                for b in range(RING):
                    n = turn * RING + b
                    if b < RING - 1:
                        act_of(n + 1, b + 1, turn, first and b == 0)
                    elif not final:
                        act_of(n + 1, 0, turn + 1, False)
                    out_of(n, b, turn, first and b == 0, final and b == RING - 1)

            act_of(0, 0, 0, True)
            tiles(0, True, False)
            with pe.Fori(1, TURNS - 1) as i:
                tiles(i, False, False)
            tiles(TURNS - 1, False, True)

        def turns(eng, body):
            for b in range(RING):
                body(b, b, b < 2)
            with eng.Fori(1, TURNS) as i:
                for b in range(RING):
                    body(i * RING + b, b, False)

        @block.scalar
        def _(act):
            def gelu(n, b, first):
                act.wait_ge(act_full, n + 1)
                if not first:
                    act.wait_ge(w_ready, n - 1)
                act.activation(act_buf[b % 2], k.ps[:, 4 + b % 2, 0:T], ACT.Gelu).then_inc(gelu_done, 1)
            turns(act, gelu)

        @block.vector
        def _(dve):
            def weigh(n, b, first):
                dve.wait_ge(gelu_done, n + 1)
                if not first:
                    dve.wait_ge(out_done, n - 1)
                dve.tensor_tensor(w_buf[b % 2].unsqueeze(1), act_buf[b % 2].unsqueeze(1), k.gates[:, one(dve, n), :],
                                  ALU.mult).then_inc(w_ready, 1)
            turns(dve, weigh)
            dve.wait_ge(out_done, PEER_KEYS)
            for t in range(TT):
                x = k.x[:, t, :].rearrange("p (b n) -> p b n", b=2)
                dve.tensor_tensor(x, x, k.ps[:, 2 * t:2 * t + 2, :], ALU.add).then_inc(added, 1)
            dve.wait_ge(added, TT)
    k.peer_done = True


def scaled_gains(k, name, layer, gain, part):
    base = 400 + 32 * layer + (16 if part else 0)
    gs = k.small[:, base:base + 16].rearrange("p (s c) -> p s c", s=2)
    scale = k.mod[:, layer, (3 * part + 1) * C:(3 * part + 2) * C, :].rearrange("p c s -> p s c")
    with k.nc.Block(no_gpsimd_drain=True) as block:
        @block.vector
        def _(dve):
            st = k.step_v.after
            st(dve, dve.tensor_scalar(gs, scale, 1.0, None, ALU.add))
            st(dve, dve.tensor_tensor(gs, gs, gain.unsqueeze(1).to_broadcast([P, 2, C]), ALU.mult))
    shift = k.mod[:, layer, 3 * part * C:(3 * part + 1) * C, :]
    return [(gs[:, s, :], shift[:, :, s]) for s in range(2)]


def row_gates(k, name, layer, part, seqs, dst):
    nc = k.nc
    diag = work(k, 20480, 256)
    made, full, free = (k.shared[s] for s in ("diag_made", "row_full", "row_kept"))
    order = [(i, s, c) for i, s in enumerate(seqs) for c in range(C)]
    with nc.Block(no_gpsimd_drain=True) as block:
        @block.vector
        def _(dve):
            for j, (i, s, c) in enumerate(order):
                if j >= 2:
                    dve.wait_ge(*full.at(j - 1))
                dve.tensor_scalar(diag[:, P * (j % 2):P * (j % 2) + P], k.ident[:],
                                  k.mod[:, layer, part * C + c, s:s + 1], None, ALU.mult).then_inc(made.sem, 1)

        @block.tensor
        def _(pe):
            for j, (i, s, c) in enumerate(order):
                pe.wait_ge(*made.at(j + 1))
                if j >= 4:
                    pe.wait_ge(*free.at(j - 3))
                pe.matmul(k.ps[:, j % 4, 0:P], k.ones[:], diag[:, P * (j % 2):P * (j % 2) + P],
                          start=True, stop=True).then_inc(full.sem, 1)

        @block.scalar
        def _(act):
            for j, (i, s, c) in enumerate(order):
                act.wait_ge(*full.at(j + 1))
                act.activation(dst[:, i, c * P:(c + 1) * P], k.ps[:, j % 4, 0:P], ACT.Copy).then_inc(free.sem, 1)
    for s in (made, full, free):
        s.base += len(order)


def add_gated(k, buf):
    def evac(eng, t, ps):
        k.step_v.after(eng, eng.tensor_tensor(buf, ps, t.gate, ALU.mult))
        return eng.tensor_tensor(t.dst, t.dst, buf, ALU.add)
    return evac


def mlstm_inputs(k):
    nc = k.nc
    xn = work(k, 0, 4096).rearrange("p (a d) -> p a d", a=4)
    ht = work(k, 4160, 4096).rearrange("p (c t) -> p c t", c=C)
    raw = work(k, 0, 4160).rearrange("p (c s t) -> p c s t", c=C, s=2)
    k.qk = work(k, 4160, 4096).rearrange("p (c t) -> p c t", c=C)
    k.v = work(k, 8256, 4 * A_HEADS * (A_DV + 1)).rearrange("p (a h d) -> p a h d", a=4, h=A_HEADS)
    k.o = work(k, 12384, 4096).rearrange("p (a d) -> p a d", a=4)
    rows = [work(k, 16480 + 512 * j, 512)[0:16, :] for j in range(7)] + [work(k, 20480, 512)[0:16, :]]
    n0, g0 = k.stage["a_in"], k.stage["a_gates"]
    lat, con = scaled_gains(k, "a", 0, k.col("norm_mix")[:, 0:C], 0)
    norm_transpose(k, "a_norm", [k.cx[:, 0, :], k.cx[:, 1, :], k.x[:, 0, :], k.x[:, 1, :]], xn, ht, [con, lat],
                   n0 + SLOTS)
    tiles = []
    for a in range(2):
        w = weights(k, n0 + a, 512)
        for b in range(4):
            tiles.append(tile([(w[:, c, b * P:(b + 1) * P], ht[:, c, :]) for c in range(C)], 512, n0 + a,
                              dst=raw[:, 4 * a + b, :, 2:2 + T]))
    for a in range(2, 6):
        w = weights(k, n0 + a, 512)
        for t in range(4):
            dst = k.v[:, t, 4 * (a % 2):4 * (a % 2) + 4, 0:A_DV] if a < 4 \
                else k.o[:, t, 512 * (a % 2):512 * (a % 2) + 512]
            tiles.append(tile([(ht[:, c, t * P:(t + 1) * P], w[:, c, :]) for c in range(C)], 512, n0 + a, dst=dst))
    w = weights(k, g0, 32)
    for a in range(2):
        tiles.append(tile([(w[:, c, 16 * a:16 * a + 16], ht[:, c, :]) for c in range(C)], 512, g0, m=16, dst=rows[a],
                          bias=k.col(("ig_b", "fg_b")[a])[0:16, :]))

    def evac(eng, t, ps):
        if t.m == 16:
            return eng.activation(t.dst, ps, ACT.Identity, bias=t.bias)
        if len(t.dst.shape) == 3:
            ps = ps.rearrange("p (s t) -> p s t", s=t.dst.shape[1])
        return eng.activation(t.dst, ps, ACT.Copy)
    gemm(k, "a_in", tiles, evac, g0 + 1 + SLOTS)

    edges, conv, silu, logs, scans, ex, colf, kept = (
        k.sem(f"conv_{s}") for s in ("edges", "done", "silu", "logs", "scans", "exp", "columns", "kept"))
    ig, fg, ff, fb, lo, ze, m_, nm = rows
    k.neg_m = nm
    k.g_col = k.small[:, 64:128].rearrange("p (a r) -> p a r", a=4)
    k.e_col = k.small[:, 128:192].rearrange("p (a r) -> p a r", a=4)
    is_f, is_b = k.key_before[0:16, 8:9], k.key_from[0:16, 8:9]
    cw, cb = k.col("conv_w").rearrange("p (c w) -> p c w", c=C), k.col("conv_b")
    with nc.Block(no_gpsimd_drain=True) as block:
        @block.gpsimd
        def _(pool):
            pool.memset(raw[:, :, :, 0:2], 0.0).then_inc(edges, 1)
            pool.memset(raw[:, :, :, 2 + T:4 + T], 0.0).then_inc(edges, 1)
            pool.memset(ze, 0.0).then_inc(edges, 1)
            pool.memset(k.v[:, :, :, A_DV:A_DV + 1], 1.0).then_inc(edges, 1)

        @block.scalar
        def _(act):
            st = k.step_a.after
            st(act, act.activation(lo, fg, ACT.Abs))
            st(act, act.activation(lo, lo, ACT.Exp, scale=-1.0))
            act.activation(lo, lo, ACT.Ln, bias=1.0).then_inc(logs, 1)
            for c in range(C):
                act.wait_ge(conv, c + 1)
                act.activation(k.qk[:, c, :], k.qk[:, c, :], ACT.Silu, bias=cb[:, c:c + 1]).then_inc(silu, 1)
            act.wait_ge(scans, 1)
            act.activation(ff, ff, ACT.Exp, scale=-1.0).then_inc(ex, 1)
            act.wait_ge(colf, 1)
            act.activation(k.small[:, 64:192], k.ps[:, 0, 0:128], ACT.Copy).then_inc(kept, 1)

        @block.tensor
        def _(pe):
            pe.wait_ge(ex, 1)
            for j, src in enumerate((m_, ff)):
                for t in range(4):
                    last = pe.transpose(k.ps[:, 0, 64 * j + 16 * t:64 * j + 16 * t + 16], src[:, t * P:(t + 1) * P],
                                        k.ident[0:16, 0:16])
            last.then_inc(colf, 1)

        @block.vector
        def _(dve):
            st = k.step_v.after
            dve.wait_ge(edges, 4)
            for c in range(C):
                out = k.qk[:, c, :].rearrange("p (s t) -> p s t", s=2)
                st(dve, dve.tensor_scalar(out, raw[:, c, :, 0:T], cw[:, c, 0:1], None, ALU.mult))
                for w_ in range(1, CONV_W):
                    last = dve.scalar_tensor_tensor(out=out, in0=raw[:, c, :, w_:w_ + T], scalar=cw[:, c, w_:w_ + 1],
                                                    in1=out, op0=ALU.mult, op1=ALU.add)
                    if w_ < CONV_W - 1:
                        st(dve, last)
                last.then_inc(conv, 1)
            dve.wait_ge(logs, 1)
            st(dve, dve.tensor_scalar(fg, fg, 0.0, None, ALU.min))
            st(dve, dve.tensor_tensor(fg, fg, lo, ALU.subtract))

            def scan(fwd, bwd, src, other, op0, op1):
                st(dve, dve.tensor_tensor_scan(fwd, src, other, 0.0, op0, op1))
                st(dve, dve.tensor_tensor_scan(bwd[:, 0:T][:, ::-1], src[:, 0:T][:, ::-1], other[:, 0:T][:, ::-1],
                                               0.0, op0, op1))
                st(dve, dve.tensor_tensor_scan(bwd[:, T:2 * T][:, ::-1], src[:, T:2 * T][:, ::-1],
                                               other[:, T:2 * T][:, ::-1], bwd[:, 0:1], op0, op1))
                st(dve, dve.tensor_scalar(fwd, fwd, is_f, None, ALU.mult))
                st(dve, dve.scalar_tensor_tensor(out=fwd, in0=bwd, scalar=is_b, in1=fwd, op0=ALU.mult, op1=ALU.add))
            scan(ff, fb, fg, ze, ALU.add, ALU.add)
            st(dve, dve.tensor_tensor(m_, ig, ff, ALU.subtract))
            scan(lo, fb, m_, m_, ALU.max, ALU.max)
            st(dve, dve.tensor_tensor(ff, ff, lo, ALU.add))
            dve.tensor_scalar(nm, lo, -1.0, None, ALU.mult).then_inc(scans, 1)
            dve.wait_ge(silu, 4)
            q = k.qk[:, 0:4, :]
            st(dve, dve.tensor_scalar(q, q, A_DK ** -0.5, None, ALU.mult))


def mlstm_heads(k):
    nc = k.nc
    buffers = 3
    wt = [work(k, 16480 + 1280 * b, 1280) for b in range(buffers)]
    k.y = work(k, 0, 4096).rearrange("p (a d) -> p a d", a=4)
    den, inv = k.small[:, 192:196], k.small[:, 196:200]
    s_full, m_full, t_ready, e_ready, masked, w_ready, n_full, y_done = (
        k.sem(f"scan_{s}") for s in ("scores", "maxima", "exponent", "exp", "masked", "weights", "num", "out"))
    blocks = (((0, 0, 512, 0), (1, 128, 384, 0), (2, 256, 256, 0), (3, 384, 128, 0)),
              ((1, 0, 512, 128), (0, 0, 128, 0), (0, 256, 256, None), (2, 256, 128, 0), (3, 256, 256, 128)))
    units = [(h, d) for h in range(A_HEADS) for d in range(2)]

    def places(d):
        at = 0
        for kt, q0, n, diag in blocks[d]:
            yield kt, q0, n, diag, at
            at += n

    def s_of(kt, q0, n):
        if kt < 2:
            return k.ps[:, kt, q0:q0 + n]
        return k.ps[:, 2, T * (kt - 2) + q0 - T:T * (kt - 2) + q0 - T + n]

    def out_of(n):
        b = 4 + 2 * (n % 2)
        return k.ps[:, b:b + 2, :].rearrange("p b (t d) -> p (b t) d", t=2)

    with nc.Block(no_gpsimd_drain=True) as block:
        @block.tensor
        def _(pe):
            def score(h):
                if h:
                    pe.wait_ge(w_ready, 2 * h)
                off, c = A_DK * (h % 2), h // 2
                q, key = k.qk[off:off + A_DK, c, :], k.qk[off:off + A_DK, 4 + c, :]
                for kt in range(4):
                    q0 = 0 if kt < 2 else T
                    last = pe.matmul(s_of(kt, q0, 512 - q0), key[:, kt * P:(kt + 1) * P], q[:, q0:512],
                                     start=True, stop=True)
                last.then_inc(s_full, 1)

            def maxima(n):
                h, d = units[n]
                if n:
                    pe.wait_ge(t_ready, n)
                pe.matmul(k.ps[:, 3, :], k.ident[0:16, 8 * d + h:8 * d + h + 1].to_broadcast([16, P]),
                          k.neg_m, start=True, stop=True).then_inc(m_full, 1)

            score(0)
            maxima(0)
            for n, (h, d) in enumerate(units):
                if n + 1 < len(units):
                    maxima(n + 1)
                pe.wait_ge(w_ready, n + 1)
                if n + 1 < len(units) and d == 1:
                    score(h + 1)
                if n >= 2:
                    pe.wait_ge(y_done, n - 1)
                w = wt[n % buffers]
                for t in range(4):
                    terms = [(kt, at + t * P - q0) for kt, q0, m, _, at in places(d) if q0 <= t * P < q0 + m]
                    for j, (kt, a) in enumerate(terms):
                        last = pe.matmul(out_of(n)[:, t, 0:A_DV + 1], w[:, a:a + P], k.v[:, kt, h, :],
                                         start=(j == 0), stop=(j == len(terms) - 1))
                last.then_inc(n_full, 1)

        @block.vector
        def _(dve):
            st = k.step_v.after

            def exponents(n):
                h, d = units[n]
                dve.wait_ge(m_full, n + 1)
                if n >= buffers:
                    dve.wait_ge(n_full, n - buffers + 1)
                for kt, q0, m, _, at in places(d):
                    last = dve.tensor_scalar(wt[n % buffers][:, at:at + m], k.ps[:, 3, q0:q0 + m],
                                             k.g_col[:, kt, 8 * d + h:8 * d + h + 1], 0.0, ALU.add, ALU.min)
                last.then_inc(t_ready, 1)

            def weigh(n):
                h, d = units[n]
                dve.wait_ge(s_full, h + 1)
                dve.wait_ge(masked, n + 1)
                for kt, q0, m, _, at in places(d):
                    w = wt[n % buffers][:, at:at + m]
                    last = dve.tensor_tensor(w, w, s_of(kt, q0, m), ALU.mult)
                last.then_inc(w_ready, 1)

            def finish(n):
                h, d = units[n]
                dve.wait_ge(n_full, n + 1)
                d_ = out_of(n)[:, :, A_DV]
                st(dve, dve.scalar_tensor_tensor(out=inv, in0=d_, scalar=-1.0,
                                                 in1=k.e_col[:, :, 8 * d + h], op0=ALU.mult, op1=ALU.max))
                st(dve, dve.tensor_tensor(den, d_, inv, ALU.max))
                st(dve, dve.reciprocal(inv, den))
                num = out_of(n)[:, :, 0:A_DV]
                y = k.y[:, :, h * A_DV:(h + 1) * A_DV]
                if d == 0:
                    dve.tensor_tensor(y, num, inv.unsqueeze(2).to_broadcast([P, 4, P]), ALU.mult).then_inc(y_done, 1)
                    dve.wait_ge(y_done, n + 1)
                else:
                    for t in range(4):
                        last = dve.scalar_tensor_tensor(out=y[:, t, :], in0=num[:, t, :], scalar=inv[:, t:t + 1],
                                                        in1=y[:, t, :], op0=ALU.mult, op1=ALU.add)
                    last.then_inc(y_done, 1)
                    dve.wait_ge(y_done, n + 1)

            exponents(0)
            for n in range(len(units)):
                if n + 1 < len(units):
                    exponents(n + 1)
                weigh(n)
                if n:
                    finish(n - 1)
            finish(len(units) - 1)

        @block.scalar
        def _(act):
            for n in range(len(units)):
                act.wait_ge(t_ready, n + 1)
                act.activation(wt[n % buffers], wt[n % buffers], ACT.Exp).then_inc(e_ready, 1)

        @block.gpsimd
        def _(pool):
            for n, (h, d) in enumerate(units):
                pool.wait_ge(e_ready, n + 1)
                mask = k.key_from if d else k.key_upto
                diags = [at + diag for _, _, _, diag, at in places(d) if diag is not None]
                for j, a in enumerate(diags):
                    w = wt[n % buffers][:, a:a + P]
                    last = pool.tensor_tensor(w, w, mask[:], ALU.mult)
                    if j < len(diags) - 1:
                        k.step_p.after(pool, last)
                last.then_inc(masked, 1)


def head_finish(k, name, y, tiles, heads, centre, gate, func):
    nc = k.nc
    n = tiles * heads
    sq = work(k, 4160, tiles * D)
    opened = k.sem(f"{name}_open")
    mean, ss, v, r, tmp = (k.small[:, 208 + 32 * j:208 + 32 * j + n] for j in range(5))
    y3 = y.rearrange("p a (h d) -> p (a h) d", d=P)
    s3 = sq.rearrange("p (n d) -> p n d", d=P)
    with nc.Block(no_gpsimd_drain=True) as block:
        @block.scalar
        def _(act):
            act.activation(gate, gate, func).then_inc(opened, 1)

        @block.vector
        def _(dve):
            st = k.step_v.after
            if centre:
                st(dve, dve.tensor_reduce(mean, y3, AX.X, ALU.add))
                st(dve, dve.tensor_scalar(mean, mean, 1.0 / P, None, ALU.mult))
                st(dve, dve.tensor_tensor(y3, y3, mean.unsqueeze(2).to_broadcast([P, n, P]), ALU.subtract))
            st(dve, dve.tensor_tensor(s3, y3, y3, ALU.mult))
            st(dve, dve.tensor_reduce(ss, s3, AX.X, ALU.add))
            st(dve, dve.tensor_scalar(v, ss, 1.0 / P, EPS, ALU.mult, ALU.add))
            rsqrt(k, dve, v, r, tmp)
            st(dve, dve.tensor_tensor(y3, y3, r.unsqueeze(2).to_broadcast([P, n, P]), ALU.mult))
            dve.wait_ge(opened, 1)
            st(dve, dve.tensor_tensor(y, y, gate, ALU.mult))


def gated_out(k, name, y, tokens, col, stage, rows, layer, seqs):
    yt = work(k, 4160, 4096)[:, 0:len(tokens) * D].rearrange("p (c t) -> p c t", c=C)
    gates = work(k, rows, len(seqs) * D).rearrange("p (s d) -> p s d", s=len(seqs))
    turn(k, f"{name}_y", y, yt, col)
    row_gates(k, f"{name}_rows", layer, 2, seqs, gates)
    n0 = k.stage[stage]
    tiles = []
    for a in range(2):
        w = weights(k, n0 + a, 512)
        cs = slice(512 * a, 512 * a + 512)
        for j, x in enumerate(tokens):
            tiles.append(tile([(yt[:, c, j * P:(j + 1) * P], w[:, c, :]) for c in range(C)], 512, n0 + a,
                              dst=x[:, cs], gate=gates[:, j // TT, cs]))
    gemm(k, f"{name}_out", tiles, add_gated(k, work(k, 19520, 512)), n0 + 2 + SLOTS, "dve")


def experts(k, name, layer, sets, stage):
    nc = k.nc
    S, N = len(sets), CAPACITY
    NT = S * TT
    M = S * N
    PER = P // M
    GROUPS = EXPERTS // PER
    tiles = [x for _, xs in sets for x in xs]
    xn = work(k, 0, NT * D).rearrange("p (a d) -> p a d", a=NT)
    ht = work(k, 4096, NT * D).rearrange("p (c t) -> p c t", c=C)
    hot = work(k, 8192, NT * 512).rearrange("p (a e s) -> p a e s", a=NT, e=EXPERTS)
    xs = work(k, 10240, C * EXPERTS * M).rearrange("p (c e s n) -> p c e s n", c=C, e=EXPERTS, s=S)
    aff = work(k, 18432, NT * 16).rearrange("p (a e) -> p a e", a=NT)
    aff_t = work(k, 18496, S * T)[0:16, :]
    rank = work(k, 19008, 2 * NT * 16).rearrange("p (j a e) -> p j a e", j=2, a=NT)
    before = work(k, 19136, 2 * T).rearrange("p (a t) -> p a t", a=TT)
    scr = [work(k, 10240 + T * j, T) for j in range(8)]
    router = work(k, 19648, 128).rearrange("p (c e) -> p c e", c=C)
    order = (1, 0) if S == 2 else (0,)
    ga = scaled_gains(k, name, layer, k.col("norm_ffn")[:, C * layer:C * layer + C], 1)
    affine = [ga[s] for s, _ in sets]
    base = k.stage[stage]
    norm_transpose(k, f"{name}_norm", tiles, xn, ht, affine)

    got, full, exped, normed, turned, kept, spread, read, ready = (
        k.sem(f"{name}_{s}") for s in ("router", "logits", "exp", "affinity", "turned", "kept", "rows", "ranked", "hot"))
    mx, sm = k.small[:, 208:208 + NT], k.small[:, 216:216 + NT]
    with nc.Block(no_gpsimd_drain=True) as block:
        @block.sync
        def _(sp):
            sp.dma_start(router, k.dram["moe_router_2"][layer].rearrange("(c p) e -> p c e", p=P)).then_inc(got, 16)
            sp.wait_ge(got, 16)

        @block.tensor
        def _(pe):
            pe.wait_ge(got, 16)
            for t in range(NT):
                for c in range(C):
                    last = pe.matmul(k.ps[:, 0, 16 * t:16 * t + 16], ht[:, c, t * P:(t + 1) * P], router[:, c, :],
                                     start=(c == 0), stop=(c == C - 1))
            last.then_inc(full, 1)
            pe.wait_ge(normed, 1)
            for t in range(NT):
                last = pe.transpose(k.ps[0:16, 1, t * P:(t + 1) * P], aff[:, t, :], k.ident[:])
            last.then_inc(turned, 1)
            pe.wait_ge(kept, 1)
            for e in range(EXPERTS):
                if e >= 2:
                    pe.wait_ge(read, 2 * (e - 1) * NT)
                pe.matmul(k.ps[:, 2 + e % 2, 0:S * T], k.ident[0:16, e:e + 1].to_broadcast([16, P]), aff_t,
                          start=True, stop=True).then_inc(spread, 1)

        @block.scalar
        def _(act):
            act.wait_ge(exped, 1)
            act.activation(aff, aff, ACT.Exp).then_inc(exped, 1)
            act.wait_ge(turned, 1)
            act.activation(aff_t, k.ps[0:16, 1, 0:S * T], ACT.Copy).then_inc(kept, 1)

        @block.vector
        def _(dve):
            st = k.step_v.after
            st(dve, dve.memset(before[:, 1, 0:P], 1.0))
            st(dve, dve.memset(before[:, 0, P:T], 0.0))
            st(dve, dve.tensor_copy(before[:, 0, 0:P], k.key_after[:]))
            st(dve, dve.tensor_copy(before[:, 1, P:T], k.key_after[:]))
            dve.wait_ge(full, 1)
            logits = k.ps[:, 0, 0:16 * NT].rearrange("p (a e) -> p a e", a=NT)
            st(dve, dve.tensor_reduce(mx, logits, AX.X, ALU.max))
            dve.tensor_tensor(aff, logits, mx.unsqueeze(2).to_broadcast([P, NT, 16]), ALU.subtract).then_inc(exped, 1)
            dve.wait_ge(exped, 2)
            st(dve, dve.tensor_reduce(sm, aff, AX.X, ALU.add))
            st(dve, dve.reciprocal(sm, sm))
            dve.tensor_tensor(aff, aff, sm.unsqueeze(2).to_broadcast([P, NT, 16]), ALU.mult).then_inc(normed, 1)
            for e in range(EXPERTS):
                dve.wait_ge(spread, e + 1)
                for t in range(NT):
                    n = e * NT + t
                    row = k.ps[:, 2 + e % 2, T * (t // TT):T * (t // TT) + T]
                    a = aff[:, t, e:e + 1]
                    if n >= 4:
                        dve.wait_ge(read, 2 * (n - 3))
                    dve.tensor_scalar(scr[2 * (n % 4)], row, a, 0.0, ALU.is_gt, ALU.add,
                                      accum_out=rank[:, 0, t, e:e + 1]).then_inc(read, 1)
                    dve.scalar_tensor_tensor(out=scr[2 * (n % 4) + 1], in0=row, scalar=a, in1=before[:, t % TT, :],
                                             op0=ALU.is_equal, op1=ALU.mult, accum_out=rank[:, 1, t, e:e + 1])\
                       .then_inc(read, 1)
            dve.wait_ge(read, 2 * EXPERTS * NT)
            st(dve, dve.tensor_tensor(rank[:, 0], rank[:, 0], rank[:, 1], ALU.add))
            for t in range(NT):
                st(dve, dve.tensor_tensor(hot[:, t], rank[:, 0, t, :].unsqueeze(2).to_broadcast([P, 16, N]),
                                          k.iota[:, 0:N].unsqueeze(1).to_broadcast([P, 16, N]), ALU.is_equal))

    jobs = [tile([(xn[:, TT * s + t, c * P:(c + 1) * P], hot[:, TT * s + t].rearrange("p e n -> p (e n)"))
                  for t in range(TT)], 512, s=s, c=c) for c in range(C) for s in range(S)]

    def place(eng, t, ps):
        scale, shift = affine[t.s]
        return eng.activation(xs[:, t.c, :, t.s, :], ps.rearrange("p (e n) -> p e n", e=EXPERTS), ACT.Identity,
                              scale=scale[:, t.c:t.c + 1], bias=shift[:, t.c:t.c + 1])
    gemm(k, f"{name}_gather", jobs, place, 0)

    back = work(k, 4096, NT * EXPERTS * M).rearrange("p (a e s n) -> p a e s n", a=NT, e=EXPERTS, s=S)
    back_t = work(k, 0, GROUPS * S * T).rearrange("p (g t) -> p g t", g=GROUPS)
    filled = k.sem(f"{name}_filled")
    with nc.Block(no_gpsimd_drain=True) as block:
        @block.vector
        def _(dve):
            st = k.step_v.after
            st(dve, dve.memset(back, 0.0))
            for t in range(NT):
                st(dve, dve.tensor_tensor(back[:, t, :, t // TT, :], hot[:, t],
                                          aff[:, t, :].unsqueeze(2).to_broadcast([P, 16, N]), ALU.mult))
    turn(k, f"{name}_back", back.rearrange("p a e s n -> p a (e s n)"), back_t, None)

    Q = P // M
    W = D // Q
    silu_b, hid = work(k, 8192, W), work(k, 8192 + 512, W)
    ys = work(k, 8192 + 1024, D)
    wb = work(k, 18432, S * T)
    xe = work(k, 18944, C * M).rearrange("p (c m) -> p c m", c=C)
    hid_t = work(k, 19456, P * W // P).rearrange("p (j q m) -> p j q m", j=W // P, q=Q)
    acc = work(k, 4096, NT * D).rearrange("p (a d) -> p a d", a=NT)
    g_full, u_full, silu_d, hid_d, t_full, t_kept, y_full, y_kept, c_full, c_added, wb_kept, xe_kept = (
        k.sem(f"{name}_x_{s}") for s in ("gate", "up", "silu", "hidden", "turned", "hidden_t", "y", "y_kept", "sum",
                                         "added", "back", "tokens"))
    half_used = k.sem(f"{name}_x_half")
    srcs = [k.dram[n][layer].rearrange("e (c p) n -> p e c n", p=P)
            for n in ("moe_w_gate_2", "moe_w_up_2", "moe_w_down_2")]
    last_load = base + 6 * EXPERTS
    w4 = [slot(k, base + s).rearrange("p (c n) -> p c n", c=4) for s in range(6)]

    with nc.Block(no_gpsimd_drain=True) as block:
        @block.sync
        def _(sp):
            with sp.Fori(1, EXPERTS) as e:
                for s in range(6):
                    if s % 2 == 0:
                        sp.wait_ge(half_used, e * 3 - 3 + s // 2 + 1)
                    else:
                        sp.wait_ge((g_full, u_full, y_full)[s // 2], e)
                    sp.dma_start(w4[s].unsqueeze(1), srcs[s // 2][:, bass.ds(e, 1), 4 * (s % 2):4 * (s % 2) + 4, :])\
                      .then_inc(k.slot_loaded[(base + s) % SLOTS], 16)
            for n in range(last_load, min(last_load + SLOTS, len(k.loads))):
                s = n - last_load
                if s % 2 == 0:
                    sp.wait_ge(half_used, 3 * EXPERTS - 3 + s // 2 + 1)
                else:
                    sp.wait_ge((g_full, u_full, y_full)[s // 2], EXPERTS)
                k.used.add(n - SLOTS)
                k.issued = n
                issue(k, sp, n + 1)

        @block.tensor
        def _(pe):
            def product(e, s0, bank, lhsT, done):
                for half in range(2):
                    s = s0 + half
                    pe.wait_ge(k.slot_loaded[(base + s) % SLOTS], e * 16 + 16 * ((base + s) // SLOTS + 1))
                    for c in range(4):
                        kc = 4 * half + c
                        for q in range(Q):
                            last = pe.matmul(k.ps[q * M:q * M + M, bank, 0:W], lhsT(kc),
                                             w4[s][:, c, q * W:q * W + W], start=(kc == 0), stop=(kc == C - 1),
                                             skip_group_check=True)
                    last.then_inc(done if half else half_used, 1)

            def expert(e, steady):
                pe.wait_ge(xe_kept, e + 1)
                product(e, 0, 0, lambda kc: xe[:, kc, :], g_full)
                product(e, 2, 1, lambda kc: xe[:, kc, :], u_full)
                pe.wait_ge(hid_d, e + 1)
                for j in range(W // P):
                    last = pe.transpose(k.ps[:, 2, j * P:(j + 1) * P], hid[:, j * P:(j + 1) * P], k.ident[:])
                last.then_inc(t_full, 1)
                pe.wait_ge(t_kept, e + 1)
                if steady:
                    pe.wait_ge(y_kept, e * Q)
                product(e, 4, 3, lambda kc: hid_t[:, kc % (W // P), kc // (W // P), :], y_full)

            def combine(group, steady):
                pe.wait_ge(y_kept, group * (PER * Q) + PER * Q)
                pe.wait_ge(wb_kept, group + 1)
                for j in range(2 * NT):
                    t, nh = j // 2, j % 2
                    if steady or j >= 2:
                        pe.wait_ge(c_added, group * (2 * NT) + j - 1)
                    pe.matmul(k.ps[:, 4 + j % 2, :], wb[:, t * P:(t + 1) * P], ys[:, 512 * nh:512 * nh + 512],
                              start=True, stop=True).then_inc(c_full, 1)

            def group_of(group, steady):
                for b in range(PER):
                    expert(group * PER + b, steady or b > 0)
                combine(group, steady)

            group_of(0, False)
            with pe.Fori(1, GROUPS) as g:
                group_of(g, True)

        @block.scalar
        def _(act):
            def group_of(group, steady):
                if steady:
                    act.wait_ge(c_full, group * (2 * NT))
                act.activation(wb.unsqueeze(1), back_t[:, bass.ds(group, 1), :], ACT.Copy).then_inc(wb_kept, 1)
                for b in range(PER):
                    e = group * PER + b
                    act.wait_ge(g_full, e + 1)
                    if steady or b:
                        act.wait_ge(hid_d, e)
                    act.activation(silu_b, k.ps[:, 0, 0:W], ACT.Silu).then_inc(silu_d, 1)
                    act.wait_ge(t_full, e + 1)
                    act.activation(hid_t.rearrange("p j q m -> p (j q m)"), k.ps[:, 2, 0:W], ACT.Copy)\
                       .then_inc(t_kept, 1)
                    act.wait_ge(y_full, e + 1)
                    for q in range(Q):
                        act.activation(ys[M * b:M * b + M, q * W:q * W + W], k.ps[M * q:M * q + M, 3, 0:W],
                                       ACT.Copy).then_inc(y_kept, 1)

            group_of(0, False)
            with act.Fori(1, GROUPS) as g:
                group_of(g, True)

        @block.vector
        def _(dve):
            def group_of(group, steady):
                for b in range(PER):
                    e = group * PER + b
                    if steady or b:
                        dve.wait_ge(u_full, e)
                    dve.tensor_copy(xe.unsqueeze(2),
                                    xs.rearrange("p c e s n -> p c e (s n)")[:, :, bass.ds(e, 1), :])\
                       .then_inc(xe_kept, 1)
                    dve.wait_ge(silu_d, e + 1)
                    dve.wait_ge(u_full, e + 1)
                    if steady or b:
                        dve.wait_ge(t_full, e)
                    dve.tensor_tensor(hid, silu_b, k.ps[:, 1, 0:W], ALU.mult).then_inc(hid_d, 1)
                for j in range(2 * NT):
                    dve.wait_ge(c_full, group * (2 * NT) + j + 1)
                    out = acc[:, j // 2, 512 * (j % 2):512 * (j % 2) + 512]
                    if steady:
                        dve.tensor_tensor(out, out, k.ps[:, 4 + j % 2, :], ALU.add).then_inc(c_added, 1)
                    else:
                        dve.tensor_copy(out, k.ps[:, 4 + j % 2, :]).then_inc(c_added, 1)

            group_of(0, False)
            with dve.Fori(1, GROUPS) as g:
                group_of(g, True)
            dve.wait_ge(c_added, 2 * NT * GROUPS)
    k.used |= set(range(base, last_load))
    k.issued = max(k.issued, last_load)
    gates = work(k, 10240, S * D).rearrange("p (s d) -> p s d", s=S)
    row_gates(k, f"{name}_rows", layer, 5, [s for s, _ in sets], gates)
    with nc.Block(no_gpsimd_drain=True) as block:
        @block.vector
        def _(dve):
            st = k.step_v.after
            for t in range(NT):
                st(dve, dve.tensor_tensor(acc[:, t, :], acc[:, t, :], gates[:, t // TT, :], ALU.mult))
                st(dve, dve.tensor_tensor(tiles[t], tiles[t], acc[:, t, :], ALU.add))


def retention(k):
    nc = k.nc
    xn = work(k, 0, 4096).rearrange("p (a d) -> p a d", a=4)
    ht = work(k, 4160, 4096).rearrange("p (c t) -> p c t", c=C)
    q = work(k, 8256, 2048).rearrange("p (a d) -> p a d", a=TT)
    kk = work(k, 10304, 2048).rearrange("p (a d) -> p a d", a=TT)
    gate = work(k, 12352, 2048).rearrange("p (a d) -> p a d", a=TT)
    kt_ = work(k, 14400, 4096).rearrange("p (h t) -> p h t", h=8)
    v = work(k, 0, 4096).rearrange("p (a d) -> p a d", a=4)
    n0 = k.stage["b_in"]
    lat, con = scaled_gains(k, "b", 1, k.col("norm_mix")[:, C:2 * C], 0)
    norm_transpose(k, "b_norm", [k.cx[:, 0, :], k.cx[:, 1, :], k.x[:, 0, :], k.x[:, 1, :]], xn, ht, [con, lat])
    tiles = []
    for a in range(8):
        w = weights(k, n0 + a, 512)
        cs = slice(512 * (a % 2), 512 * (a % 2) + 512)
        if a in (2, 3):
            for b in range(4):
                tiles.append(tile([(w[:, c, b * P:(b + 1) * P], ht[:, c, 0:T]) for c in range(C)], T, n0 + a,
                                  dst=kt_[:, 4 * (a - 2) + b, 0:T]))
        for t in range(0 if a in (4, 5) else 2, 4):
            dst = v[:, t, cs] if a in (4, 5) else (q, kk, None, gate)[a // 2][:, t - 2, cs]
            tiles.append(tile([(ht[:, c, t * P:(t + 1) * P], w[:, c, :]) for c in range(C)], 512, n0 + a, dst=dst))
    gemm(k, "b_in", tiles, lambda eng, t, ps: eng.activation(t.dst, ps, ACT.Copy), n0 + 8 + SLOTS)

    rot = work(k, 4160, 256).rearrange("p (a j n) -> p a j n", a=2, j=2)
    t1 = work(k, 4416, 512)
    t2 = work(k, 4928, 512)
    got = k.sem("rope_tables")
    with nc.Block(no_gpsimd_drain=True) as block:
        @block.sync
        def _(sp):
            sp.dma_start(rot, k.dram["rope"].rearrange("s (a p) n -> p s a n", p=P)).then_inc(got, 16)
            sp.wait_ge(got, 16)

        @block.vector
        def _(dve):
            st = k.step_v.after
            dve.wait_ge(got, 16)
            for src in (q, kk):
                for t in range(TT):
                    a = src[:, t, :].rearrange("p (h f s n) -> p h f s n", h=8, f=2, s=2)
                    x1, x2 = a[:, :, :, 0, :], a[:, :, :, 1, :]
                    cos, sin = (rot[:, s, t, :].rearrange("p (f n) -> p f n", f=2).unsqueeze(1)
                                .to_broadcast([P, 8, 2, 32]) for s in range(2))
                    u1, u2 = (b.rearrange("p (h f n) -> p h f n", h=8, f=2) for b in (t1, t2))
                    st(dve, dve.tensor_tensor(u1, x1, sin, ALU.mult))
                    st(dve, dve.tensor_tensor(u2, x2, sin, ALU.mult))
                    st(dve, dve.tensor_tensor(x1, x1, cos, ALU.mult))
                    st(dve, dve.tensor_tensor(x1, x1, u2, ALU.subtract))
                    st(dve, dve.tensor_tensor(x2, x2, cos, ALU.mult))
                    st(dve, dve.tensor_tensor(x2, x2, u1, ALU.add))
    turn(k, "b_k", kk, kt_[:, :, T:2 * T], None)
    qt = work(k, 18496, 2048).rearrange("p (h t) -> p h t", h=8)
    turn(k, "b_q", q, qt, None)

    dist = [work(k, 4160 + 1024 * j, 1024) for j in range(2)]
    masks = [work(k, 6208 + 512 * j, 512) for j in range(2)]
    ex = [work(k, 8256 + 1024 * j, 1024) for j in range(2)]
    wt = [work(k, 10304 + 1024 * b, 1024) for b in range(2)]
    idx = [work(k, 10304 + 1024 * b, 1024).bitcast(I32) for b in range(2)]
    logg = k.small[:, 64:80]
    exped, e_used, s_full, w_ready, o_full, o_done, made, ready = (
        k.sem(f"ret_{s}") for s in ("exp", "exp_used", "scores", "weights", "out", "stored", "index", "ready"))
    y = k.big[:, R_CTX:R_CTX + 2048].rearrange("p (a d) -> p a d", a=TT)
    with nc.Block(no_gpsimd_drain=True) as block:
        @block.gpsimd
        def _(pool):
            pool.iota(idx[0], pattern=[[-P, 4], [1, T]], base=T, channel_multiplier=-1).then_inc(made, 1)
            pool.iota(idx[1][:, 0:512], pattern=[[P, 2], [-1, T]], base=T, channel_multiplier=1).then_inc(made, 1)
            pool.iota(idx[1][:, 512:1024], pattern=[[P, 2], [-1, T]], base=0, channel_multiplier=1).then_inc(made, 1)

        @block.scalar
        def _(act):
            st = k.step_a.after
            def store(h):
                act.wait_ge(o_full, h + 1)
                act.activation(y[:, :, h * P:(h + 1) * P], k.ps[:, 4 + h % 2, 0:T].rearrange("p (a d) -> p a d", a=2),
                               ACT.Copy).then_inc(o_done, 1)

            a = k.small[:, 80:96]
            st(act, act.activation(a, k.col("decay"), ACT.Abs))
            st(act, act.activation(a, a, ACT.Exp, scale=-1.0))
            st(act, act.activation(a, a, ACT.Ln, bias=1.0))
            act.activation(a, a, ACT.Copy).then_inc(exped, 1)
            act.wait_ge(ready, 1)
            for h in range(B_HEADS + 1):
                if h < B_HEADS:
                    if h:
                        act.wait_ge(e_used, h)
                    for d in range(2):
                        act.activation(ex[d], dist[d], ACT.Exp, scale=logg[:, 8 * d + h:8 * d + h + 1])\
                           .then_inc(exped, 1)
                if h:
                    store(h - 1)

        @block.tensor
        def _(pe):
            def score(h):
                if h >= 2:
                    pe.wait_ge(w_ready, h - 1)
                for kt in range(4):
                    last = pe.matmul(k.ps[:, 2 * (h % 2) + kt // 2, T * (kt % 2):T * (kt % 2) + T],
                                     kt_[:, h, kt * P:(kt + 1) * P], qt[:, h, :], start=True, stop=True)
                last.then_inc(s_full, 1)
            score(0)
            for h in range(B_HEADS):
                if h + 1 < B_HEADS:
                    score(h + 1)
                pe.wait_ge(w_ready, h + 1)
                if h >= 2:
                    pe.wait_ge(o_done, h - 1)
                for t in range(TT):
                    for kt in range(4):
                        last = pe.matmul(k.ps[:, 4 + h % 2, t * P:(t + 1) * P],
                                         wt[h % 2][:, T * kt + t * P:T * kt + (t + 1) * P],
                                         v[:, kt, h * P:(h + 1) * P], start=(kt == 0), stop=(kt == 3))
                last.then_inc(o_full, 1)

        @block.vector
        def _(dve):
            st = k.step_v.after
            dve.wait_ge(made, 3)
            for j in range(2):
                st(dve, dve.tensor_copy(dist[j], idx[j]))
                st(dve, dve.tensor_scalar(masks[j], dist[j][:, 512:1024], 0.0, None, ALU.is_ge))
                st(dve, dve.tensor_scalar(dist[j], dist[j], 0.0, None, ALU.max))
            dve.wait_ge(exped, 1)
            st(dve, dve.tensor_scalar(logg, k.col("decay"), 0.0, None, ALU.min))
            dve.tensor_tensor(logg, logg, k.small[:, 80:96], ALU.subtract).then_inc(ready, 1)
            for h in range(B_HEADS):
                dve.wait_ge(exped, 2 * h + 3)
                for j in range(2):
                    st(dve, dve.tensor_tensor(ex[j][:, 512:1024], ex[j][:, 512:1024], masks[j], ALU.mult))
                st(dve, dve.tensor_tensor(ex[0], ex[0], ex[1], ALU.add))
                dve.wait_ge(s_full, h + 1)
                if h >= 2:
                    dve.wait_ge(o_full, h - 1)
                s = k.ps[:, 2 * (h % 2):2 * (h % 2) + 2, :].rearrange("p b n -> p (b n)")
                dve.scalar_tensor_tensor(out=wt[h % 2], in0=s, scalar=B_DIM ** -0.5, in1=ex[0], op0=ALU.mult,
                                         op1=ALU.mult).then_inc(w_ready, 1)
                dve.wait_ge(w_ready, h + 1)
                dve.tensor_copy(k.small[:, 96:97], k.ones[:, 0:1]).then_inc(e_used, 1)
    head_finish(k, "b_fin", y, 2, B_HEADS, True, gate, ACT.Silu)
    gated_out(k, "b", y, [k.x[:, 0, :], k.x[:, 1, :]], k.col("b_norm"), "b_out", 8256, 1, [0])


def final_norm(k):
    gain = work(k, 0, 1024)
    got, done, stored = k.sem("final_gain"), k.sem("final_done"), k.sem("final_stored")
    ss, v, r, tmp = (k.small[:, 4 * j:4 * j + TT] for j in range(4))
    scr = work(k, 1024, 2048).rearrange("p (a d) -> p a d", a=TT)
    with k.nc.Block(no_gpsimd_drain=True) as block:
        @block.sync
        def _(sp):
            sp.dma_start(gain, k.dram["final_gain"].to_broadcast([P, D])).then_inc(got, 16)
            sp.wait_ge(done, TT)
            sp.dma_start(k.dram["out"][0].rearrange("(a p) d -> p a d", p=P), scr).then_inc(stored, 16)
            sp.wait_ge(stored, 16)

        @block.vector
        def _(dve):
            st = k.step_v.after
            for t in range(TT):
                st(dve, dve.scalar_tensor_tensor(out=scr[:, t, :], in0=k.x[:, t, :], scalar=1.0, in1=k.x[:, t, :],
                                                 op0=ALU.mult, op1=ALU.mult, accum_out=ss[:, t:t + 1]))
            st(dve, dve.tensor_scalar(v, ss, 1.0 / D, EPS, ALU.mult, ALU.add))
            rsqrt(k, dve, v, r, tmp)
            dve.wait_ge(got, 16)
            for t in range(TT):
                dve.scalar_tensor_tensor(out=scr[:, t, :], in0=k.x[:, t, :], scalar=r[:, t:t + 1], in1=gain,
                                         op0=ALU.mult, op1=ALU.mult).then_inc(done, 1)


def two_blocks_kernel(nc, dram):
    with ExitStack() as ctx:
        k = setup(nc, ctx, dram)
        plan_loads(k)

        def mlstm():
            mlstm_inputs(k)
            mlstm_heads(k)

        def mlstm_out():
            head_finish(k, "a_fin", k.y, 4, A_HEADS, False, k.o, ACT.Sigmoid)
            gated_out(k, "a", k.y, [k.cx[:, 0, :], k.cx[:, 1, :], k.x[:, 0, :], k.x[:, 1, :]], k.col("a_norm"),
                      "a_out", 8256, 0, [1, 0])

        cx, x = [k.cx[:, t, :] for t in range(TT)], [k.x[:, t, :] for t in range(TT)]
        stages = [("constants", lambda: constants(k)), 
                  ("proj", lambda: first_projections(k)), ("sb", lambda: stick_breaking(k)),
                  ("heads", lambda: head_norms(k)), ("softmax", lambda: softmax_attentions(k)),
                  ("merge", lambda: gated_merge(k)), ("select", lambda: peer_select(k)),
                  ("gates", lambda: peer_gates(k)), ("peer", lambda: peer_experts(k)),
                  ("mlstm", mlstm), ("mlstm_out", mlstm_out),
                  ("moe0", lambda: experts(k, "m0", 0, [(1, cx), (0, x)], "moe0")),
                  ("ret", lambda: retention(k)),
                  ("moe1", lambda: experts(k, "m1", 1, [(0, x)], "moe1")),
                  ("final", lambda: final_norm(k))]
        for _, stage in stages:
            stage()


def layout(a):
    def col(v):
        return v.reshape(-1, P).T

    parts = dict(
        g_mix=col(a["g_mix"]), g_mem=col(a["g_mem"]), g_ffn=col(a["g_ffn"]), norm_mix=col(a["norm_mix_g_2"]),
        norm_ffn=col(a["norm_ffn_g_2"]), ada_b=col(a["ada_b_2"]),
        cvec=np.stack([col(a["c_2"]), col(a["c_ctx_2"])], axis=2).reshape(P, 2 * C),
        gq_dil=np.tile(a["g_q_dil"].reshape(-1), 2)[:, None], gk_dil=np.tile(a["g_k_dil"].reshape(-1), 2)[:, None],
        gq_mem=a["g_q_mem"].reshape(P, 1), gk_mem=a["g_k_mem"].reshape(P, 1),
        conv_w=a["mlstm_conv_w_2"].reshape(CONV_W, C, P).transpose(2, 1, 0).reshape(P, C * CONV_W),
        conv_b=col(a["mlstm_conv_b_2"]), ig_b=np.tile(a["mlstm_igate_b_2"].reshape(16, 1), (8, 1)),
        fg_b=np.tile(a["mlstm_fgate_b_2"].reshape(16, 1), (8, 1)), a_norm=col(a["mlstm_head_norm_g_2"]),
        b_norm=col(a["ret_group_norm_g_2"]), decay=np.tile(a["ret_decay_logit_2"].reshape(1, 16), (P, 1)))
    out = {n: a[n] for n in ("x", "mem", "ctx_2", "w_in", "w_mem_kv", "w_o_sb", "w_o_dil", "w_o_mem", "w_gate",
                             "w_out", "w_peer_q", "peer_v", "ada_w_2", "mlstm_w_in_2", "mlstm_w_out_2", "ret_w_in_2",
                             "ret_w_out_2", "moe_router_2", "moe_w_gate_2", "moe_w_up_2", "moe_w_down_2", "b_gate")}
    out["columns"] = np.concatenate([parts[n] for n in COLUMNS], axis=1)
    out["final_gain"] = a["final_norm_g_2"].reshape(1, D)
    out["peer_u_t"] = a["peer_u"].reshape(PEER_KEYS, PEER_KEYS, C, P).transpose(1, 3, 2, 0)
    out["subkeys_t"] = a["peer_subkeys"].reshape(16, PEER_KEYS, P).transpose(2, 0, 1)
    inv = np.float32(10000.0) ** (-np.arange(32, dtype=np.float32) / np.float32(32))
    place = np.arange(T)
    angles = np.concatenate([(place // 64).astype(np.float32)[:, None] * inv,
                             (place % 64).astype(np.float32)[:, None] * inv], axis=1)
    out["rope"] = np.stack([np.cos(angles), np.sin(angles)])
    return {n: np.ascontiguousarray(v) for n, v in out.items()}


def kernel(**inputs):
    import concourse.bacc as _bacc
    from concourse.bass_utils import run_bass_kernel_spmd as _run

    arrays = {f"in_{n}_dram": v for n, v in layout({n: np.asarray(v) for n, v in inputs.items()}).items()}
    nc = _bacc.Bacc("TRN2", target_bir_lowering=False, num_devices=1)
    dram = {n[3:-5]: nc.dram_tensor(n, v.shape, mybir.dt.from_np(v.dtype), kind="ExternalInput").ap()
            for n, v in arrays.items()}
    dram["out"] = nc.dram_tensor("out_0_dram", (1, T, D), F32, kind="ExternalOutput").ap()
    two_blocks_kernel(nc, dram)
    r = _run(nc, [arrays], core_ids=[0])
    return r.results[0]["out_0_dram"]
```

```python
from contextlib import ExitStack

import numpy as np

import concourse.bass as bass
from concourse import mybir

F32 = mybir.dt.float32
I32 = mybir.dt.int32
U32 = mybir.dt.uint32
ALU = mybir.AluOpType
ACT = mybir.ActivationFunctionType
AX = mybir.AxisListType

P = 128
D = 1024
C = D // P
T = 256
TT = T // P
EPS = 1e-6
SLOTS = 6
SLOT = 4096
BANKS = 8
NEG = -1e30

SB_HEADS, SB_DIM = 8, 64
DIL_GROUPS, DIL_SLOTS, DIL_DIM = 3, 4, 64
DILATIONS = (1, 4, 16)
DIL_HEADS = DIL_GROUPS * DIL_SLOTS
DIL_REACH = 128
MEM_HEADS, MEM_DIM = 4, 128
PEER_HEADS, PEER_KEYS, PEER_TOPK = 8, 128, 16
EXPERTS = 16
CAPACITY = 2 * T // EXPERTS
A_HEADS, A_DK, A_DV = 8, 64, 128
CONV_W = 5
B_HEADS, B_DIM = 8, 128

R_X, R_CTX, R_RING = 0, 2048, 4096
R_WORK = R_RING + SLOTS * SLOT
BIG = R_WORK + 20992


def column_plan():
    widths = dict(g_mix=C, g_mem=C, g_ffn=C, norm_mix=2 * C, norm_ffn=2 * C, ada_b=2 * 48, cvec=2 * C,
                  gq_dil=1, gk_dil=1, gq_mem=1, gk_mem=1, conv_w=C * CONV_W, conv_b=C, ig_b=1, fg_b=1,
                  a_norm=C, b_norm=C, decay=16)
    plan, at = {}, 0
    for name, width in widths.items():
        plan[name] = (at, at + width)
        at += width
    return plan, at


COLUMNS, N_COLUMNS = column_plan()


class Steps:

    def __init__(self, sem):
        self.sem, self.n = sem, 0

    def after(self, eng, ins):
        ins.then_inc(self.sem, 1)
        self.n += 1
        eng.wait_ge(self.sem, self.n)

    def both(self, eng, one, other):
        one.then_inc(self.sem, 1)
        other.then_inc(self.sem, 1)
        self.n += 2
        eng.wait_ge(self.sem, self.n)


class Kernel:

    def __init__(self, nc, ctx, dram):
        self.nc, self.ctx, self.dram = nc, ctx, dram
        self.release = {}
        self.used = set()
        self.numbers = {}
        self.tables = []
        self.loads, self.issued, self.stage, self.peer_done = [], 0, {}, False

    def sem(self, name):
        return self.ctx.enter_context(self.nc.semaphore(name))

    def col(self, name):
        return self.cols[:, COLUMNS[name][0]:COLUMNS[name][1]]


class Tile:

    def __init__(self, pairs, n, load, m, row, dst, gate, bias, s, c, needs):
        self.pairs, self.n, self.load, self.m, self.row = pairs, n, load, m, row
        self.dst, self.gate, self.bias, self.s, self.c = dst, gate, bias, s, c
        self.needs = needs


class Shared:

    def __init__(self, sem):
        self.sem, self.base = sem, 0

    def at(self, n):
        return self.sem, self.base + n


def setup(nc, ctx, dram):
    k = Kernel(nc, ctx, dram)

    def sb(name, shape, dt=F32):
        return ctx.enter_context(nc.sbuf_tensor(name, shape, dt))

    k.big = sb("big", [P, BIG])
    k.ps = ctx.enter_context(nc.psum_tensor("ps", [P, BANKS, 512], F32))
    k.ident = sb("ident", [P, P])
    k.ones = sb("ones", [P, P])
    k.key_before = sb("key_before", [P, P])
    k.key_upto = sb("key_upto", [P, P])
    k.key_after = sb("key_after", [P, P])
    k.key_from = sb("key_from", [P, P])
    k.iota = sb("iota", [P, P])
    k.cols = sb("cols", [P, N_COLUMNS])
    k.mod = sb("mod", [P, 2, 48, 2])
    k.small = sb("small", [P, 512])
    k.step_v = Steps(k.sem("vector_steps"))
    k.step_a = Steps(k.sem("scalar_steps"))
    k.step_p = Steps(k.sem("pool_steps"))
    k.slot_loaded = [k.sem(f"slot{s}_loaded") for s in range(SLOTS)]
    k.x = k.big[:, R_X:R_X + 2048].rearrange("p (a d) -> p a d", a=TT)
    k.cx = k.big[:, R_CTX:R_CTX + 2048].rearrange("p (a d) -> p a d", a=TT)

    k.shared = {n: Shared(k.sem(n)) for n in ("tile_full", "tile_free", "rows_normed", "chunk_turned", "chunk_stored",
                                             "diag_made", "row_full", "row_kept")}
    return k


def work(k, at, n):
    assert at + n <= BIG - R_WORK, (at, n)
    return k.big[:, R_WORK + at:R_WORK + at + n]


def slot(k, n):
    s = R_RING + (n % SLOTS) * SLOT
    return k.big[:, s:s + SLOT]


def plan_loads(k):
    d = k.dram

    def add(name, width, view):
        k.stage.setdefault(name, len(k.loads))
        k.numbers.setdefault(name, []).append(len(k.loads))
        k.loads.append((width, view))

    def tiles(name, w, n0, n1, step=512):
        v = w.rearrange("(c p) n -> p c n", p=P)
        for a in range(n0, n1, step):
            b = min(a + step, n1)
            add(name, v.shape[1] * (b - a), v[:, :, a:b])

    def experts(name, layer):
        k.stage.setdefault(name, len(k.loads))
        for s in range(6):
            w = d[("moe_w_gate_2", "moe_w_up_2", "moe_w_down_2")[s // 2]][layer]
            k.loads.append((SLOT, w[0].rearrange("(c p) n -> p c n", p=P)[:, 4 * (s % 2):4 * (s % 2) + 4, :]))
        for s in range(6 * (EXPERTS - 1)):
            k.loads.append(None)

    tiles("mem_kv", d["w_mem_kv"][0], 0, D)
    tiles("proj", d["w_in"][0], 0, 4352)
    tiles("o_sb", d["w_o_sb"][0], 0, D, D)
    tiles("o_dil", d["w_o_dil"][0], 0, D, D)
    tiles("o_mem", d["w_o_mem"][0], 0, D, D)
    for half in range(2):
        for br in range(3):
            tiles("gate", d["w_gate"][0], br * D + half * 512, br * D + half * 512 + 512)
    tiles("mix_out", d["w_out"][0], 0, D)
    ada = [(layer, a) for layer in range(2) for a in range(0, 6 * D, 512)]
    behind = (2, 5, 9, 13)
    for q in range(4):
        for layer, a in ada[behind[q - 1] if q else 0:behind[q]]:
            tiles("ada", d["ada_w_2"][layer], a, a + 512)
        tiles("peer_q", d["w_peer_q"][0], 512 * q, 512 * q + 512)
    for layer, a in ada[behind[-1]:]:
        tiles("ada", d["ada_w_2"][layer], a, a + 512)
    tiles("a_gates", d["mlstm_w_in_2"][0], 3072, 3104)
    tiles("a_in", d["mlstm_w_in_2"][0], 0, 3072)
    tiles("a_out", d["mlstm_w_out_2"][0], 0, D)
    experts("moe0", 0)
    tiles("b_in", d["ret_w_in_2"][0], 0, 4096)
    tiles("b_out", d["ret_w_out_2"][0], 0, D)
    experts("moe1", 1)


def issue(k, eng, upto):
    upto = min(upto, len(k.loads) if k.peer_done else k.stage["a_gates"])
    for n in range(k.issued, upto):
        width, src = k.loads[n]
        m = n - SLOTS
        if m in k.release:
            eng.wait_ge(*k.release[m])
        else:
            assert m < 0 or m in k.used, (n, m)
        dst = slot(k, n)[:, 0:width]
        if len(src.shape) == 3:
            dst = dst.rearrange("p (c n) -> p c n", c=src.shape[1])
        eng.dma_start(dst, src).then_inc(k.slot_loaded[n % SLOTS], 16)
    k.issued = max(k.issued, upto)


def retire(k):
    k.used |= set(k.release)
    k.release.clear()


def arrived(k, eng, n):
    eng.wait_ge(k.slot_loaded[n % SLOTS], 16 * (n // SLOTS + 1))


def rsqrt(k, eng, v, r, tmp):
    st = k.step_v.after
    st(eng, eng.tensor_scalar(tmp.bitcast(I32), v.bitcast(I32), 1, None, ALU.arith_shift_right))
    st(eng, eng.tensor_scalar(r.bitcast(I32), tmp.bitcast(I32), -1.0, 1597463007.0, ALU.mult, ALU.add))
    for _ in range(4):
        st(eng, eng.tensor_tensor(tmp, r, r, ALU.mult))
        st(eng, eng.tensor_tensor(tmp, tmp, v, ALU.mult))
        st(eng, eng.tensor_scalar(tmp, tmp, -0.5, 1.5, ALU.mult, ALU.add))
        st(eng, eng.tensor_tensor(r, r, tmp, ALU.mult))


def constants(k):
    nc, d = k.nc, k.dram
    loaded = k.sem("inputs_loaded")
    made = k.sem("constants_made")
    mem = work(k, 0, 2048).rearrange("p (a d) -> p a d", a=TT)
    idx = work(k, 2048, P).bitcast(I32)
    with nc.Block(no_gpsimd_drain=True) as block:
        @block.sync
        def _(sp):
            for dst, name in ((k.x, "x"), (mem, "mem"), (k.cx, "ctx_2")):
                sp.dma_start(dst, d[name][0].rearrange("(a p) d -> p a d", p=P)).then_inc(loaded, 16)
            sp.dma_start(k.cols[:], d["columns"]).then_inc(loaded, 16)
            issue(k, sp, SLOTS)
            sp.wait_ge(loaded, 64)

        @block.gpsimd
        def _(pool):
            st = k.step_p.after
            st(pool, pool.memset(k.ones[:], 1.0))
            st(pool, pool.memset(k.ident[:], 0.0))
            pool.affine_select(out=k.ident[:], in_=k.ident[:], compare_op=ALU.not_equal, fill=1.0, base=0,
                               pattern=[[-1, P]], channel_multiplier=1).then_inc(made, 1)
            for dst, base, sign in ((k.key_before, -1, 1), (k.key_upto, 0, 1),
                                    (k.key_after, -1, -1), (k.key_from, 0, -1)):
                pool.affine_select(out=dst[:], in_=k.ones[:], compare_op=ALU.is_ge, fill=0.0, base=base,
                                   pattern=[[sign, P]], channel_multiplier=-sign).then_inc(made, 1)
            st(pool, pool.iota(idx, pattern=[[1, P]], base=0, channel_multiplier=0))
            pool.tensor_copy(k.iota[:], idx).then_inc(made, 1)
            pool.wait_ge(made, 6)


def norm_transpose(k, name, tiles, xn, ht, affine, upto=0):
    nc = k.nc
    n = len(tiles)
    normed, full, free = (k.shared[s] for s in ("rows_normed", "chunk_turned", "chunk_stored"))
    ss, v, r, tmp = (k.small[:, 4 * j:4 * j + n] for j in range(4))
    with nc.Block(no_gpsimd_drain=True) as block:
        @block.vector
        def _(dve):
            st = k.step_v.after
            for t in range(n):
                st(dve, dve.scalar_tensor_tensor(out=xn[:, t, :], in0=tiles[t], scalar=1.0, in1=tiles[t],
                                                 op0=ALU.mult, op1=ALU.mult, accum_out=ss[:, t:t + 1]))
            st(dve, dve.tensor_scalar(v, ss, 1.0 / D, EPS, ALU.mult, ALU.add))
            rsqrt(k, dve, v, r, tmp)
            for t in range(n):
                dve.tensor_scalar(xn[:, t, :], tiles[t], r[:, t:t + 1], None, ALU.mult).then_inc(normed.sem, 1)

        @block.tensor
        def _(pe):
            for c in range(C):
                if c >= 4:
                    pe.wait_ge(*free.at(c - 3))
                for t in range(n):
                    if c == 0:
                        pe.wait_ge(*normed.at(t + 1))
                    last = pe.transpose(k.ps[:, c % 4, t * P:(t + 1) * P], xn[:, t, c * P:(c + 1) * P], k.ident[:])
                last.then_inc(full.sem, 1)

        @block.scalar
        def _(act):
            for c in range(C):
                act.wait_ge(*full.at(c + 1))
                for s, (scale, shift) in enumerate(affine):
                    a, b = s * T, s * T + T
                    last = act.activation(ht[:, c, a:b], k.ps[:, c % 4, a:b], ACT.Identity,
                                          scale=scale[:, c:c + 1], bias=0.0 if shift is None else shift[:, c:c + 1])
                last.then_inc(free.sem, 1)

        @block.sync
        def _(sp):
            issue(k, sp, upto)
    normed.base, full.base, free.base = normed.base + n, full.base + C, free.base + C


def gemm(k, name, tiles, evac, upto, engine="act", banks=4, beside=None, between=None, behind=None,
         after=None):
    nc = k.nc
    full, free = k.shared["tile_full"], k.shared["tile_free"]

    def bank(i):
        t = tiles[i]
        return k.ps[t.row:t.row + t.m, i % banks, 0:t.n]

    def stored(eng, i):
        eng.wait_ge(*free.at(i + 1))

    def empty(eng):
        for i, t in enumerate(tiles):
            eng.wait_ge(*full.at(i + 1))
            if i and engine == "dve":
                eng.wait_ge(*free.at(i))
            evac(eng, t, bank(i)).then_inc(free.sem, 1)
            if between:
                between(eng, i, stored)
        if after:
            after[0](eng)

    with nc.Block(no_gpsimd_drain=True) as block:
        @block.tensor
        def _(pe):
            seen = None
            for i, t in enumerate(tiles):
                if t.load is not None and t.load != seen:
                    arrived(k, pe, t.load)
                    seen = t.load
                if t.needs is not None:
                    stored(pe, t.needs)
                if i >= banks:
                    pe.wait_ge(*free.at(i - banks + 1))
                for j, (lhsT, rhs) in enumerate(t.pairs):
                    last = pe.matmul(bank(i), lhsT, rhs, start=(j == 0), stop=(j == len(t.pairs) - 1))
                last.then_inc(full.sem, 1)
                if t.load is not None:
                    k.release[t.load] = full.at(i + 1)
                if behind:
                    behind(pe, i)
            if after:
                after[1](pe)

        if engine == "act":
            block.scalar(empty)
        else:
            block.vector(empty)

        if beside:
            @block.vector
            def _(dve):
                beside(dve, stored)

        @block.sync
        def _(sp):
            for dst, src, loaded in k.tables:
                sp.dma_start(dst, src).then_inc(loaded, 16)
            issue(k, sp, upto)
            for _, _, loaded in k.tables:
                sp.wait_ge(loaded, 16)
    k.tables = []
    retire(k)
    full.base, free.base = full.base + len(tiles), free.base + len(tiles)


def tile(pairs, n, load=None, m=P, row=0, dst=None, gate=None, bias=None, s=None, c=None, needs=None):
    return Tile(pairs, n, load, m, row, dst, gate, bias, s, c, needs)


def weights(k, n, step):
    w = slot(k, n)
    return w[:, 0:(k.loads[n][0])].rearrange("p (c n) -> p c n", n=step)


class Modulations:

    TILES = 24

    def __init__(self, k, at):
        self.k = k
        self.sc, self.pick = work(k, at, 16), work(k, at + 16, 2)
        self.res = [work(k, at + 18 + 512 * j, 512) for j in range(2)]
        self.ready, self.full, self.done, self.kept, self.turned = (
            k.sem(f"mod_{s}") for s in ("sigmoid", "full", "silu", "kept", "turned"))

    def scalar_start(self, act):
        act.activation(self.sc, self.k.col("cvec"), ACT.Sigmoid).then_inc(self.ready, 1)

    def scalar(self, act, a):
        act.wait_ge(self.full, a + 1)
        if a >= 2:
            act.wait_ge(self.turned, a - 1)
        act.activation(self.res[a % 2], self.k.ps[:, 4 + a % 2, :], ACT.Copy).then_inc(self.kept, 1)

    def vector_start(self, dve):
        k, pick = self.k, self.pick
        st = k.step_v.after
        dve.memset(k.ps[:, 4:6, :], 0.0).then_inc(self.done, 1)
        st(dve, dve.tensor_tensor(pick, k.ident[:, 0:2], k.ident[:, 32:34], ALU.add))
        st(dve, dve.tensor_tensor(pick, pick, k.ident[:, 64:66], ALU.add))
        dve.tensor_tensor(pick, pick, k.ident[:, 96:98], ALU.add).then_inc(self.done, 1)
        dve.wait_ge(self.ready, 1)
        dve.tensor_tensor(self.sc, self.sc, k.col("cvec"), ALU.mult).then_inc(self.done, 1)

    def vector_end(self, dve):
        k = self.k
        for layer in range(2):
            dve.wait_ge(self.turned, 12 * (layer + 1))
            bias = k.col("ada_b")[:, 48 * layer:48 * layer + 48]
            k.step_v.after(dve, dve.tensor_tensor(k.mod[:, layer, :, :],
                                                  k.ps[:, 6 + layer, 0:96].rearrange("p (n s) -> p n s", s=2),
                                                  bias.unsqueeze(2).to_broadcast([P, 48, 2]), ALU.add))

    def turn_rows(self, pe, a):
        pe.wait_ge(self.kept, a + 1)
        for b in range(4):
            at = 2 * (4 * (a % 12) + b)
            last = pe.matmul(self.k.ps[:, 6 + a // 12, at:at + 2], self.res[a % 2][:, b * P:(b + 1) * P], self.pick,
                             start=True, stop=True)
        last.then_inc(self.turned, 1)

    def tensor(self, pe, a):
        k = self.k
        if a == 0:
            pe.wait_ge(self.done, 3)
        else:
            self.turn_rows(pe, a - 1)
        n = k.numbers["ada"][a]
        arrived(k, pe, n)
        w = weights(k, n, 512)
        for c in range(C):
            q = 32 * (c % 4)
            last = pe.matmul(k.ps[q:q + 2, 4 + a % 2, :], self.sc[:, 2 * c:2 * c + 2], w[:, c, :], start=(c < 4),
                             stop=(c >= 4), skip_group_check=True)
        last.then_inc(self.full, 1)
        k.release[n] = (self.full, a + 1)


class StickBreaking:

    PAIRS = SB_HEADS // 2
    W = 384

    def __init__(self, k):
        self.k = k
        (self.z_full, self.logs, self.sp_ready, self.bet_full, self.zb_ready, self.exped, self.a_ready, self.o_full,
         self.o_done) = (k.sem(f"sb_{s}") for s in ("scores", "logs", "softplus", "between", "exponent", "exp",
                                                    "weights", "out", "stored"))

        def buffers(at):
            return [work(k, at + 2 * self.W * b, 2 * self.W).rearrange("p (h w) -> p h w", h=2) for b in range(2)]
        self.A, self.B, self.M = buffers(0), buffers(4096), buffers(16896)
        self.mask = work(k, 18432, self.W)
        k.o_sb = work(k, 18944, 1024).rearrange("p (c t) -> p c t", c=4)

    def tensor_scores(self, pe, g):
        k = self.k
        for j in range(2):
            off = SB_DIM * j
            q, key = k.qkt[off:off + SB_DIM, g, :], k.qkt[off:off + SB_DIM, 4 + g, :]
            pe.matmul(k.ps[:, 3 + j, 0:T], key[:, 0:P], q, start=True, stop=True)
            last = pe.matmul(k.ps[:, 3 + j, T:self.W], key[:, P:T], q[:, P:T], start=True, stop=True)
        last.then_inc(self.z_full, 1)

    def tensor_between(self, pe, g):
        k, M = self.k, self.M[g % 2]
        pe.wait_ge(self.sp_ready, g + 1)
        for j in range(2):
            out = k.ps[:, 5 + j, :]
            pe.matmul(out[:, 0:P], k.key_after[:], M[:, j, 0:P], start=True, stop=True)
            pe.matmul(out[:, P:T], k.key_after[:], M[:, j, P:T], start=True, stop=False)
            pe.matmul(out[:, P:T], k.ones[:], M[:, j, T:self.W], start=False, stop=True)
            last = pe.matmul(out[:, T:self.W], k.key_after[:], M[:, j, T:self.W], start=True, stop=True)
        last.then_inc(self.bet_full, 1)

    def tensor_out(self, pe, g):
        k, A = self.k, self.A[g % 2]
        pe.wait_ge(self.a_ready, g + 1)
        if g:
            pe.wait_ge(self.o_done, g)
        for j in range(2):
            h, off = 2 * g + j, SB_DIM * j
            v = k.tok[:, :, h * SB_DIM:(h + 1) * SB_DIM]
            out = k.ps[off:off + SB_DIM, 7, :]
            pe.matmul(out[:, 0:P], v[:, 0, :], A[:, j, 0:P], start=True, stop=True)
            pe.matmul(out[:, P:T], v[:, 0, :], A[:, j, P:T], start=True, stop=False)
            last = pe.matmul(out[:, P:T], v[:, 1, :], A[:, j, T:self.W], start=False, stop=True)
        last.then_inc(self.o_full, 1)

    def scalar_logs(self, act, g):
        k, st = self.k, self.k.step_a.after
        A, B = self.A[g % 2], self.B[g % 2]
        act.wait_ge(self.z_full, g + 1)
        st(act, act.activation(B, k.ps[:, 3:5, 0:self.W], ACT.Copy, scale=SB_DIM ** -0.5))
        st(act, act.activation(A, B, ACT.Abs))
        st(act, act.activation(A, A, ACT.Exp, scale=-1.0))
        act.activation(A, A, ACT.Ln, bias=1.0).then_inc(self.logs, 1)

    def scalar_exp(self, act, g):
        act.wait_ge(self.zb_ready, g + 1)
        act.activation(self.A[g % 2], self.B[g % 2], ACT.Exp).then_inc(self.exped, 1)

    def scalar_store(self, act, g):
        act.wait_ge(self.o_full, g + 1)
        act.activation(self.k.o_sb[:, g, :], self.k.ps[:, 7, 0:T], ACT.Copy).then_inc(self.o_done, 1)

    def vector_mask(self, dve):
        k, mask, st = self.k, self.mask, self.k.step_v.after
        st(dve, dve.tensor_copy(mask[:, 0:P], k.key_before[:]))
        st(dve, dve.tensor_copy(mask[:, P:T], k.ones[:]))
        st(dve, dve.tensor_copy(mask[:, T:self.W], k.key_before[:]))

    def vector(self, dve, g):
        k, st = self.k, self.k.step_v.after
        A, B, M = self.A[g % 2], self.B[g % 2], self.M[g % 2]
        mask = self.mask.unsqueeze(1).to_broadcast([P, 2, self.W])
        dve.wait_ge(self.logs, g + 1)
        A2, B2, M2 = (v.rearrange("p h w -> p (h w)") for v in (A, B, M))
        st(dve, dve.scalar_tensor_tensor(out=M2, in0=B2, scalar=0.0, in1=A2, op0=ALU.max, op1=ALU.add))
        st(dve, dve.tensor_tensor(B, B, M, ALU.subtract))
        dve.tensor_tensor(M, M, mask, ALU.mult).then_inc(self.sp_ready, 1)
        dve.wait_ge(self.bet_full, g + 1)
        dve.tensor_tensor(B, B, k.ps[:, 5:7, 0:self.W], ALU.subtract).then_inc(self.zb_ready, 1)
        dve.wait_ge(self.exped, g + 1)
        dve.tensor_tensor(A, A, mask, ALU.mult).then_inc(self.a_ready, 1)


def first_projections(k):
    xn = work(k, 0, 2048).rearrange("p (a d) -> p a d", a=TT)
    mem = work(k, 0, 2048).rearrange("p (a d) -> p a d", a=TT)
    k.ht = work(k, 2048, 2048).rearrange("p (c t) -> p c t", c=C)
    mht = work(k, 4096, 2048).rearrange("p (c t) -> p c t", c=C)
    k.tok = work(k, 6144, 6656).rearrange("p (a n) -> p a n", a=TT)
    k.kv = work(k, 12800, 2048).rearrange("p (a n) -> p a n", a=TT)
    k.qkt = work(k, 14848, 2048).rearrange("p (c t) -> p c t", c=C)
    mn = work(k, 16896, 2048).rearrange("p (a d) -> p a d", a=TT)
    norm_transpose(k, "mem", [mem[:, t, :] for t in range(TT)], mn, mht, [(k.col("g_mem"), None)])
    norm_transpose(k, "x1", [k.x[:, t, :] for t in range(TT)], xn, k.ht, [(k.col("g_mix"), None)])
    tiles = []
    tile_of = {}
    p0, m0 = k.stage["proj"], k.stage["mem_kv"]
    for a in range(2):
        w = weights(k, m0 + a, 512)
        for t in range(TT):
            tiles.append(tile([(mht[:, c, t * P:(t + 1) * P], w[:, c, :]) for c in range(C)], 512, m0 + a,
                              dst=k.kv[:, t, 512 * a:512 * a + 512]))
            if a == 0:
                tile_of["mem_k", t] = len(tiles) - 1
    for a in range(2):
        w = weights(k, p0 + a, 512)
        for b in range(4):
            tiles.append(tile([(w[:, c, b * P:(b + 1) * P], k.ht[:, c, :]) for c in range(C)], T, p0 + a,
                              dst=k.qkt[:, 4 * a + b, :]))
    for a in range(2, 9):
        n = min(512, 4352 - 512 * a)
        w = weights(k, p0 + a, n)
        for t in range(TT):
            at = 512 * (a - 2)
            tiles.append(tile([(k.ht[:, c, t * P:(t + 1) * P], w[:, c, :]) for c in range(C)], n, p0 + a,
                              dst=k.tok[:, t, at:at + n]))
            if (a, t) == (2, 1):
                values = len(tiles) - 1
            if a in (5, 8):
                tile_of[("dil", "mem_q")[a // 8], t] = len(tiles) - 1
    sb = StickBreaking(k)
    norms = head_norms(k, tile_of)
    scores_of = {values + 3 * g: g for g in range(sb.PAIRS)}
    between_of = {values + 3 * g + 2: g for g in range(sb.PAIRS)}
    out_of = {values + 3 * g + 3: g for g in range(sb.PAIRS)}
    assert max(out_of) <= len(tiles) - 1

    def behind(pe, i):
        if i == values:
            pe.wait_ge(*k.shared["tile_free"].at(values + 1))
        if i in between_of:
            sb.tensor_between(pe, between_of[i])
        if i in out_of:
            sb.tensor_out(pe, out_of[i])
        if i in scores_of:
            sb.tensor_scores(pe, scores_of[i])

    def between(act, i, stored):
        if i in between_of:
            sb.scalar_exp(act, between_of[i])
        if i in out_of:
            sb.scalar_store(act, out_of[i])
        if i in scores_of:
            sb.scalar_logs(act, scores_of[i])

    def beside(dve, stored):
        sb.vector_mask(dve)
        for g in range(sb.PAIRS):
            sb.vector(dve, g)
            if g == 1:
                norms(dve, stored, 0)
        norms(dve, stored, 1)

    gemm(k, "proj", tiles, lambda eng, t, ps: eng.activation(t.dst, ps, ACT.Copy), p0 + 9 + SLOTS, banks=3,
         beside=beside, between=between, behind=behind)


def head_norms(k, tile_of):
    sq = work(k, 16896, 2048)
    nd, nm = 2 * DIL_HEADS, MEM_HEADS
    rounds = ([(k.tok[:, t, 512:512 + nd * DIL_DIM], nd, DIL_DIM, tile_of["dil", t]) for t in range(TT)],
              [(k.kv[:, t, 0:512], nm, MEM_DIM, tile_of["mem_k", t]) for t in range(TT)]
              + [(k.tok[:, t, 2816:3328], nm, MEM_DIM, tile_of["mem_q", t]) for t in range(TT)])

    def norms(dve, stored, r):
        st = k.step_v.after
        groups = rounds[r]
        total = sum(n for _, n, _, _ in groups)
        ss, v, r, tmp = (k.small[:, 64 + 64 * j:64 + 64 * j + total] for j in range(4))
        at = 0
        for src, n, width, made in groups:
            stored(dve, made)
            s = sq[:, 0:n * width]
            st(dve, dve.tensor_tensor(s, src, src, ALU.mult))
            st(dve, dve.tensor_reduce(ss[:, at:at + n], s.rearrange("p (n w) -> p n w", n=n), AX.X, ALU.add))
            st(dve, dve.tensor_scalar(v[:, at:at + n], ss[:, at:at + n], 1.0 / width, EPS, ALU.mult, ALU.add))
            at += n
        rsqrt(k, dve, v, r, tmp)
        at = 0
        for src, n, width, _ in groups:
            s = src.rearrange("p (n w) -> p n w", n=n)
            st(dve, dve.tensor_tensor(s, s, r[:, at:at + n].unsqueeze(2).to_broadcast([P, n, width]), ALU.mult))
            at += n
    return norms


def head_turns(k):
    nc = k.nc
    full, free = k.sem("heads_turned"), k.sem("heads_stored")
    dq = k.tok[:, :, 512:512 + 2 * DIL_HEADS * DIL_DIM]
    mq = k.tok[:, :, 2816:3328]
    mk = k.kv[:, :, 0:512]
    k.dqt = work(k, 0, 1536).rearrange("p (c t) -> p c t", c=6)
    k.dkt = work(k, 4096 + 0, 1536).rearrange("p (c t) -> p c t", c=6)
    k.mqt = work(k, 14848, 1024).rearrange("p (c t) -> p c t", c=4)
    k.mkt = work(k, 15872, 1024).rearrange("p (c t) -> p c t", c=4)
    turns = [(dq[:, :, c * P:(c + 1) * P], k.dqt[:, c, :], "gq_dil") for c in range(6)] \
        + [(dq[:, :, 768 + c * P:768 + (c + 1) * P], k.dkt[:, c, :], "gk_dil") for c in range(6)] \
        + [(mq[:, :, c * P:(c + 1) * P], k.mqt[:, c, :], "gq_mem") for c in range(4)] \
        + [(mk[:, :, c * P:(c + 1) * P], k.mkt[:, c, :], "gk_mem") for c in range(4)]
    with nc.Block(no_gpsimd_drain=True) as block:
        @block.tensor
        def _(pe):
            for i, (src, _, _) in enumerate(turns):
                if i >= 4:
                    pe.wait_ge(free, i - 3)
                for t in range(TT):
                    last = pe.transpose(k.ps[:, i % 4, t * P:(t + 1) * P], src[:, t, :], k.ident[:])
                last.then_inc(full, 1)

        @block.scalar
        def _(act):
            for i, (_, dst, g) in enumerate(turns):
                act.wait_ge(full, i + 1)
                act.activation(dst, k.ps[:, i % 4, 0:T], ACT.Identity, scale=k.col(g), bias=0.0).then_inc(free, 1)


def softmax_attentions(k):
    nc = k.nc
    scores, soft, turned, copied, out_full, out_done, exped, maxed, idx_made = (
        k.sem(f"sm_{s}") for s in ("scores", "normed", "turned", "copied", "out", "stored", "exp", "max", "index"))
    S = [work(k, at, 768) for at in (6144, 6912, 12288)]
    PT = [work(k, 9472 + 768 * b, 768) for b in range(2)]
    idx = work(k, 7680, 512).bitcast(I32)
    low = work(k, 6144, 512).bitcast(I32)
    far = work(k, 6656, 512)
    dist = work(k, 11008, 512)
    bar = work(k, 16896, 1536)
    k.o_dil = work(k, 18432, 512).rearrange("p (c t) -> p c t", c=2)
    k.o_mem = work(k, 19968, 1024).rearrange("p (c t) -> p c t", c=4)
    neg, tot, inv = (k.small[:, 320 + 2 * j:322 + 2 * j] for j in range(3))
    units = [("dil", h, t) for t in range(TT) for h in range(DIL_SLOTS)] + \
            [("mem", h, t) for t in range(TT) for h in range(MEM_HEADS)]
    dv = k.tok[:, :, 2048:2816]
    mv = k.kv[:, :, 512:1024]
    flat = k.ps[:].rearrange("p b n -> p (b n)")

    def width(u):
        return P * (u[2] + 1) if u[0] == "dil" else T

    def groups(u):
        return DIL_GROUPS if u[0] == "dil" else 1

    def block_of(u, buf):
        return buf[:, 0:groups(u) * T].rearrange("p (g j) -> p g j", j=T)[:, :, 0:width(u)]

    with nc.Block(no_gpsimd_drain=True) as block:
        @block.gpsimd
        def _(pool):
            pool.iota(idx, pattern=[[P, TT], [-1, T]], base=0, channel_multiplier=1).then_inc(idx_made, 1)

        @block.tensor
        def _(pe):
            def score(i):
                kind, h, t = u = units[i]
                if i >= 2:
                    pe.wait_ge(maxed, i - 1)
                base = 1024 * (i % 2)
                for g in range(groups(u)):
                    out = flat[:, base + T * g:base + T * g + width(u)]
                    if kind == "dil":
                        head = DIL_SLOTS * g + h
                        off, c = DIL_DIM * (head % 2), head // 2
                        last = pe.matmul(out, k.dqt[off:off + DIL_DIM, c, t * P:(t + 1) * P],
                                         k.dkt[off:off + DIL_DIM, c, 0:width(u)], start=True, stop=True)
                    else:
                        last = pe.matmul(out, k.mqt[:, h, t * P:(t + 1) * P], k.mkt[:, h, :], start=True, stop=True)
                last.then_inc(scores, 1)

            score(0)
            score(1)
            for i, u in enumerate(units):
                kind, h, t = u
                kts = width(u) // P
                if i + 2 < len(units):
                    score(i + 2)
                pe.wait_ge(soft, i + 1)
                if i:
                    pe.wait_ge(copied, i)
                for g in range(groups(u)):
                    for j in range(kts):
                        at = 2048 + P * (g * kts + j)
                        last = pe.transpose(flat[:, at:at + P], S[i % 3][:, T * g + P * j:T * g + P * j + P],
                                            k.ident[:])
                last.then_inc(turned, 1)
                pe.wait_ge(copied, i + 1)
                if i >= 2:
                    pe.wait_ge(out_done, i - 1)
                n = groups(u) * kts
                off = DIL_DIM * (h % 2)
                for j in range(n):
                    g, kt = j // kts, j % kts
                    if kind == "dil":
                        v = dv[:, kt, (DIL_SLOTS * g + h) * DIL_DIM:(DIL_SLOTS * g + h + 1) * DIL_DIM]
                        out = k.ps[off:off + DIL_DIM, 6 + i % 2, 0:P]
                    else:
                        v, out = mv[:, kt, h * P:(h + 1) * P], k.ps[:, 6 + i % 2, 0:P]
                    last = pe.matmul(out, v, PT[i % 2][:, j * P:(j + 1) * P], start=(j == 0), stop=(j == n - 1))
                last.then_inc(out_full, 1)

        @block.vector
        def _(dve):
            st = k.step_v.after
            dve.wait_ge(idx_made, 1)
            st(dve, dve.tensor_copy(dist, idx))
            st(dve, dve.tensor_scalar(far, dist, 0.0, NEG, ALU.is_lt, ALU.mult))
            for g, dil in enumerate(DILATIONS):
                b = bar[:, 512 * g:512 * g + 512]
                st(dve, dve.tensor_scalar(low, idx, dil - 1, None, ALU.bitwise_and))
                st(dve, dve.tensor_scalar(b, low, 0.0, NEG, ALU.not_equal, ALU.mult))
                st(dve, dve.tensor_tensor(b, b, far, ALU.min))
            for g, dil in enumerate(DILATIONS):
                if DIL_REACH * dil < T:
                    b = bar[:, 512 * g:512 * g + 512]
                    st(dve, dve.tensor_scalar(far, dist, float(DIL_REACH * dil), NEG, ALU.is_gt, ALU.mult))
                    st(dve, dve.tensor_tensor(b, b, far, ALU.min))

            def biased(i):
                kind, h, t = u = units[i]
                dve.wait_ge(scores, i + 1)
                if i >= 3:
                    dve.wait_ge(turned, i - 2)
                s = block_of(u, S[i % 3])
                ps = block_of(u, flat[:, 1024 * (i % 2):1024 * (i % 2) + 1024])
                if kind == "dil":
                    b = bar.rearrange("p (g t j) -> p g t j", g=DIL_GROUPS, t=TT)[:, :, t, 0:width(u)]
                    st(dve, dve.scalar_tensor_tensor(out=s, in0=ps, scalar=DIL_DIM ** -0.5, in1=b,
                                                     op0=ALU.mult, op1=ALU.add))
                    for g in range(DIL_GROUPS):
                        slope = 2.0 ** (-8.0 * (DIL_SLOTS * g + h + 1) / DIL_HEADS)
                        sg = S[i % 3][:, T * g:T * g + width(u)]
                        last = dve.scalar_tensor_tensor(out=sg, in0=dist[:, T * t:T * t + width(u)], scalar=-slope,
                                                        in1=sg, op0=ALU.mult, op1=ALU.add)
                        st(dve, last)
                else:
                    st(dve, dve.tensor_scalar(s, ps, MEM_DIM ** -0.5, None, ALU.mult))
                dve.tensor_reduce(neg[:, i % 2:i % 2 + 1], s, AX.XY, ALU.max, negate=True).then_inc(maxed, 1)

            biased(0)
            for i, u in enumerate(units):
                if i + 1 < len(units):
                    biased(i + 1)
                dve.wait_ge(exped, i + 1)
                b = slice(i % 2, i % 2 + 1)
                st(dve, dve.reciprocal(inv[:, b], tot[:, b]))
                s = block_of(u, S[i % 3])
                dve.tensor_scalar(s, s, inv[:, b], None, ALU.mult).then_inc(soft, 1)

        @block.scalar
        def _(act):
            def exp(i):
                act.wait_ge(maxed, i + 1)
                b = slice(i % 2, i % 2 + 1)
                if i >= 2:
                    act.wait_ge(soft, i - 1)
                s = block_of(units[i], S[i % 3])
                act.activation(s, s, ACT.Exp, bias=neg[:, b], accum_out=tot[:, b]).then_inc(exped, 1)

            def store(i):
                kind, h, t = units[i]
                act.wait_ge(out_full, i + 1)
                if kind == "dil":
                    off = DIL_DIM * (h % 2)
                    act.activation(k.o_dil[off:off + DIL_DIM, h // 2, t * P:(t + 1) * P],
                                   k.ps[off:off + DIL_DIM, 6 + i % 2, 0:P], ACT.Copy).then_inc(out_done, 1)
                else:
                    act.activation(k.o_mem[:, h, t * P:(t + 1) * P], k.ps[:, 6 + i % 2, 0:P], ACT.Copy)\
                       .then_inc(out_done, 1)

            exp(0)
            for i, u in enumerate(units):
                if i + 1 < len(units):
                    exp(i + 1)
                act.wait_ge(turned, i + 1)
                if i >= 2:
                    act.wait_ge(out_full, i - 1)
                n = P * groups(u) * (width(u) // P)
                act.activation(PT[i % 2][:, 0:n], flat[:, 2048:2048 + n], ACT.Copy).then_inc(copied, 1)
                if i:
                    store(i - 1)
            store(len(units) - 1)


def gated_merge(k):
    nc = k.nc
    y = work(k, 4096, 6144).rearrange("p (b a d) -> p b a d", b=3, a=TT)
    merged = work(k, 10240, 2048).rearrange("p (a d) -> p a d", a=TT)
    gates = [work(k, 12288 + 512 * b, 512) for b in range(2)]
    b_gate = work(k, 13312, 3072)[0:1, :]
    mt = work(k, 16384, 2048).rearrange("p (c t) -> p c t", c=C)
    tiles = []
    for br, (name, o) in enumerate((("o_sb", k.o_sb), ("o_dil", k.o_dil), ("o_mem", k.o_mem))):
        n = k.stage[name]
        w = weights(k, n, D)
        for t in range(TT):
            for half in range(2):
                cs = slice(512 * half, 512 * half + 512)
                tiles.append(tile([(o[:, c, t * P:(t + 1) * P], w[:, c, cs]) for c in range(w.shape[1])], 512, n,
                                  dst=y[:, br, t, cs]))
    gemm(k, "branches", tiles, lambda eng, t, ps: eng.activation(t.dst, ps, ACT.Copy), k.stage["gate"] + SLOTS)

    loaded, full, opened, merged_n = (k.sem(f"gates_{s}") for s in ("bias", "full", "open", "merged"))
    g0 = k.stage["gate"]
    order = [(half, br, t) for half in range(2) for br in range(3) for t in range(TT)]
    with nc.Block(no_gpsimd_drain=True) as block:
        @block.tensor
        def _(pe):
            pe.wait_ge(loaded, 16)
            for i, (half, br, t) in enumerate(order):
                n = g0 + 3 * half + br
                arrived(k, pe, n)
                if i >= 4:
                    pe.wait_ge(opened, i - 3)
                w = weights(k, n, 512)
                for c in range(C):
                    pe.matmul(k.ps[:, i % 4, :], k.ht[:, c, t * P:(t + 1) * P], w[:, c, :], start=(c == 0), stop=False)
                at = D * br + 512 * half
                pe.matmul(k.ps[:, i % 4, :], k.ones[0:1, :], b_gate[:, at:at + 512], start=False, stop=True)\
                  .then_inc(full, 1)
                k.release[n] = (full, i + 1)

        @block.scalar
        def _(act):
            for i in range(len(order)):
                act.wait_ge(full, i + 1)
                if i >= 2:
                    act.wait_ge(merged_n, i - 1)
                act.activation(gates[i % 2], k.ps[:, i % 4, :], ACT.Sigmoid).then_inc(opened, 1)

        @block.vector
        def _(dve):
            for i, (half, br, t) in enumerate(order):
                dve.wait_ge(opened, i + 1)
                cs = slice(512 * half, 512 * half + 512)
                g, out = gates[i % 2], merged[:, t, cs]
                if br == 0:
                    dve.tensor_tensor(out, g, y[:, br, t, cs], ALU.mult).then_inc(merged_n, 1)
                else:
                    k.step_v.after(dve, dve.tensor_tensor(g, g, y[:, br, t, cs], ALU.mult))
                    dve.wait_ge(merged_n, i)
                    dve.tensor_tensor(out, out, g, ALU.add).then_inc(merged_n, 1)

        @block.sync
        def _(sp):
            sp.dma_start(b_gate, k.dram["b_gate"]).then_inc(loaded, 16)
            issue(k, sp, g0 + 6 + SLOTS)
            sp.wait_ge(loaded, 16)
    retire(k)
    turn(k, "merged", merged, mt, None)
    n0 = k.stage["mix_out"]
    tiles = []
    for a in range(2):
        w = weights(k, n0 + a, 512)
        for t in range(TT):
            tiles.append(tile([(mt[:, c, t * P:(t + 1) * P], w[:, c, :]) for c in range(C)], 512, n0 + a,
                              dst=k.x[:, t, 512 * a:512 * a + 512]))
    k.subkeys = work(k, 14336, 2048).rearrange("p (h n) -> p h n", h=16)
    k.tables.append((k.subkeys, k.dram["subkeys_t"], k.sem("subkeys_loaded")))
    gemm(k, "mix_out", tiles, lambda eng, t, ps: eng.tensor_tensor(t.dst, t.dst, ps, ALU.add), n0 + 2 + SLOTS, "dve")


def turn(k, name, src, dst, scale):
    full, free = k.shared["chunk_turned"], k.shared["chunk_stored"]
    n, chunks = src.shape[1], src.shape[2] // P
    with k.nc.Block(no_gpsimd_drain=True) as block:
        @block.tensor
        def _(pe):
            for c in range(chunks):
                if c >= 4:
                    pe.wait_ge(*free.at(c - 3))
                for t in range(n):
                    last = pe.transpose(k.ps[:, c % 4, t * P:(t + 1) * P], src[:, t, c * P:(c + 1) * P], k.ident[:])
                last.then_inc(full.sem, 1)

        @block.scalar
        def _(act):
            for c in range(chunks):
                act.wait_ge(*full.at(c + 1))
                ps = k.ps[:, c % 4, 0:n * P]
                if scale is None:
                    act.activation(dst[:, c, :], ps, ACT.Copy).then_inc(free.sem, 1)
                else:
                    act.activation(dst[:, c, :], ps, ACT.Identity, scale=scale[:, c:c + 1], bias=0.0)\
                       .then_inc(free.sem, 1)
    full.base, free.base = full.base + chunks, free.base + chunks


def peer_select(k):
    xn = work(k, 4096, 2048).rearrange("p (a d) -> p a d", a=TT)
    k.h2t = work(k, 8192, 2048).rearrange("p (c t) -> p c t", c=C)
    qpt = work(k, 0, 4096).rearrange("p (h t) -> p h t", h=16)
    sc = work(k, 10240, 4096).rearrange("p (a h n) -> p a h n", a=TT, h=16)
    norm_transpose(k, "x2", [k.x[:, t, :] for t in range(TT)], xn, k.h2t, [(k.col("g_ffn"), None)])
    tiles, score_of, mod_at = [], {}, {}

    def query(h):
        n, b = k.numbers["peer_q"][h // 4], h % 4
        w = weights(k, n, 512)
        tiles.append(tile([(w[:, c, b * P:(b + 1) * P], k.h2t[:, c, :]) for c in range(C)], T, n,
                          dst=qpt[:, h, :]))
        return len(tiles) - 1

    made = [query(0)]
    mod_at[0] = (0, 1)
    for h in range(16):
        if h + 1 < 16:
            made.append(query(h + 1))
        for t in range(TT):
            score_of[t, h] = len(tiles)
            tiles.append(tile([(qpt[:, h, t * P:(t + 1) * P], k.subkeys[:, h, :])], P, needs=made[h],
                              dst=sc[:, t, h, :]))
        if h < 12:
            mod_at[len(tiles) - 1] = (h + 2,)
    mixed_in = 14

    K, H = PEER_TOPK, PEER_HEADS
    vals = work(k, 4096, 512).rearrange("p (a h n) -> p a h n", a=TT, h=16)
    inds = work(k, 4608, 512).bitcast(U32).rearrange("p (a h n) -> p a h n", a=TT, h=16)
    indf = work(k, 5120, 64).rearrange("p (s a n) -> p s a n", s=2, a=TT)
    tops = work(k, 5632, 256).rearrange("p (a h n) -> p a h n", a=TT, h=H)
    pos = work(k, 5888, 256).bitcast(U32).rearrange("p (a h n) -> p a h n", a=TT, h=H)
    rest = (work(k, 6144, P), work(k, 17432, P))
    cand = (work(k, 6272, 256), work(k, 17560, 256))
    rest2 = (work(k, 6528, 256), work(k, 17816, 256))
    half = work(k, 6784, 64).bitcast(U32).rearrange("p (s a n) -> p s a n", s=2, a=TT)
    halff = work(k, 7040, 64).rearrange("p (s a n) -> p s a n", s=2, a=TT)
    pick = work(k, 7296, 512).rearrange("p (s a h n) -> p s a h n", s=2, a=TT, h=H)
    gate = work(k, 7808, 256).rearrange("p (a h n) -> p a h n", a=TT, h=H)
    one_hot = work(k, 19200, 1024).rearrange("p (s n m) -> p s n m", s=2 * TT, n=K)
    k.e_t = work(k, 18432, 768).rearrange("p (s t) -> p s t", s=3)
    sums, inv = k.small[:, 0:16], k.small[:, 16:32]
    mods = Modulations(k, 16384)
    picked = k.sem("select_picked")
    shifted, exped, ready, full, turned = (
        k.sem(f"select_{s}") for s in ("shifted", "exp", "ready", "turned", "stored"))

    def between(act, i, stored):
        if i == 0:
            mods.scalar_start(act)
        for a in mod_at.get(i, ()):
            mods.scalar(act, a)

    def behind(pe, i):
        for a in mod_at.get(i, ()):
            mods.tensor(pe, a)

    def select(dve, stored):
        st = k.step_v.after
        both = k.step_v.both
        low = -3.0e38
        mods.vector_start(dve)

        def best(v, i, src, scratch):
            for r in range(2):
                at = slice(8 * r, 8 * r + 8)
                s = scratch if r else src
                both(dve, *(dve.max(v[t][:, at], s[t]) for t in range(TT)))
                both(dve, *(dve.max_index(i[t][:, at], v[t][:, at], s[t]) for t in range(TT)))
                if r == 0:
                    both(dve, *(dve.match_replace(scratch[t], v[t][:, at], src[t], low) for t in range(TT)))

        for head in range(H):
            for h in (2 * head, 2 * head + 1):
                stored(dve, score_of[1, h])
                best(*([src[:, t, h, :] for t in range(TT)] for src in (vals, inds, sc)), rest)
            both(dve, *(dve.tensor_tensor(cand[t].rearrange("p (a b) -> p a b", a=K),
                                          vals[:, t, 2 * head, :].unsqueeze(2).to_broadcast([P, K, K]),
                                          vals[:, t, 2 * head + 1, :].unsqueeze(1).to_broadcast([P, K, K]), ALU.add)
                        for t in range(TT)))
            best(*([src[:, t, head, :] for t in range(TT)] for src in (tops, pos)), cand, rest2)
            both(dve, dve.tensor_scalar(half[:, 0], pos[:, :, head, :], 4, None, ALU.logical_shift_right),
                 dve.tensor_scalar(half[:, 1], pos[:, :, head, :], 15, None, ALU.bitwise_and))
            both(dve, dve.tensor_copy(halff, half),
                 dve.tensor_copy(indf, inds[:, :, 2 * head:2 * head + 2, :].rearrange("p a s n -> p s a n")))
            st(dve, dve.tensor_tensor(one_hot, halff.rearrange("p s a n -> p (s a) n").unsqueeze(3)
                                      .to_broadcast([P, 2 * TT, K, K]),
                                      k.iota[:, 0:K].unsqueeze(1).unsqueeze(1).to_broadcast([P, 2 * TT, K, K]),
                                      ALU.is_equal))
            st(dve, dve.tensor_tensor(one_hot, one_hot, indf.rearrange("p s a n -> p (s a) n").unsqueeze(2)
                                      .to_broadcast([P, 2 * TT, K, K]), ALU.mult))
            for sel in range(2):
                dve.tensor_reduce(pick[:, sel, :, head, :], one_hot[:, TT * sel:TT * sel + TT], AX.X, ALU.add)\
                   .then_inc(picked, 1)
            dve.wait_ge(picked, 2 * head + 2)
        t3 = tops.rearrange("p a h n -> p (a h) n")
        g3 = gate.rearrange("p a h n -> p (a h) n")
        dve.tensor_tensor(g3, t3, t3[:, :, 0:1].to_broadcast([P, TT * H, K]), ALU.subtract).then_inc(shifted, 1)
        dve.wait_ge(exped, 1)
        st(dve, dve.tensor_reduce(sums, g3, AX.X, ALU.add))
        st(dve, dve.reciprocal(inv, sums))
        dve.tensor_tensor(g3, g3, inv.unsqueeze(2).to_broadcast([P, TT * H, K]), ALU.mult).then_inc(ready, 1)
        mods.vector_end(dve)

    def scalar_part(act):
        for a in range(mixed_in, mods.TILES):
            mods.scalar(act, a)
        act.wait_ge(shifted, 1)
        act.activation(gate, gate, ACT.Exp).then_inc(exped, 1)
        act.wait_ge(full, 1)
        act.activation(k.e_t, k.ps[:, 0:3, 0:T], ACT.Copy).then_inc(turned, 1)

    def tensor_part(pe):
        for a in range(mixed_in, mods.TILES):
            mods.tensor(pe, a)
        mods.turn_rows(pe, mods.TILES - 1)
        pe.wait_ge(ready, 1)
        for s in range(3):
            for t in range(TT):
                src = (gate[:, t, :, :] if s == 2 else pick[:, s, t, :, :]).rearrange("p h n -> p (h n)")
                last = pe.transpose(k.ps[:, s, t * P:(t + 1) * P], src, k.ident[:])
        last.then_inc(full, 1)

    gemm(k, "peer_q", tiles, lambda eng, t, ps: eng.activation(t.dst, ps, ACT.Copy), k.stage["a_gates"],
         beside=select, between=between, behind=behind, after=(scalar_part, tensor_part))


def peer_gates(k):
    nc = k.nc
    N, STEPS = 8, 4
    TURNS = T // (N * STEPS)
    k.gates = k.big[:, R_RING:R_RING + PEER_KEYS * T].rearrange("p (i t) -> p i t", i=PEER_KEYS)
    first = [work(k, 10240 + 1024 * b, 1024).rearrange("p (t i) -> p t i", t=N) for b in range(STEPS)]
    second = [work(k, 14336 + 1024 * b, 1024).rearrange("p (t i) -> p t i", t=N) for b in range(STEPS)]
    row = k.iota[:].unsqueeze(1).to_broadcast([P, N, P])
    hot, made, full, stored = (k.sem(f"gates_{s}") for s in ("hot", "weighted", "products", "spread"))
    e_t = k.e_t

    def columns(s, t):
        return e_t[:, s, bass.ds(t, N)].unsqueeze(2).to_broadcast([P, N, P])

    with nc.Block(no_gpsimd_drain=True) as block:
        def turns(eng, body):
            for b in range(STEPS):
                body(b, b, False)
            with eng.Fori(1, TURNS) as i:
                for b in range(STEPS):
                    body(i * STEPS + b, b, True)

        @block.vector
        def _(dve):
            def step(n, b, later):
                if later:
                    dve.wait_ge(full, n - STEPS + 1)
                dve.tensor_tensor(first[b], row, columns(0, n * N), ALU.is_equal).then_inc(hot, 1)
                dve.tensor_tensor(second[b], row, columns(1, n * N), ALU.is_equal).then_inc(hot, 1)
            turns(dve, step)

        @block.gpsimd
        def _(pool):
            def step(n, b, later):
                pool.wait_ge(hot, n * 2 + 1)
                pool.tensor_tensor(first[b], first[b], columns(2, n * N), ALU.mult).then_inc(made, 1)
            turns(pool, step)

        @block.tensor
        def _(pe):
            def step(n, b, later):
                pe.wait_ge(made, n + 1)
                pe.wait_ge(hot, n * 2 + 2)
                if later:
                    pe.wait_ge(stored, n - STEPS + 1)
                for t in range(N):
                    last = pe.matmul(k.ps[:, 2 * b + t // 4, (t % 4) * P:(t % 4 + 1) * P],
                                     first[b][:, t, :], second[b][:, t, :], start=True, stop=True)
                last.then_inc(full, 1)
            turns(pe, step)

        @block.scalar
        def _(act):
            def step(n, b, later):
                act.wait_ge(full, n + 1)
                src = k.ps[:, 2 * b:2 * b + 2, :].rearrange("p b (t i) -> p i (b t)", i=P)
                act.activation(k.gates[:, :, bass.ds(n * N, N)], src, ACT.Copy).then_inc(stored, 1)
            turns(act, step)


def peer_experts(k):
    nc = k.nc
    RING = 4
    u_slot = [work(k, 10240 + 1024 * b, 1024).rearrange("p (c i) -> p c i", c=C) for b in range(RING)]
    v_slot = [work(k, 14336 + 1024 * b, 1024) for b in range(RING)]
    act_buf = [work(k, 19200 + T * b, T) for b in range(2)]
    w_buf = [work(k, 19712 + T * b, T) for b in range(2)]
    u_loaded = [k.sem(f"u_loaded{b}") for b in range(RING)]
    v_loaded = [k.sem(f"v_loaded{b}") for b in range(RING)]
    act_full, gelu_done, w_ready, out_done, added = (
        k.sem(f"peer_{s}") for s in ("act_full", "gelu_done", "w_ready", "out_done", "added"))
    u = k.dram["peer_u_t"].rearrange("j p c i -> p j (c i)")
    v = k.dram["peer_v"][0].rearrange("(i j) d -> i j d", j=PEER_KEYS)
    TURNS = PEER_KEYS // RING

    def one(eng, n):
        return bass.ds(n, 1)

    with nc.Block(no_gpsimd_drain=True) as block:
        @block.sync
        def _(sp):
            def load(n, b, later):
                if later:
                    sp.wait_ge(act_full, n - 3)
                sp.dma_start(u_slot[b].rearrange("p c i -> p (c i)").unsqueeze(1), u[:, one(sp, n), :])\
                  .then_inc(u_loaded[b], 16)
                if later:
                    sp.wait_ge(out_done, n - 3)
                sp.dma_start(v_slot[b].unsqueeze(1), v[:, one(sp, n), :]).then_inc(v_loaded[b], 16)
            for b in range(RING):
                load(b, b, False)
            with sp.Fori(1, TURNS) as i:
                for b in range(RING):
                    load(i * RING + b, b, True)

        @block.tensor
        def _(pe):
            def act_of(n, b, turn, first):
                pe.wait_ge(u_loaded[b], turn * 16 + 16)
                if not first:
                    pe.wait_ge(gelu_done, n - 1)
                for c in range(C):
                    last = pe.matmul(k.ps[:, 4 + b % 2, 0:T], u_slot[b][:, c, :], k.h2t[:, c, :],
                                     start=(c == 0), stop=(c == C - 1))
                last.then_inc(act_full, 1)

            def out_of(n, b, turn, first, final):
                pe.wait_ge(w_ready, n + 1)
                pe.wait_ge(v_loaded[b], turn * 16 + 16)
                for t in range(TT):
                    for half in range(2):
                        last = pe.matmul(k.ps[:, 2 * t + half, :], w_buf[b % 2][:, t * P:(t + 1) * P],
                                         v_slot[b][:, 512 * half:512 * half + 512], start=first, stop=final,
                                         skip_group_check=True)
                last.then_inc(out_done, 1)

            def tiles(turn, first, final):
                for b in range(RING):
                    n = turn * RING + b
                    if b < RING - 1:
                        act_of(n + 1, b + 1, turn, first and b == 0)
                    elif not final:
                        act_of(n + 1, 0, turn + 1, False)
                    out_of(n, b, turn, first and b == 0, final and b == RING - 1)

            act_of(0, 0, 0, True)
            tiles(0, True, False)
            with pe.Fori(1, TURNS - 1) as i:
                tiles(i, False, False)
            tiles(TURNS - 1, False, True)

        def turns(eng, body):
            for b in range(RING):
                body(b, b, b < 2)
            with eng.Fori(1, TURNS) as i:
                for b in range(RING):
                    body(i * RING + b, b, False)

        @block.scalar
        def _(act):
            def gelu(n, b, first):
                act.wait_ge(act_full, n + 1)
                if not first:
                    act.wait_ge(w_ready, n - 1)
                act.activation(act_buf[b % 2], k.ps[:, 4 + b % 2, 0:T], ACT.Gelu).then_inc(gelu_done, 1)
            turns(act, gelu)

        @block.vector
        def _(dve):
            def weigh(n, b, first):
                dve.wait_ge(gelu_done, n + 1)
                if not first:
                    dve.wait_ge(out_done, n - 1)
                dve.tensor_tensor(w_buf[b % 2].unsqueeze(1), act_buf[b % 2].unsqueeze(1), k.gates[:, one(dve, n), :],
                                  ALU.mult).then_inc(w_ready, 1)
            turns(dve, weigh)
            dve.wait_ge(out_done, PEER_KEYS)
            for t in range(TT):
                x = k.x[:, t, :].rearrange("p (b n) -> p b n", b=2)
                dve.tensor_tensor(x, x, k.ps[:, 2 * t:2 * t + 2, :], ALU.add).then_inc(added, 1)
            dve.wait_ge(added, TT)
    k.peer_done = True


def scaled_gains(k, name, layer, gain, part):
    base = 400 + 32 * layer + (16 if part else 0)
    gs = k.small[:, base:base + 16].rearrange("p (s c) -> p s c", s=2)
    scale = k.mod[:, layer, (3 * part + 1) * C:(3 * part + 2) * C, :].rearrange("p c s -> p s c")
    with k.nc.Block(no_gpsimd_drain=True) as block:
        @block.vector
        def _(dve):
            st = k.step_v.after
            st(dve, dve.tensor_scalar(gs, scale, 1.0, None, ALU.add))
            st(dve, dve.tensor_tensor(gs, gs, gain.unsqueeze(1).to_broadcast([P, 2, C]), ALU.mult))
    shift = k.mod[:, layer, 3 * part * C:(3 * part + 1) * C, :]
    return [(gs[:, s, :], shift[:, :, s]) for s in range(2)]


def row_gates(k, name, layer, part, seqs, dst):
    nc = k.nc
    diag = work(k, 20480, 256)
    made, full, free = (k.shared[s] for s in ("diag_made", "row_full", "row_kept"))
    order = [(i, s, c) for i, s in enumerate(seqs) for c in range(C)]
    with nc.Block(no_gpsimd_drain=True) as block:
        @block.vector
        def _(dve):
            for j, (i, s, c) in enumerate(order):
                if j >= 2:
                    dve.wait_ge(*full.at(j - 1))
                dve.tensor_scalar(diag[:, P * (j % 2):P * (j % 2) + P], k.ident[:],
                                  k.mod[:, layer, part * C + c, s:s + 1], None, ALU.mult).then_inc(made.sem, 1)

        @block.tensor
        def _(pe):
            for j, (i, s, c) in enumerate(order):
                pe.wait_ge(*made.at(j + 1))
                if j >= 4:
                    pe.wait_ge(*free.at(j - 3))
                pe.matmul(k.ps[:, j % 4, 0:P], k.ones[:], diag[:, P * (j % 2):P * (j % 2) + P],
                          start=True, stop=True).then_inc(full.sem, 1)

        @block.scalar
        def _(act):
            for j, (i, s, c) in enumerate(order):
                act.wait_ge(*full.at(j + 1))
                act.activation(dst[:, i, c * P:(c + 1) * P], k.ps[:, j % 4, 0:P], ACT.Copy).then_inc(free.sem, 1)
    for s in (made, full, free):
        s.base += len(order)


def add_gated(k, buf):
    def evac(eng, t, ps):
        k.step_v.after(eng, eng.tensor_tensor(buf, ps, t.gate, ALU.mult))
        return eng.tensor_tensor(t.dst, t.dst, buf, ALU.add)
    return evac


def mlstm_inputs(k):
    nc = k.nc
    xn = work(k, 0, 4096).rearrange("p (a d) -> p a d", a=4)
    ht = work(k, 4160, 4096).rearrange("p (c t) -> p c t", c=C)
    raw = work(k, 0, 4160).rearrange("p (c s t) -> p c s t", c=C, s=2)
    k.qk = work(k, 0, 4160).rearrange("p (c t) -> p c t", c=C)[:, :, 0:2 * T]
    mixed = [work(k, 19040 + 512 * b, 512).rearrange("p (s t) -> p s t", s=2) for b in range(2)]
    k.v = work(k, 8256, 4 * A_HEADS * (A_DV + 1)).rearrange("p (a h d) -> p a h d", a=4, h=A_HEADS)
    k.o = work(k, 12384, 4096).rearrange("p (a d) -> p a d", a=4)
    ig, fg, ff, lo, m_, fb = (work(k, at, 512)[0:16, :] for at in (16480, 16992, 17504, 18016, 18528, 20480))
    n0, g0 = k.stage["a_in"], k.stage["a_gates"]
    lat, con = scaled_gains(k, "a", 0, k.col("norm_mix")[:, 0:C], 0)
    norm_transpose(k, "a_norm", [k.cx[:, 0, :], k.cx[:, 1, :], k.x[:, 0, :], k.x[:, 1, :]], xn, ht, [con, lat],
                   g0 + SLOTS)
    tiles = []
    w = weights(k, g0, 32)
    for a in range(2):
        tiles.append(tile([(w[:, c, 16 * a:16 * a + 16], ht[:, c, :]) for c in range(C)], 512, g0, m=16,
                          dst=(ig, fg)[a], bias=k.col(("ig_b", "fg_b")[a])[0:16, :]))
    for a in range(2):
        w = weights(k, n0 + a, 512)
        for b in range(4):
            tiles.append(tile([(w[:, c, b * P:(b + 1) * P], ht[:, c, :]) for c in range(C)], 512, n0 + a,
                              dst=raw[:, 4 * a + b, :, 2:2 + T]))
    for a in range(2, 6):
        w = weights(k, n0 + a, 512)
        for t in range(4):
            dst = k.v[:, t, 4 * (a % 2):4 * (a % 2) + 4, 0:A_DV] if a < 4 \
                else k.o[:, t, 512 * (a % 2):512 * (a % 2) + 512]
            tiles.append(tile([(ht[:, c, t * P:(t + 1) * P], w[:, c, :]) for c in range(C)], 512, n0 + a, dst=dst))

    def evac(eng, t, ps):
        if t.m == 16:
            return eng.activation(t.dst, ps, ACT.Identity, bias=t.bias)
        if len(t.dst.shape) == 3:
            ps = ps.rearrange("p (s t) -> p s t", s=t.dst.shape[1])
        return eng.activation(t.dst, ps, ACT.Copy)

    edges, conv, silu, logs, scans, ex, colf, kept = (
        k.sem(f"conv_{s}") for s in ("edges", "done", "silu", "logs", "scans", "exp", "columns", "kept"))
    ze = m_
    k.neg_m = nm = fb
    k.g_col = k.small[:, 64:128].rearrange("p (a r) -> p a r", a=4)
    k.e_col = k.small[:, 128:192].rearrange("p (a r) -> p a r", a=4)
    is_f, is_b = k.key_before[0:16, 8:9], k.key_from[0:16, 8:9]
    cw, cb = k.col("conv_w").rearrange("p (c w) -> p c w", c=C), k.col("conv_b")
    with nc.Block(no_gpsimd_drain=True) as block:
        @block.gpsimd
        def _(pool):
            pool.memset(raw[:, :, :, 0:2], 0.0).then_inc(edges, 1)
            pool.memset(raw[:, :, :, 2 + T:4 + T], 0.0).then_inc(edges, 1)
            pool.memset(ze, 0.0).then_inc(edges, 1)
            pool.memset(k.v[:, :, :, A_DV:A_DV + 1], 1.0).then_inc(edges, 1)
            pool.wait_ge(edges, 4)

    def logs_and_silus(act, i, stored):
        if i == 1:
            st = k.step_a.after
            stored(act, 1)
            st(act, act.activation(lo, fg, ACT.Abs))
            st(act, act.activation(lo, lo, ACT.Exp, scale=-1.0))
            act.activation(lo, lo, ACT.Ln, bias=1.0).then_inc(logs, 1)
        c = i - 3
        if 0 <= c < C:
            act.wait_ge(conv, c + 1)
            act.activation(k.qk[:, c, :].rearrange("p (s t) -> p s t", s=2), mixed[c % 2], ACT.Silu,
                           bias=cb[:, c:c + 1]).then_inc(silu, 1)

    def decays(act):
        act.wait_ge(scans, 1)
        act.activation(ff, ff, ACT.Exp, scale=-1.0).then_inc(ex, 1)
        act.wait_ge(colf, 1)
        act.activation(k.small[:, 64:192], k.ps[:, 7, 0:128], ACT.Copy).then_inc(kept, 1)

    def columns(pe):
        pe.wait_ge(ex, 1)
        for j, src in enumerate((m_, ff)):
            for t in range(4):
                last = pe.transpose(k.ps[:, 7, 64 * j + 16 * t:64 * j + 16 * t + 16], src[:, t * P:(t + 1) * P],
                                    k.ident[0:16, 0:16])
        last.then_inc(colf, 1)

    def convolve(dve, stored):
        st = k.step_v.after
        for c in range(C):
            stored(dve, 2 + c)
            if c >= 2:
                dve.wait_ge(silu, c - 1)
            out = mixed[c % 2]
            st(dve, dve.tensor_scalar(out, raw[:, c, :, 0:T], cw[:, c, 0:1], None, ALU.mult))
            for w_ in range(1, CONV_W):
                last = dve.scalar_tensor_tensor(out=out, in0=raw[:, c, :, w_:w_ + T], scalar=cw[:, c, w_:w_ + 1],
                                                in1=out, op0=ALU.mult, op1=ALU.add)
                if w_ < CONV_W - 1:
                    st(dve, last)
            last.then_inc(conv, 1)
        dve.wait_ge(logs, 1)
        st(dve, dve.tensor_scalar(fg, fg, 0.0, None, ALU.min))
        st(dve, dve.tensor_tensor(fg, fg, lo, ALU.subtract))

        def scan(fwd, bwd, src, other, op0, op1):
            st(dve, dve.tensor_tensor_scan(fwd, src, other, 0.0, op0, op1))
            st(dve, dve.tensor_tensor_scan(bwd[:, 0:T][:, ::-1], src[:, 0:T][:, ::-1], other[:, 0:T][:, ::-1],
                                           0.0, op0, op1))
            st(dve, dve.tensor_tensor_scan(bwd[:, T:2 * T][:, ::-1], src[:, T:2 * T][:, ::-1],
                                           other[:, T:2 * T][:, ::-1], bwd[:, 0:1], op0, op1))
            st(dve, dve.tensor_scalar(fwd, fwd, is_f, None, ALU.mult))
            st(dve, dve.scalar_tensor_tensor(out=fwd, in0=bwd, scalar=is_b, in1=fwd, op0=ALU.mult, op1=ALU.add))
        scan(ff, fb, fg, ze, ALU.add, ALU.add)
        st(dve, dve.tensor_tensor(m_, ig, ff, ALU.subtract))
        scan(lo, fb, m_, m_, ALU.max, ALU.max)
        st(dve, dve.tensor_tensor(ff, ff, lo, ALU.add))
        dve.tensor_scalar(nm, lo, -1.0, None, ALU.mult).then_inc(scans, 1)
        dve.wait_ge(silu, 4)
        q = k.qk[:, 0:4, :]
        st(dve, dve.tensor_scalar(q, q, A_DK ** -0.5, None, ALU.mult))

    gemm(k, "a_in", tiles, evac, n0 + 6 + SLOTS, beside=convolve, between=logs_and_silus, after=(decays, columns))


def mlstm_heads(k):
    nc = k.nc
    buffers = 3
    wt = [work(k, 16480 + 1280 * b, 1280) for b in range(buffers)]
    k.y = work(k, 4160, 4096).rearrange("p (a d) -> p a d", a=4)
    den, inv = k.small[:, 192:196], k.small[:, 196:200]
    s_full, m_full, t_ready, e_ready, masked, w_ready, n_full, y_done = (
        k.sem(f"scan_{s}") for s in ("scores", "maxima", "exponent", "exp", "masked", "weights", "num", "out"))
    blocks = (((0, 0, 512, 0), (1, 128, 384, 0), (2, 256, 256, 0), (3, 384, 128, 0)),
              ((1, 0, 512, 128), (0, 0, 128, 0), (0, 256, 256, None), (2, 256, 128, 0), (3, 256, 256, 128)))
    units = [(h, d) for h in range(A_HEADS) for d in range(2)]

    def places(d):
        at = 0
        for kt, q0, n, diag in blocks[d]:
            yield kt, q0, n, diag, at
            at += n

    def s_of(kt, q0, n):
        if kt < 2:
            return k.ps[:, kt, q0:q0 + n]
        return k.ps[:, 2, T * (kt - 2) + q0 - T:T * (kt - 2) + q0 - T + n]

    def out_of(n):
        b = 4 + 2 * (n % 2)
        return k.ps[:, b:b + 2, :].rearrange("p b (t d) -> p (b t) d", t=2)

    with nc.Block(no_gpsimd_drain=True) as block:
        @block.tensor
        def _(pe):
            def score(h):
                if h:
                    pe.wait_ge(w_ready, 2 * h)
                off, c = A_DK * (h % 2), h // 2
                q, key = k.qk[off:off + A_DK, c, :], k.qk[off:off + A_DK, 4 + c, :]
                for kt in range(4):
                    q0 = 0 if kt < 2 else T
                    last = pe.matmul(s_of(kt, q0, 512 - q0), key[:, kt * P:(kt + 1) * P], q[:, q0:512],
                                     start=True, stop=True)
                last.then_inc(s_full, 1)

            def maxima(n):
                h, d = units[n]
                if n:
                    pe.wait_ge(t_ready, n)
                pe.matmul(k.ps[:, 3, :], k.ident[0:16, 8 * d + h:8 * d + h + 1].to_broadcast([16, P]),
                          k.neg_m, start=True, stop=True).then_inc(m_full, 1)

            score(0)
            maxima(0)
            for n, (h, d) in enumerate(units):
                if n + 1 < len(units):
                    maxima(n + 1)
                pe.wait_ge(w_ready, n + 1)
                if n + 1 < len(units) and d == 1:
                    score(h + 1)
                if n >= 2:
                    pe.wait_ge(y_done, n - 1)
                w = wt[n % buffers]
                for t in range(4):
                    terms = [(kt, at + t * P - q0) for kt, q0, m, _, at in places(d) if q0 <= t * P < q0 + m]
                    for j, (kt, a) in enumerate(terms):
                        last = pe.matmul(out_of(n)[:, t, 0:A_DV + 1], w[:, a:a + P], k.v[:, kt, h, :],
                                         start=(j == 0), stop=(j == len(terms) - 1))
                last.then_inc(n_full, 1)

        @block.vector
        def _(dve):
            st = k.step_v.after

            def exponents(n):
                h, d = units[n]
                dve.wait_ge(m_full, n + 1)
                if n >= buffers:
                    dve.wait_ge(n_full, n - buffers + 1)
                for kt, q0, m, _, at in places(d):
                    last = dve.tensor_scalar(wt[n % buffers][:, at:at + m], k.ps[:, 3, q0:q0 + m],
                                             k.g_col[:, kt, 8 * d + h:8 * d + h + 1], 0.0, ALU.add, ALU.min)
                last.then_inc(t_ready, 1)

            def weigh(n):
                h, d = units[n]
                dve.wait_ge(s_full, h + 1)
                dve.wait_ge(masked, n + 1)
                for kt, q0, m, _, at in places(d):
                    w = wt[n % buffers][:, at:at + m]
                    last = dve.tensor_tensor(w, w, s_of(kt, q0, m), ALU.mult)
                last.then_inc(w_ready, 1)

            def finish(n):
                h, d = units[n]
                dve.wait_ge(n_full, n + 1)
                d_ = out_of(n)[:, :, A_DV]
                st(dve, dve.scalar_tensor_tensor(out=inv, in0=d_, scalar=-1.0,
                                                 in1=k.e_col[:, :, 8 * d + h], op0=ALU.mult, op1=ALU.max))
                st(dve, dve.tensor_tensor(den, d_, inv, ALU.max))
                st(dve, dve.reciprocal(inv, den))
                num = out_of(n)[:, :, 0:A_DV]
                y = k.y[:, :, h * A_DV:(h + 1) * A_DV]
                if d == 0:
                    dve.tensor_tensor(y, num, inv.unsqueeze(2).to_broadcast([P, 4, P]), ALU.mult).then_inc(y_done, 1)
                    dve.wait_ge(y_done, n + 1)
                else:
                    for t in range(4):
                        last = dve.scalar_tensor_tensor(out=y[:, t, :], in0=num[:, t, :], scalar=inv[:, t:t + 1],
                                                        in1=y[:, t, :], op0=ALU.mult, op1=ALU.add)
                    last.then_inc(y_done, 1)
                    dve.wait_ge(y_done, n + 1)

            exponents(0)
            for n in range(len(units)):
                weigh(n)
                if n + 1 < len(units):
                    exponents(n + 1)
                if n:
                    finish(n - 1)
            finish(len(units) - 1)

        @block.scalar
        def _(act):
            for n in range(len(units)):
                act.wait_ge(t_ready, n + 1)
                act.activation(wt[n % buffers], wt[n % buffers], ACT.Exp).then_inc(e_ready, 1)

        @block.gpsimd
        def _(pool):
            for n, (h, d) in enumerate(units):
                pool.wait_ge(e_ready, n + 1)
                mask = k.key_from if d else k.key_upto
                diags = [at + diag for _, _, _, diag, at in places(d) if diag is not None]
                for j, a in enumerate(diags):
                    w = wt[n % buffers][:, a:a + P]
                    last = pool.tensor_tensor(w, w, mask[:], ALU.mult)
                    if j < len(diags) - 1:
                        k.step_p.after(pool, last)
                last.then_inc(masked, 1)


def head_finish(k, name, y, tiles, heads, centre, gate, func, at):
    nc = k.nc
    n = tiles * heads
    sq = work(k, at, tiles * D)
    opened = k.sem(f"{name}_open")
    mean, ss, v, r, tmp = (k.small[:, 208 + 32 * j:208 + 32 * j + n] for j in range(5))
    y3 = y.rearrange("p a (h d) -> p (a h) d", d=P)
    s3 = sq.rearrange("p (n d) -> p n d", d=P)
    with nc.Block(no_gpsimd_drain=True) as block:
        @block.scalar
        def _(act):
            act.activation(gate, gate, func).then_inc(opened, 1)

        @block.vector
        def _(dve):
            st = k.step_v.after
            if centre:
                st(dve, dve.tensor_reduce(mean, y3, AX.X, ALU.add))
                st(dve, dve.tensor_scalar(mean, mean, 1.0 / P, None, ALU.mult))
                st(dve, dve.tensor_tensor(y3, y3, mean.unsqueeze(2).to_broadcast([P, n, P]), ALU.subtract))
            st(dve, dve.tensor_tensor(s3, y3, y3, ALU.mult))
            st(dve, dve.tensor_reduce(ss, s3, AX.X, ALU.add))
            st(dve, dve.tensor_scalar(v, ss, 1.0 / P, EPS, ALU.mult, ALU.add))
            rsqrt(k, dve, v, r, tmp)
            st(dve, dve.tensor_tensor(y3, y3, r.unsqueeze(2).to_broadcast([P, n, P]), ALU.mult))
            dve.wait_ge(opened, 1)
            st(dve, dve.tensor_tensor(y, y, gate, ALU.mult))


def gated_out(k, name, y, tokens, col, stage, at, rows, layer, seqs):
    yt = work(k, at, 4096)[:, 0:len(tokens) * D].rearrange("p (c t) -> p c t", c=C)
    gates = work(k, rows, len(seqs) * D).rearrange("p (s d) -> p s d", s=len(seqs))
    turn(k, f"{name}_y", y, yt, col)
    row_gates(k, f"{name}_rows", layer, 2, seqs, gates)
    n0 = k.stage[stage]
    tiles = []
    for a in range(2):
        w = weights(k, n0 + a, 512)
        cs = slice(512 * a, 512 * a + 512)
        for j, x in enumerate(tokens):
            tiles.append(tile([(yt[:, c, j * P:(j + 1) * P], w[:, c, :]) for c in range(C)], 512, n0 + a,
                              dst=x[:, cs], gate=gates[:, j // TT, cs]))
    gemm(k, f"{name}_out", tiles, add_gated(k, work(k, 19520, 512)), n0 + 2 + SLOTS, "dve")


def experts(k, name, layer, sets, stage):
    nc = k.nc
    S, N = len(sets), CAPACITY
    NT = S * TT
    M = S * N
    PER = P // M
    GROUPS = EXPERTS // PER
    tiles = [x for _, xs in sets for x in xs]
    xn = work(k, 0, NT * D).rearrange("p (a d) -> p a d", a=NT)
    ht = work(k, 4096, NT * D).rearrange("p (c t) -> p c t", c=C)
    hot = work(k, 8192, NT * 512).rearrange("p (a e s) -> p a e s", a=NT, e=EXPERTS)
    xs = work(k, 10240, C * EXPERTS * M).rearrange("p (c e s n) -> p c e s n", c=C, e=EXPERTS, s=S)
    aff = work(k, 18432, NT * 16).rearrange("p (a e) -> p a e", a=NT)
    aff_t = work(k, 18496, S * T)[0:16, :]
    rank = work(k, 19008, 2 * NT * 16).rearrange("p (j a e) -> p j a e", j=2, a=NT)
    before = work(k, 19136, 2 * T).rearrange("p (a t) -> p a t", a=TT)
    scr = [work(k, 10240 + T * j, T) for j in range(8)]
    router = work(k, 19648, 128).rearrange("p (c e) -> p c e", c=C)
    ga = scaled_gains(k, name, layer, k.col("norm_ffn")[:, C * layer:C * layer + C], 1)
    affine = [ga[s] for s, _ in sets]
    base = k.stage[stage]
    norm_transpose(k, f"{name}_norm", tiles, xn, ht, affine)

    got, full, exped, normed, turned, kept, spread, read, ready = (
        k.sem(f"{name}_{s}") for s in ("router", "logits", "exp", "affinity", "turned", "kept", "rows", "ranked", "hot"))
    mx, sm = k.small[:, 208:208 + NT], k.small[:, 216:216 + NT]
    with nc.Block(no_gpsimd_drain=True) as block:
        @block.sync
        def _(sp):
            sp.dma_start(router, k.dram["moe_router_2"][layer].rearrange("(c p) e -> p c e", p=P)).then_inc(got, 16)
            sp.wait_ge(got, 16)

        @block.tensor
        def _(pe):
            pe.wait_ge(got, 16)
            for t in range(NT):
                for c in range(C):
                    last = pe.matmul(k.ps[:, 0, 16 * t:16 * t + 16], ht[:, c, t * P:(t + 1) * P], router[:, c, :],
                                     start=(c == 0), stop=(c == C - 1))
            last.then_inc(full, 1)
            pe.wait_ge(normed, 1)
            for t in range(NT):
                last = pe.transpose(k.ps[0:16, 1, t * P:(t + 1) * P], aff[:, t, :], k.ident[:])
            last.then_inc(turned, 1)
            pe.wait_ge(kept, 1)
            for e in range(EXPERTS):
                if e >= 2:
                    pe.wait_ge(read, 2 * (e - 1) * NT)
                pe.matmul(k.ps[:, 2 + e % 2, 0:S * T], k.ident[0:16, e:e + 1].to_broadcast([16, P]), aff_t,
                          start=True, stop=True).then_inc(spread, 1)

        @block.scalar
        def _(act):
            act.wait_ge(exped, 1)
            act.activation(aff, aff, ACT.Exp).then_inc(exped, 1)
            act.wait_ge(turned, 1)
            act.activation(aff_t, k.ps[0:16, 1, 0:S * T], ACT.Copy).then_inc(kept, 1)

        @block.vector
        def _(dve):
            st = k.step_v.after
            st(dve, dve.memset(before[:, 1, 0:P], 1.0))
            st(dve, dve.memset(before[:, 0, P:T], 0.0))
            st(dve, dve.tensor_copy(before[:, 0, 0:P], k.key_after[:]))
            st(dve, dve.tensor_copy(before[:, 1, P:T], k.key_after[:]))
            dve.wait_ge(full, 1)
            logits = k.ps[:, 0, 0:16 * NT].rearrange("p (a e) -> p a e", a=NT)
            st(dve, dve.tensor_reduce(mx, logits, AX.X, ALU.max))
            dve.tensor_tensor(aff, logits, mx.unsqueeze(2).to_broadcast([P, NT, 16]), ALU.subtract).then_inc(exped, 1)
            dve.wait_ge(exped, 2)
            st(dve, dve.tensor_reduce(sm, aff, AX.X, ALU.add))
            st(dve, dve.reciprocal(sm, sm))
            dve.tensor_tensor(aff, aff, sm.unsqueeze(2).to_broadcast([P, NT, 16]), ALU.mult).then_inc(normed, 1)
            for e in range(EXPERTS):
                dve.wait_ge(spread, e + 1)
                for t in range(NT):
                    n = e * NT + t
                    row = k.ps[:, 2 + e % 2, T * (t // TT):T * (t // TT) + T]
                    a = aff[:, t, e:e + 1]
                    if n >= 4:
                        dve.wait_ge(read, 2 * (n - 3))
                    dve.tensor_scalar(scr[2 * (n % 4)], row, a, 0.0, ALU.is_gt, ALU.add,
                                      accum_out=rank[:, 0, t, e:e + 1]).then_inc(read, 1)
                    dve.scalar_tensor_tensor(out=scr[2 * (n % 4) + 1], in0=row, scalar=a, in1=before[:, t % TT, :],
                                             op0=ALU.is_equal, op1=ALU.mult, accum_out=rank[:, 1, t, e:e + 1])\
                       .then_inc(read, 1)
            dve.wait_ge(read, 2 * EXPERTS * NT)
            st(dve, dve.tensor_tensor(rank[:, 0], rank[:, 0], rank[:, 1], ALU.add))
            for t in range(NT):
                st(dve, dve.tensor_tensor(hot[:, t], rank[:, 0, t, :].unsqueeze(2).to_broadcast([P, 16, N]),
                                          k.iota[:, 0:N].unsqueeze(1).to_broadcast([P, 16, N]), ALU.is_equal))

    jobs = [tile([(xn[:, TT * s + t, c * P:(c + 1) * P], hot[:, TT * s + t].rearrange("p e n -> p (e n)"))
                  for t in range(TT)], 512, s=s, c=c) for c in range(C) for s in range(S)]

    def place(eng, t, ps):
        scale, shift = affine[t.s]
        return eng.activation(xs[:, t.c, :, t.s, :], ps.rearrange("p (e n) -> p e n", e=EXPERTS), ACT.Identity,
                              scale=scale[:, t.c:t.c + 1], bias=shift[:, t.c:t.c + 1])
    gemm(k, f"{name}_gather", jobs, place, 0)

    back = work(k, 4096, NT * EXPERTS * M).rearrange("p (a e s n) -> p a e s n", a=NT, e=EXPERTS, s=S)
    back_t = work(k, 0, GROUPS * S * T).rearrange("p (g t) -> p g t", g=GROUPS)
    with nc.Block(no_gpsimd_drain=True) as block:
        @block.vector
        def _(dve):
            st = k.step_v.after
            st(dve, dve.memset(back, 0.0))
            for t in range(NT):
                st(dve, dve.tensor_tensor(back[:, t, :, t // TT, :], hot[:, t],
                                          aff[:, t, :].unsqueeze(2).to_broadcast([P, 16, N]), ALU.mult))
    turn(k, f"{name}_back", back.rearrange("p a e s n -> p a (e s n)"), back_t, None)

    Q = P // M
    W = D // Q
    silu_b, hid = work(k, 8192, W), work(k, 8192 + 512, W)
    ys = work(k, 8192 + 1024, D)
    wb = work(k, 18432, S * T)
    xe = work(k, 18944, C * M).rearrange("p (c m) -> p c m", c=C)
    hid_t = work(k, 19456, P * W // P).rearrange("p (j q m) -> p j q m", j=W // P, q=Q)
    acc = work(k, 4096, NT * D).rearrange("p (a d) -> p a d", a=NT)
    g_full, u_full, silu_d, hid_d, t_full, t_kept, y_full, y_kept, c_full, c_added, wb_kept, xe_kept = (
        k.sem(f"{name}_x_{s}") for s in ("gate", "up", "silu", "hidden", "turned", "hidden_t", "y", "y_kept", "sum",
                                         "added", "back", "tokens"))
    half_used = k.sem(f"{name}_x_half")
    srcs = [k.dram[n][layer].rearrange("e (c p) n -> p e c n", p=P)
            for n in ("moe_w_gate_2", "moe_w_up_2", "moe_w_down_2")]
    last_load = base + 6 * EXPERTS
    w4 = [slot(k, base + s).rearrange("p (c n) -> p c n", c=4) for s in range(6)]

    with nc.Block(no_gpsimd_drain=True) as block:
        @block.sync
        def _(sp):
            with sp.Fori(1, EXPERTS) as e:
                for s in range(6):
                    if s % 2 == 0:
                        sp.wait_ge(half_used, e * 3 - 3 + s // 2 + 1)
                    else:
                        sp.wait_ge((g_full, u_full, y_full)[s // 2], e)
                    sp.dma_start(w4[s].unsqueeze(1), srcs[s // 2][:, bass.ds(e, 1), 4 * (s % 2):4 * (s % 2) + 4, :])\
                      .then_inc(k.slot_loaded[(base + s) % SLOTS], 16)
            for n in range(last_load, min(last_load + SLOTS, len(k.loads))):
                s = n - last_load
                if s % 2 == 0:
                    sp.wait_ge(half_used, 3 * EXPERTS - 3 + s // 2 + 1)
                else:
                    sp.wait_ge((g_full, u_full, y_full)[s // 2], EXPERTS)
                k.used.add(n - SLOTS)
                k.issued = n
                issue(k, sp, n + 1)

        @block.tensor
        def _(pe):
            def product(e, s0, bank, lhsT, done):
                for half in range(2):
                    s = s0 + half
                    pe.wait_ge(k.slot_loaded[(base + s) % SLOTS], e * 16 + 16 * ((base + s) // SLOTS + 1))
                    for c in range(4):
                        kc = 4 * half + c
                        for q in range(Q):
                            last = pe.matmul(k.ps[q * M:q * M + M, bank, 0:W], lhsT(kc),
                                             w4[s][:, c, q * W:q * W + W], start=(kc == 0), stop=(kc == C - 1),
                                             skip_group_check=True)
                    last.then_inc(done if half else half_used, 1)

            def expert(e, steady):
                pe.wait_ge(xe_kept, e + 1)
                product(e, 0, 0, lambda kc: xe[:, kc, :], g_full)
                product(e, 2, 1, lambda kc: xe[:, kc, :], u_full)
                pe.wait_ge(hid_d, e + 1)
                for j in range(W // P):
                    last = pe.transpose(k.ps[:, 2, j * P:(j + 1) * P], hid[:, j * P:(j + 1) * P], k.ident[:])
                last.then_inc(t_full, 1)
                pe.wait_ge(t_kept, e + 1)
                if steady:
                    pe.wait_ge(y_kept, e * Q)
                product(e, 4, 3, lambda kc: hid_t[:, kc % (W // P), kc // (W // P), :], y_full)

            def combine(group, steady):
                pe.wait_ge(y_kept, group * (PER * Q) + PER * Q)
                pe.wait_ge(wb_kept, group + 1)
                for j in range(2 * NT):
                    t, nh = j // 2, j % 2
                    if steady or j >= 2:
                        pe.wait_ge(c_added, group * (2 * NT) + j - 1)
                    pe.matmul(k.ps[:, 4 + j % 2, :], wb[:, t * P:(t + 1) * P], ys[:, 512 * nh:512 * nh + 512],
                              start=True, stop=True).then_inc(c_full, 1)

            def group_of(group, steady):
                for b in range(PER):
                    expert(group * PER + b, steady or b > 0)
                combine(group, steady)

            group_of(0, False)
            with pe.Fori(1, GROUPS) as g:
                group_of(g, True)

        @block.scalar
        def _(act):
            def group_of(group, steady):
                if steady:
                    act.wait_ge(c_full, group * (2 * NT))
                act.activation(wb.unsqueeze(1), back_t[:, bass.ds(group, 1), :], ACT.Copy).then_inc(wb_kept, 1)
                for b in range(PER):
                    e = group * PER + b
                    act.wait_ge(g_full, e + 1)
                    if steady or b:
                        act.wait_ge(hid_d, e)
                    act.activation(silu_b, k.ps[:, 0, 0:W], ACT.Silu).then_inc(silu_d, 1)
                    act.wait_ge(t_full, e + 1)
                    act.activation(hid_t.rearrange("p j q m -> p (j q m)"), k.ps[:, 2, 0:W], ACT.Copy)\
                       .then_inc(t_kept, 1)
                    act.wait_ge(y_full, e + 1)
                    for q in range(Q):
                        act.activation(ys[M * b:M * b + M, q * W:q * W + W], k.ps[M * q:M * q + M, 3, 0:W],
                                       ACT.Copy).then_inc(y_kept, 1)

            group_of(0, False)
            with act.Fori(1, GROUPS) as g:
                group_of(g, True)

        @block.vector
        def _(dve):
            def group_of(group, steady):
                for b in range(PER):
                    e = group * PER + b
                    if steady or b:
                        dve.wait_ge(u_full, e)
                    dve.tensor_copy(xe.unsqueeze(2),
                                    xs.rearrange("p c e s n -> p c e (s n)")[:, :, bass.ds(e, 1), :])\
                       .then_inc(xe_kept, 1)
                    dve.wait_ge(silu_d, e + 1)
                    dve.wait_ge(u_full, e + 1)
                    if steady or b:
                        dve.wait_ge(t_full, e)
                    dve.tensor_tensor(hid, silu_b, k.ps[:, 1, 0:W], ALU.mult).then_inc(hid_d, 1)
                for j in range(2 * NT):
                    dve.wait_ge(c_full, group * (2 * NT) + j + 1)
                    out = acc[:, j // 2, 512 * (j % 2):512 * (j % 2) + 512]
                    if steady:
                        dve.tensor_tensor(out, out, k.ps[:, 4 + j % 2, :], ALU.add).then_inc(c_added, 1)
                    else:
                        dve.tensor_copy(out, k.ps[:, 4 + j % 2, :]).then_inc(c_added, 1)

            group_of(0, False)
            with dve.Fori(1, GROUPS) as g:
                group_of(g, True)
            dve.wait_ge(c_added, 2 * NT * GROUPS)
    k.used |= set(range(base, last_load))
    k.issued = max(k.issued, last_load)
    gates = work(k, 10240, S * D).rearrange("p (s d) -> p s d", s=S)
    row_gates(k, f"{name}_rows", layer, 5, [s for s, _ in sets], gates)
    with nc.Block(no_gpsimd_drain=True) as block:
        @block.vector
        def _(dve):
            st = k.step_v.after
            for t in range(NT):
                st(dve, dve.tensor_tensor(acc[:, t, :], acc[:, t, :], gates[:, t // TT, :], ALU.mult))
                st(dve, dve.tensor_tensor(tiles[t], tiles[t], acc[:, t, :], ALU.add))


def retention(k):
    nc = k.nc
    xn = work(k, 0, 4096).rearrange("p (a d) -> p a d", a=4)
    ht = work(k, 4160, 4096).rearrange("p (c t) -> p c t", c=C)
    q = work(k, 8256, 2048).rearrange("p (a d) -> p a d", a=TT)
    kk = work(k, 10304, 2048).rearrange("p (a d) -> p a d", a=TT)
    gate = work(k, 12352, 2048).rearrange("p (a d) -> p a d", a=TT)
    kt_ = work(k, 14400, 4096).rearrange("p (h t) -> p h t", h=8)
    v = work(k, 0, 4096).rearrange("p (a d) -> p a d", a=4)
    n0 = k.stage["b_in"]
    lat, con = scaled_gains(k, "b", 1, k.col("norm_mix")[:, C:2 * C], 0)
    norm_transpose(k, "b_norm", [k.cx[:, 0, :], k.cx[:, 1, :], k.x[:, 0, :], k.x[:, 1, :]], xn, ht, [con, lat])
    rot = work(k, 18496, 256).rearrange("p (a j n) -> p a j n", a=2, j=2)
    t1, t2 = work(k, 18752, 512), work(k, 19264, 512)
    got = k.sem("rope_tables")
    k.tables.append((rot, k.dram["rope"].rearrange("s (a p) n -> p s a n", p=P), got))
    last_tile = {}

    def rope(dve, stored):
        st = k.step_v.after
        dve.wait_ge(got, 16)
        for j, src in enumerate((q, kk)):
            for t in range(TT):
                stored(dve, last_tile[j, t])
                a = src[:, t, :].rearrange("p (h f s n) -> p h f s n", h=8, f=2, s=2)
                x1, x2 = a[:, :, :, 0, :], a[:, :, :, 1, :]
                cos, sin = (rot[:, s, t, :].rearrange("p (f n) -> p f n", f=2).unsqueeze(1)
                            .to_broadcast([P, 8, 2, 32]) for s in range(2))
                u1, u2 = (b.rearrange("p (h f n) -> p h f n", h=8, f=2) for b in (t1, t2))
                st(dve, dve.tensor_tensor(u1, x1, sin, ALU.mult))
                st(dve, dve.tensor_tensor(u2, x2, sin, ALU.mult))
                st(dve, dve.tensor_tensor(x1, x1, cos, ALU.mult))
                st(dve, dve.tensor_tensor(x1, x1, u2, ALU.subtract))
                st(dve, dve.tensor_tensor(x2, x2, cos, ALU.mult))
                st(dve, dve.tensor_tensor(x2, x2, u1, ALU.add))

    tiles = []
    for a in range(8):
        w = weights(k, n0 + a, 512)
        cs = slice(512 * (a % 2), 512 * (a % 2) + 512)
        if a in (2, 3):
            for b in range(4):
                tiles.append(tile([(w[:, c, b * P:(b + 1) * P], ht[:, c, 0:T]) for c in range(C)], T, n0 + a,
                                  dst=kt_[:, 4 * (a - 2) + b, 0:T]))
        for t in range(0 if a in (4, 5) else 2, 4):
            dst = v[:, t, cs] if a in (4, 5) else (q, kk, None, gate)[a // 2][:, t - 2, cs]
            if a < 4:
                last_tile[a // 2, t - 2] = len(tiles)
            tiles.append(tile([(ht[:, c, t * P:(t + 1) * P], w[:, c, :]) for c in range(C)], 512, n0 + a, dst=dst))
    gemm(k, "b_in", tiles, lambda eng, t, ps: eng.activation(t.dst, ps, ACT.Copy), n0 + 8 + SLOTS, beside=rope)

    turn(k, "b_k", kk, kt_[:, :, T:2 * T], None)
    qt = work(k, 18496, 2048).rearrange("p (h t) -> p h t", h=8)
    turn(k, "b_q", q, qt, None)

    dist = [work(k, 4160 + 1024 * j, 1024) for j in range(2)]
    masks = [work(k, 6208 + 512 * j, 512) for j in range(2)]
    ex = [work(k, 8256 + 1024 * j, 1024) for j in range(2)]
    wt = [work(k, 10304 + 1024 * b, 1024) for b in range(2)]
    idx = [work(k, 10304 + 1024 * b, 1024).bitcast(I32) for b in range(2)]
    logg = k.small[:, 64:80]
    exped, e_used, s_full, w_ready, o_full, o_done, made, ready = (
        k.sem(f"ret_{s}") for s in ("exp", "exp_used", "scores", "weights", "out", "stored", "index", "ready"))
    y = k.big[:, R_CTX:R_CTX + 2048].rearrange("p (a d) -> p a d", a=TT)
    with nc.Block(no_gpsimd_drain=True) as block:
        @block.gpsimd
        def _(pool):
            pool.iota(idx[0], pattern=[[-P, 4], [1, T]], base=T, channel_multiplier=-1).then_inc(made, 1)
            pool.iota(idx[1][:, 0:512], pattern=[[P, 2], [-1, T]], base=T, channel_multiplier=1).then_inc(made, 1)
            pool.iota(idx[1][:, 512:1024], pattern=[[P, 2], [-1, T]], base=0, channel_multiplier=1).then_inc(made, 1)

        @block.scalar
        def _(act):
            st = k.step_a.after
            def store(h):
                act.wait_ge(o_full, h + 1)
                act.activation(y[:, :, h * P:(h + 1) * P], k.ps[:, 4 + h % 2, 0:T].rearrange("p (a d) -> p a d", a=2),
                               ACT.Copy).then_inc(o_done, 1)

            a = k.small[:, 80:96]
            st(act, act.activation(a, k.col("decay"), ACT.Abs))
            st(act, act.activation(a, a, ACT.Exp, scale=-1.0))
            st(act, act.activation(a, a, ACT.Ln, bias=1.0))
            act.activation(a, a, ACT.Copy).then_inc(exped, 1)
            act.wait_ge(ready, 1)
            for h in range(B_HEADS + 1):
                if h < B_HEADS:
                    if h:
                        act.wait_ge(e_used, h)
                    for d in range(2):
                        act.activation(ex[d], dist[d], ACT.Exp, scale=logg[:, 8 * d + h:8 * d + h + 1])\
                           .then_inc(exped, 1)
                if h:
                    store(h - 1)

        @block.tensor
        def _(pe):
            def score(h):
                if h >= 2:
                    pe.wait_ge(w_ready, h - 1)
                for kt in range(4):
                    last = pe.matmul(k.ps[:, 2 * (h % 2) + kt // 2, T * (kt % 2):T * (kt % 2) + T],
                                     kt_[:, h, kt * P:(kt + 1) * P], qt[:, h, :], start=True, stop=True)
                last.then_inc(s_full, 1)
            score(0)
            for h in range(B_HEADS):
                if h + 1 < B_HEADS:
                    score(h + 1)
                pe.wait_ge(w_ready, h + 1)
                if h >= 2:
                    pe.wait_ge(o_done, h - 1)
                for t in range(TT):
                    for kt in range(4):
                        last = pe.matmul(k.ps[:, 4 + h % 2, t * P:(t + 1) * P],
                                         wt[h % 2][:, T * kt + t * P:T * kt + (t + 1) * P],
                                         v[:, kt, h * P:(h + 1) * P], start=(kt == 0), stop=(kt == 3))
                last.then_inc(o_full, 1)

        @block.vector
        def _(dve):
            st = k.step_v.after
            dve.wait_ge(made, 3)
            for j in range(2):
                st(dve, dve.tensor_copy(dist[j], idx[j]))
                st(dve, dve.tensor_scalar(masks[j], dist[j][:, 512:1024], 0.0, None, ALU.is_ge))
                st(dve, dve.tensor_scalar(dist[j], dist[j], 0.0, None, ALU.max))
            dve.wait_ge(exped, 1)
            st(dve, dve.tensor_scalar(logg, k.col("decay"), 0.0, None, ALU.min))
            dve.tensor_tensor(logg, logg, k.small[:, 80:96], ALU.subtract).then_inc(ready, 1)
            for h in range(B_HEADS):
                dve.wait_ge(exped, 2 * h + 3)
                for j in range(2):
                    st(dve, dve.tensor_tensor(ex[j][:, 512:1024], ex[j][:, 512:1024], masks[j], ALU.mult))
                if h >= 2:
                    dve.wait_ge(o_full, h - 1)
                dve.tensor_tensor(wt[h % 2], ex[0], ex[1], ALU.add).then_inc(e_used, 1)
                dve.wait_ge(e_used, h + 1)
                dve.wait_ge(s_full, h + 1)
                s = k.ps[:, 2 * (h % 2):2 * (h % 2) + 2, :].rearrange("p b n -> p (b n)")
                dve.scalar_tensor_tensor(out=wt[h % 2], in0=s, scalar=B_DIM ** -0.5, in1=wt[h % 2], op0=ALU.mult,
                                         op1=ALU.mult).then_inc(w_ready, 1)
    head_finish(k, "b_fin", y, 2, B_HEADS, True, gate, ACT.Silu, 4160)
    gated_out(k, "b", y, [k.x[:, 0, :], k.x[:, 1, :]], k.col("b_norm"), "b_out", 4160, 8256, 1, [0])


def final_norm(k):
    gain = work(k, 0, 1024)
    got, done, stored = k.sem("final_gain"), k.sem("final_done"), k.sem("final_stored")
    ss, v, r, tmp = (k.small[:, 4 * j:4 * j + TT] for j in range(4))
    scr = work(k, 1024, 2048).rearrange("p (a d) -> p a d", a=TT)
    with k.nc.Block(no_gpsimd_drain=True) as block:
        @block.sync
        def _(sp):
            sp.dma_start(gain, k.dram["final_gain"].to_broadcast([P, D])).then_inc(got, 16)
            sp.wait_ge(done, TT)
            sp.dma_start(k.dram["out"][0].rearrange("(a p) d -> p a d", p=P), scr).then_inc(stored, 16)
            sp.wait_ge(stored, 16)

        @block.vector
        def _(dve):
            st = k.step_v.after
            for t in range(TT):
                st(dve, dve.scalar_tensor_tensor(out=scr[:, t, :], in0=k.x[:, t, :], scalar=1.0, in1=k.x[:, t, :],
                                                 op0=ALU.mult, op1=ALU.mult, accum_out=ss[:, t:t + 1]))
            st(dve, dve.tensor_scalar(v, ss, 1.0 / D, EPS, ALU.mult, ALU.add))
            rsqrt(k, dve, v, r, tmp)
            dve.wait_ge(got, 16)
            for t in range(TT):
                dve.scalar_tensor_tensor(out=scr[:, t, :], in0=k.x[:, t, :], scalar=r[:, t:t + 1], in1=gain,
                                         op0=ALU.mult, op1=ALU.mult).then_inc(done, 1)


def two_blocks_kernel(nc, dram):
    with ExitStack() as ctx:
        k = setup(nc, ctx, dram)
        plan_loads(k)

        def mlstm():
            mlstm_inputs(k)
            mlstm_heads(k)

        def mlstm_out():
            head_finish(k, "a_fin", k.y, 4, A_HEADS, False, k.o, ACT.Sigmoid, 0)
            gated_out(k, "a", k.y, [k.cx[:, 0, :], k.cx[:, 1, :], k.x[:, 0, :], k.x[:, 1, :]], k.col("a_norm"),
                      "a_out", 0, 8256, 0, [1, 0])

        cx, x = [k.cx[:, t, :] for t in range(TT)], [k.x[:, t, :] for t in range(TT)]
        stages = [("constants", lambda: constants(k)), 
                  ("proj", lambda: first_projections(k)),
                  ("heads", lambda: head_turns(k)), ("softmax", lambda: softmax_attentions(k)),
                  ("merge", lambda: gated_merge(k)), ("select", lambda: peer_select(k)),
                  ("gates", lambda: peer_gates(k)), ("peer", lambda: peer_experts(k)),
                  ("mlstm", mlstm), ("mlstm_out", mlstm_out),
                  ("moe0", lambda: experts(k, "m0", 0, [(1, cx), (0, x)], "moe0")),
                  ("ret", lambda: retention(k)),
                  ("moe1", lambda: experts(k, "m1", 1, [(0, x)], "moe1")),
                  ("final", lambda: final_norm(k))]
        for _, stage in stages:
            stage()


def layout(a):
    def col(v):
        return v.reshape(-1, P).T

    parts = dict(
        g_mix=col(a["g_mix"]), g_mem=col(a["g_mem"]), g_ffn=col(a["g_ffn"]), norm_mix=col(a["norm_mix_g_2"]),
        norm_ffn=col(a["norm_ffn_g_2"]), ada_b=col(a["ada_b_2"]),
        cvec=np.stack([col(a["c_2"]), col(a["c_ctx_2"])], axis=2).reshape(P, 2 * C),
        gq_dil=np.tile(a["g_q_dil"].reshape(-1), 2)[:, None], gk_dil=np.tile(a["g_k_dil"].reshape(-1), 2)[:, None],
        gq_mem=a["g_q_mem"].reshape(P, 1), gk_mem=a["g_k_mem"].reshape(P, 1),
        conv_w=a["mlstm_conv_w_2"].reshape(CONV_W, C, P).transpose(2, 1, 0).reshape(P, C * CONV_W),
        conv_b=col(a["mlstm_conv_b_2"]), ig_b=np.tile(a["mlstm_igate_b_2"].reshape(16, 1), (8, 1)),
        fg_b=np.tile(a["mlstm_fgate_b_2"].reshape(16, 1), (8, 1)), a_norm=col(a["mlstm_head_norm_g_2"]),
        b_norm=col(a["ret_group_norm_g_2"]), decay=np.tile(a["ret_decay_logit_2"].reshape(1, 16), (P, 1)))
    out = {n: a[n] for n in ("x", "mem", "ctx_2", "w_in", "w_mem_kv", "w_o_sb", "w_o_dil", "w_o_mem", "w_gate",
                             "w_out", "w_peer_q", "peer_v", "ada_w_2", "mlstm_w_in_2", "mlstm_w_out_2", "ret_w_in_2",
                             "ret_w_out_2", "moe_router_2", "moe_w_gate_2", "moe_w_up_2", "moe_w_down_2", "b_gate")}
    out["columns"] = np.concatenate([parts[n] for n in COLUMNS], axis=1)
    out["final_gain"] = a["final_norm_g_2"].reshape(1, D)
    out["peer_u_t"] = a["peer_u"].reshape(PEER_KEYS, PEER_KEYS, C, P).transpose(1, 3, 2, 0)
    out["subkeys_t"] = a["peer_subkeys"].reshape(16, PEER_KEYS, P).transpose(2, 0, 1)
    inv = np.float32(10000.0) ** (-np.arange(32, dtype=np.float32) / np.float32(32))
    place = np.arange(T)
    angles = np.concatenate([(place // 64).astype(np.float32)[:, None] * inv,
                             (place % 64).astype(np.float32)[:, None] * inv], axis=1)
    out["rope"] = np.stack([np.cos(angles), np.sin(angles)])
    return {n: np.ascontiguousarray(v) for n, v in out.items()}


def kernel(**inputs):
    import concourse.bacc as _bacc
    from concourse.bass_utils import run_bass_kernel_spmd as _run

    arrays = {f"in_{n}_dram": v for n, v in layout({n: np.asarray(v) for n, v in inputs.items()}).items()}
    nc = _bacc.Bacc("TRN2", target_bir_lowering=False, num_devices=1)
    dram = {n[3:-5]: nc.dram_tensor(n, v.shape, mybir.dt.from_np(v.dtype), kind="ExternalInput").ap()
            for n, v in arrays.items()}
    dram["out"] = nc.dram_tensor("out_0_dram", (1, T, D), F32, kind="ExternalOutput").ap()
    two_blocks_kernel(nc, dram)
    r = _run(nc, [arrays], core_ids=[0])
    return r.results[0]["out_0_dram"]
```
